# Optimizing a Trainium2 kernel written in Bass

```python
import math
import jax, jax.numpy as jnp
from jax import lax
import numpy as np

D_MODEL = 1024
BATCH = 1
SEQ = 256
DEPTH = 1

MEM_LEN = 256
HEAD_DIM = 128
ATTN_HEADS = 6
ATTN_KV_HEADS = 2
ATTN_GROUP = ATTN_HEADS // ATTN_KV_HEADS
WINDOW = 128
BLOCK = 128
ROPE_DIM = HEAD_DIM // 4
ROPE_THETA = 500000.0
LRU_WIDTH = 768
LRU_BLOCKS = 6
LRU_BLOCK_W = LRU_WIDTH // LRU_BLOCKS
CONV_WIDTH = 4
CONV_LEFT = CONV_WIDTH // 2
LRU_C = 8.0
MEM_HEADS = 4
N_BRANCH = 3
PEER_HEADS = 8
PEER_KEYS = 128
PEER_EXPERTS = PEER_KEYS * PEER_KEYS
PEER_QDIM = 256
PEER_HALF = PEER_QDIM // 2
PEER_TOPK = 16
PEER_CHUNK = 128
EPS = 1e-6
NEG_INF = -1e30

ATTN_Q_W = ATTN_HEADS * HEAD_DIM
ATTN_KV_W = ATTN_KV_HEADS * HEAD_DIM
MEM_Q_W = MEM_HEADS * HEAD_DIM
GATE_W = N_BRANCH * D_MODEL
IN_W = ATTN_Q_W + 2 * ATTN_KV_W + 2 * LRU_WIDTH + MEM_Q_W + GATE_W


def rmsnorm(x, g):
    xf = x.astype(jnp.float32)
    y = xf * lax.rsqrt(jnp.mean(xf * xf, axis=-1, keepdims=True) + EPS) * g.astype(jnp.float32)
    return y.astype(x.dtype)

def partial_rope(t, positions):
    half = ROPE_DIM // 2
    inv_freq = ROPE_THETA ** (-jnp.arange(0, ROPE_DIM, 2, dtype=jnp.float32) / ROPE_DIM)
    ang = positions.astype(jnp.float32)[..., None] * inv_freq
    cos = jnp.cos(ang)[:, :, None, :]
    sin = jnp.sin(ang)[:, :, None, :]
    tr = t[..., :ROPE_DIM].astype(jnp.float32)
    t1, t2 = tr[..., :half], tr[..., half:]
    rot = jnp.concatenate([t1 * cos - t2 * sin, t2 * cos + t1 * sin], axis=-1)
    return jnp.concatenate([rot.astype(t.dtype), t[..., ROPE_DIM:]], axis=-1)

def band_blocks(t, nb):
    b = t.shape[0]
    tp = jnp.pad(t, ((0, 0), (BLOCK, BLOCK), (0, 0), (0, 0)))
    tp = tp.reshape(b, nb + 2, BLOCK, t.shape[2], t.shape[3])
    return jnp.concatenate([tp[:, :-2], tp[:, 1:-1], tp[:, 2:]], axis=2)

def windowed_gqa(q, k, v, sink):
    b, s = q.shape[0], q.shape[1]
    nb = s // BLOCK
    qb = q.reshape(b, nb, BLOCK, ATTN_KV_HEADS, ATTN_GROUP, HEAD_DIM)
    kb = band_blocks(k, nb)
    vb = band_blocks(v, nb)
    scores = jnp.einsum('bnqkgd,bnskd->bnkgqs', qb, kb).astype(jnp.float32) * (HEAD_DIM ** -0.5)
    blk = jnp.arange(nb, dtype=jnp.int32)[:, None]
    q_pos = blk * BLOCK + jnp.arange(BLOCK, dtype=jnp.int32)[None, :]
    k_pos = blk * BLOCK - BLOCK + jnp.arange(3 * BLOCK, dtype=jnp.int32)[None, :]
    valid = ((k_pos[:, None, :] >= 0) & (k_pos[:, None, :] < s)
             & (jnp.abs(k_pos[:, None, :] - q_pos[:, :, None]) <= WINDOW))
    scores = jnp.where(valid[None, :, None, None], scores, NEG_INF)
    sink_b = jnp.broadcast_to(sink.astype(jnp.float32).reshape(ATTN_KV_HEADS, ATTN_GROUP)[None, None, :, :, None, None],
                              scores.shape[:-1] + (1,))
    p = jax.nn.softmax(jnp.concatenate([scores, sink_b], axis=-1), axis=-1)[..., :-1]
    out = jnp.einsum('bnkgqs,bnskd->bnqkgd', p.astype(v.dtype), vb)
    return out.reshape(b, s, ATTN_Q_W)

def centred_depthwise_conv(t, w, bias):
    s = t.shape[1]
    tp = jnp.pad(t, ((0, 0), (CONV_LEFT, CONV_WIDTH - 1 - CONV_LEFT), (0, 0)))
    y = bias[None, None, :]
    for j in range(CONV_WIDTH):
        y = y + w[j][None, None, :] * tp[:, j:j + s]
    return y

def _lin_comb(c1, c2):
    a1, b1 = c1
    a2, b2 = c2
    return a1 * a2, a2 * b1 + b2

def bidir_rglru(xc, w_r, b_r, w_i, b_i, lam):
    b, s = xc.shape[0], xc.shape[1]
    xf = xc.astype(jnp.float32)
    xblk = xf.reshape(b, s, LRU_BLOCKS, LRU_BLOCK_W)
    r = jax.nn.sigmoid(jnp.einsum('bshc,dhce->dbshe', xblk, w_r.astype(jnp.float32)).reshape(2, b, s, LRU_WIDTH)
                       + b_r.astype(jnp.float32)[:, None, None, :])
    i = jax.nn.sigmoid(jnp.einsum('bshc,dhce->dbshe', xblk, w_i.astype(jnp.float32)).reshape(2, b, s, LRU_WIDTH)
                       + b_i.astype(jnp.float32)[:, None, None, :])
    log_a = -LRU_C * r * jax.nn.softplus(-lam.astype(jnp.float32))[:, None, None, :]
    a = jnp.exp(log_a)
    bx = jnp.sqrt(-jnp.expm1(2.0 * log_a)) * (i * xf[None])
    _, h_fwd = lax.associative_scan(_lin_comb, (a[0], bx[0]), axis=1)
    _, h_bwd = lax.associative_scan(_lin_comb, (a[1], bx[1]), axis=1, reverse=True)
    return (h_fwd + h_bwd).astype(xc.dtype)

def memory_cross_attention(q, k, v):
    scores = jnp.einsum('bshd,bmhd->bhsm', q, k).astype(jnp.float32) * (HEAD_DIM ** -0.5)
    p = jax.nn.softmax(scores, axis=-1)
    out = jnp.einsum('bhsm,bmhd->bshd', p.astype(v.dtype), v)
    return out.reshape(q.shape[0], q.shape[1], MEM_Q_W)

def peer_ffn(h, w_q, sub_keys, u_tab, v_tab):
    b, s, d = h.shape
    q = (h @ w_q).reshape(b, s, PEER_HEADS, 2, PEER_HALF)
    sc = jnp.einsum('bshpc,hpkc->bshpk', q, sub_keys).astype(jnp.float32)
    top_v, top_i = lax.top_k(sc, PEER_TOPK)
    cand_v = (top_v[..., 0, :, None] + top_v[..., 1, None, :]).reshape(b, s, PEER_HEADS, PEER_TOPK * PEER_TOPK)
    cand_i = (top_i[..., 0, :, None] * PEER_KEYS + top_i[..., 1, None, :]).reshape(b, s, PEER_HEADS, PEER_TOPK * PEER_TOPK)
    best_v, best_pos = lax.top_k(cand_v, PEER_TOPK)
    idx = jnp.take_along_axis(cand_i, best_pos, axis=-1)
    gate = jax.nn.softmax(best_v, axis=-1)
    n_tok = b * s
    n_chunk = n_tok // PEER_CHUNK
    hc = h.reshape(n_chunk, PEER_CHUNK, d)
    ic = idx.reshape(n_chunk, PEER_CHUNK, PEER_HEADS, PEER_TOPK)
    gc = gate.reshape(n_chunk, PEER_CHUNK, PEER_HEADS, PEER_TOPK)

    def expert_chunk(args):
        hx, ix, gx = args
        u = u_tab[ix]
        act = jax.nn.gelu(jnp.einsum('chkd,cd->chk', u, hx).astype(jnp.float32))
        vv = v_tab[ix]
        return jnp.einsum('chk,chkd->cd', (gx * act).astype(vv.dtype), vv)

    out = lax.map(expert_chunk, (hc, ic, gc))
    return out.reshape(b, s, d)

def first_inputs(seed: int = 0) -> dict:
    key = jax.random.key(seed)
    ks = jax.random.split(key, 32)
    f32 = jnp.float32
    nrm = lambda k, shape, scale: jax.random.normal(k, shape, f32) * scale
    u = jax.random.uniform(ks[12], (DEPTH, 2, LRU_WIDTH), f32, 0.9, 0.999)
    a0 = u ** (1.0 / LRU_C)
    lam = jnp.log(a0) - jnp.log1p(-a0)
    return {
        "x": nrm(ks[0], (BATCH, SEQ, D_MODEL), 1.0),
        "mem": nrm(ks[1], (BATCH, MEM_LEN, D_MODEL), 1.0),
        "positions": jnp.broadcast_to(jnp.arange(SEQ, dtype=jnp.int32)[None, :], (BATCH, SEQ)),
        "g_mix": 1.0 + nrm(ks[2], (DEPTH, D_MODEL), 0.02),
        "g_mem": 1.0 + nrm(ks[3], (DEPTH, D_MODEL), 0.02),
        "w_in": nrm(ks[4], (DEPTH, D_MODEL, IN_W), D_MODEL ** -0.5),
        "gate_b": nrm(ks[5], (DEPTH, GATE_W), 0.02),
        "attn_sink": nrm(ks[6], (DEPTH, ATTN_HEADS), 0.5),
        "conv_w": nrm(ks[7], (DEPTH, CONV_WIDTH, LRU_WIDTH), CONV_WIDTH ** -0.5),
        "conv_b": nrm(ks[8], (DEPTH, LRU_WIDTH), 0.02),
        "lru_wr": nrm(ks[9], (DEPTH, 2, LRU_BLOCKS, LRU_BLOCK_W, LRU_BLOCK_W), LRU_BLOCK_W ** -0.5),
        "lru_br": nrm(ks[10], (DEPTH, 2, LRU_WIDTH), 0.02),
        "lru_wi": nrm(ks[11], (DEPTH, 2, LRU_BLOCKS, LRU_BLOCK_W, LRU_BLOCK_W), LRU_BLOCK_W ** -0.5),
        "lru_bi": nrm(ks[13], (DEPTH, 2, LRU_WIDTH), 0.02),
        "lru_lambda": lam,
        "w_mem_kv": nrm(ks[14], (DEPTH, D_MODEL, 2 * MEM_Q_W), D_MODEL ** -0.5),
        "p_attn": nrm(ks[15], (DEPTH, ATTN_Q_W, D_MODEL), ATTN_Q_W ** -0.5),
        "p_lru": nrm(ks[16], (DEPTH, LRU_WIDTH, D_MODEL), LRU_WIDTH ** -0.5),
        "p_mem": nrm(ks[17], (DEPTH, MEM_Q_W, D_MODEL), MEM_Q_W ** -0.5),
        "w_out": nrm(ks[18], (DEPTH, D_MODEL, D_MODEL), D_MODEL ** -0.5),
        "g_ffn": 1.0 + nrm(ks[19], (DEPTH, D_MODEL), 0.02),
        "w_peer_q": nrm(ks[20], (DEPTH, D_MODEL, PEER_HEADS * PEER_QDIM), D_MODEL ** -0.5),
        "peer_sub_keys": nrm(ks[21], (DEPTH, PEER_HEADS, 2, PEER_KEYS, PEER_HALF), PEER_HALF ** -0.5),
        "peer_u": nrm(ks[22], (DEPTH, PEER_EXPERTS, D_MODEL), D_MODEL ** -0.5),
        "peer_v": nrm(ks[23], (DEPTH, PEER_EXPERTS, D_MODEL), 0.25),
        "g_final": 1.0 + nrm(ks[24], (D_MODEL,), 0.02),
    }

def first_block(x, mem, positions, g_mix, g_mem, w_in, gate_b, attn_sink, conv_w, conv_b,
              lru_wr, lru_br, lru_wi, lru_bi, lru_lambda, w_mem_kv, p_attn, p_lru, p_mem,
              w_out, g_ffn, w_peer_q, peer_sub_keys, peer_u, peer_v, g_final):
    b, s, d = x.shape
    offs = [int(o) for o in np.cumsum([ATTN_Q_W, ATTN_KV_W, ATTN_KV_W, LRU_WIDTH, LRU_WIDTH, MEM_Q_W])]
    for l in range(DEPTH):
        h = rmsnorm(x, g_mix[l])
        proj = h @ w_in[l]
        q_a, k_a, v_a, x_l, gate_l, q_m, gates = jnp.split(proj, offs, axis=-1)
        q_a = partial_rope(q_a.reshape(b, s, ATTN_HEADS, HEAD_DIM), positions)
        k_a = partial_rope(k_a.reshape(b, s, ATTN_KV_HEADS, HEAD_DIM), positions)
        v_a = v_a.reshape(b, s, ATTN_KV_HEADS, HEAD_DIM)
        attn_out = windowed_gqa(q_a, k_a, v_a, attn_sink[l])
        xc = centred_depthwise_conv(x_l, conv_w[l], conv_b[l])
        lru_out = bidir_rglru(xc, lru_wr[l], lru_br[l], lru_wi[l], lru_bi[l], lru_lambda[l]) * jax.nn.gelu(gate_l)
        kv_m = rmsnorm(mem, g_mem[l]) @ w_mem_kv[l]
        k_m = kv_m[..., :MEM_Q_W].reshape(b, MEM_LEN, MEM_HEADS, HEAD_DIM)
        v_m = kv_m[..., MEM_Q_W:].reshape(b, MEM_LEN, MEM_HEADS, HEAD_DIM)
        mem_out = memory_cross_attention(q_m.reshape(b, s, MEM_HEADS, HEAD_DIM), k_m, v_m)
        g = jax.nn.sigmoid(gates + gate_b[l]).reshape(b, s, N_BRANCH, d)
        merged = (g[:, :, 0] * (attn_out @ p_attn[l])
                  + g[:, :, 1] * (lru_out @ p_lru[l])
                  + g[:, :, 2] * (mem_out @ p_mem[l]))
        x = x + merged @ w_out[l]
        h2 = rmsnorm(x, g_ffn[l])
        x = x + peer_ffn(h2, w_peer_q[l], peer_sub_keys[l], peer_u[l], peer_v[l])
    return rmsnorm(x, g_final)


DEPTH_2 = 2

N_MIXERS = 2
D_FF = 4 * D_MODEL
RMS_EPS = 1e-6
NEG_INF_2 = -1e30

GDN_HEADS = D_MODEL // 128
GDN_DK = 128
GDN_DV = 128
GDN_CONV = 5
GDN_CHUNK = 64
GDN_QKV = GDN_HEADS * (2 * GDN_DK + GDN_DV)
GDN_IN = GDN_QKV + GDN_HEADS * GDN_DV + 4 * GDN_HEADS

DSWA_CONFIGS = ((128, 1), (512, 4), (2048, 16))
DSWA_HEADS_PER_GROUP = 6
DSWA_HEAD_DIM = 64
DSWA_HEADS = len(DSWA_CONFIGS) * DSWA_HEADS_PER_GROUP
DSWA_WIDTH = DSWA_HEADS * DSWA_HEAD_DIM

REL_BUCKETS = 32
REL_MAX_DIST = 1024

N_LAYERS_A = (DEPTH_2 + 1) // 2
N_LAYERS_B = DEPTH_2 // 2


def rmsnorm_2(x, g):
    xf = x.astype(jnp.float32)
    y = xf * lax.rsqrt(jnp.mean(xf * xf, axis=-1, keepdims=True) + RMS_EPS)
    return (y * g.astype(jnp.float32)).astype(x.dtype)

def l2norm(t):
    return t * lax.rsqrt(jnp.sum(t * t, axis=-1, keepdims=True) + 1e-6)

def rel_bucket(rel):
    nb = REL_BUCKETS // 2
    max_exact = nb // 2
    ret = jnp.where(rel > 0, nb, 0)
    n = jnp.abs(rel)
    nf = jnp.maximum(n, 1).astype(jnp.float32)
    large = max_exact + (jnp.log(nf / max_exact) / math.log(REL_MAX_DIST / max_exact)
                         * (nb - max_exact)).astype(jnp.int32)
    large = jnp.minimum(large, nb - 1)
    return ret + jnp.where(n < max_exact, n, large)

def gated_delta_chunked(q, k, v, g, beta):
    B, H, S, DK = q.shape
    DV = v.shape[-1]
    C = GDN_CHUNK
    nc = S // C
    q = q.reshape(B, H, nc, C, DK)
    k = k.reshape(B, H, nc, C, DK)
    v = v.reshape(B, H, nc, C, DV)
    g = g.reshape(B, H, nc, C)
    beta = beta.reshape(B, H, nc, C)
    G = jnp.cumsum(g, axis=-1)
    incl = jnp.tril(jnp.ones((C, C), bool))
    strict = jnp.tril(jnp.ones((C, C), bool), -1)
    diff = jnp.where(incl, G[..., :, None] - G[..., None, :], 0.0)
    decay = jnp.where(incl, jnp.exp(diff), 0.0)
    kb = k * beta[..., None]
    a = jnp.where(strict, jnp.einsum('bhnid,bhnjd->bhnij', kb, k) * decay, 0.0)
    rhs = jnp.concatenate([v * beta[..., None], kb * jnp.exp(G)[..., None]], axis=-1)
    sol = lax.linalg.triangular_solve(a, rhs, left_side=True, lower=True, unit_diagonal=True)
    u, w = sol[..., :DV], sol[..., DV:]
    intra = jnp.einsum('bhnid,bhnjd->bhnij', q, k) * decay
    g_last = G[..., -1]
    q_dec = q * jnp.exp(G)[..., None]
    k_dec = k * jnp.exp(g_last[..., None] - G)[..., None]
    xs = tuple(jnp.moveaxis(t, 2, 0) for t in (u, w, intra, q_dec, k_dec, g_last))

    def step(state, inp):
        u_c, w_c, intra_c, qd_c, kd_c, gl_c = inp
        v_new = u_c - jnp.einsum('bhck,bhkv->bhcv', w_c, state)
        o_c = (jnp.einsum('bhck,bhkv->bhcv', qd_c, state)
               + jnp.einsum('bhij,bhjv->bhiv', intra_c, v_new))
        state = (state * jnp.exp(gl_c)[..., None, None]
                 + jnp.einsum('bhck,bhcv->bhkv', kd_c, v_new))
        return state, o_c

    s0 = jnp.zeros((B, H, DK, DV), jnp.float32)
    _, o = lax.scan(step, s0, xs)
    return jnp.moveaxis(o, 0, 2).reshape(B, H, S, DV)

def gated_deltanet_bidir(h, w_in, conv_w, a_log, dt_bias, norm_w, w_out):
    B, S, _ = h.shape
    H, DK, DV = GDN_HEADS, GDN_DK, GDN_DV
    f32 = jnp.float32
    proj = h @ w_in
    qkv = proj[..., :GDN_QKV]
    z = proj[..., GDN_QKV:GDN_QKV + H * DV].reshape(B, S, H, DV)
    ab = proj[..., GDN_QKV + H * DV:]
    pad = GDN_CONV // 2
    qkv = jax.nn.silu(lax.conv_general_dilated(
        qkv, conv_w, window_strides=(1,), padding=[(pad, pad)],
        dimension_numbers=('NWC', 'WIO', 'NWC'), feature_group_count=GDN_QKV))
    qkv = qkv.astype(f32)
    q = qkv[..., :H * DK].reshape(B, S, H, DK)
    k = qkv[..., H * DK:2 * H * DK].reshape(B, S, H, DK)
    v = qkv[..., 2 * H * DK:].reshape(B, S, H, DV)
    q = l2norm(q) * (DK ** -0.5)
    k = l2norm(k)
    a = ab[..., :2 * H].reshape(B, S, 2, H).astype(f32)
    b = ab[..., 2 * H:].reshape(B, S, 2, H).astype(f32)
    g = -jnp.exp(a_log.astype(f32)) * jax.nn.softplus(a + dt_bias.astype(f32))
    beta = jax.nn.sigmoid(b)
    qh, kh, vh = (jnp.transpose(t, (0, 2, 1, 3)) for t in (q, k, v))
    gh = jnp.transpose(g, (2, 0, 3, 1))
    bh = jnp.transpose(beta, (2, 0, 3, 1))
    o_fwd = gated_delta_chunked(qh, kh, vh, gh[0], bh[0])
    flip = lambda t: jnp.flip(t, axis=2)
    o_bwd = flip(gated_delta_chunked(flip(qh), flip(kh), flip(vh), flip(gh[1]), flip(bh[1])))
    o = jnp.transpose(o_fwd + o_bwd, (0, 2, 1, 3))
    o = o * lax.rsqrt(jnp.mean(o * o, axis=-1, keepdims=True) + RMS_EPS)
    o = o * norm_w.astype(f32) * jax.nn.silu(z.astype(f32))
    return o.reshape(B, S, H * DV).astype(h.dtype) @ w_out

def banded_attention(q, k, v, bias, half):
    N, L, H, E = q.shape
    blk = half
    nb = -(-L // blk)
    lp = nb * blk
    qb = jnp.pad(q, ((0, 0), (0, lp - L), (0, 0), (0, 0))).reshape(N, nb, blk, H, E)

    def windows(t):
        tb = jnp.pad(t, ((0, 0), (blk, lp - L + blk), (0, 0), (0, 0))).reshape(N, nb + 2, blk, H, E)
        return jnp.concatenate([tb[:, :-2], tb[:, 1:-1], tb[:, 2:]], axis=2)

    kw, vw = windows(k), windows(v)
    s = jnp.einsum('nbqhe,nbkhe->nbhqk', qb, kw).astype(jnp.float32) * (E ** -0.5)
    s = s + bias[None, None]
    q_idx = jnp.arange(lp).reshape(nb, blk)
    k_idx = jnp.arange(nb)[:, None] * blk - blk + jnp.arange(3 * blk)[None, :]
    off = k_idx[:, None, :] - q_idx[:, :, None]
    valid = (jnp.abs(off) <= half) & (k_idx[:, None, :] >= 0) & (k_idx[:, None, :] < L)
    s = jnp.where(valid[None, :, None], s, NEG_INF_2)
    m = jnp.max(s, axis=-1, keepdims=True)
    lse = m + jnp.log(jnp.sum(jnp.exp(s - m), axis=-1, keepdims=True))
    p = jnp.exp(s - lse)
    o = jnp.einsum('nbhqk,nbkhe->nbqhe', p.astype(v.dtype), vw).reshape(N, lp, H, E)[:, :L]
    lse = jnp.transpose(lse[..., 0], (0, 1, 3, 2)).reshape(N, lp, H)[:, :L]
    return o, lse

def to_sub(t, d):
    B, S, Hh, E = t.shape
    return jnp.swapaxes(t.reshape(B, S // d, d, Hh, E), 1, 2).reshape(B * d, S // d, Hh, E)

def from_sub(t, d, B):
    L = t.shape[1]
    rest = t.shape[2:]
    return jnp.swapaxes(t.reshape(B, d, L, *rest), 1, 2).reshape(B, L * d, *rest)

def dilated_window_attention(h, w_in, w_out, rel_table):
    B, S, _ = h.shape
    Hg, E = DSWA_HEADS_PER_GROUP, DSWA_HEAD_DIM
    qkv = (h @ w_in).reshape(B, S, 3, DSWA_HEADS, E)
    q, k, v = qkv[:, :, 0], qkv[:, :, 1], qkv[:, :, 2]
    outs, lses = [], []
    for gi, (window, dil) in enumerate(DSWA_CONFIGS):
        half = window // (2 * dil)
        hs = slice(gi * Hg, (gi + 1) * Hg)
        rel = (jnp.arange(3 * half)[None, :] - half - jnp.arange(half)[:, None]) * dil
        bias = jnp.take(rel_table, rel_bucket(rel), axis=0)[..., hs]
        bias = jnp.transpose(bias, (2, 0, 1)).astype(jnp.float32)
        o, lse = banded_attention(to_sub(q[:, :, hs], dil), to_sub(k[:, :, hs], dil),
                                  to_sub(v[:, :, hs], dil), bias, half)
        outs.append(from_sub(o, dil, B))
        lses.append(from_sub(lse, dil, B))
    o = jnp.stack(outs, axis=2)
    alpha = jax.nn.softmax(jnp.stack(lses, axis=2), axis=2)
    o = (o * alpha[..., None].astype(o.dtype)).reshape(B, S, DSWA_WIDTH)
    return o @ w_out

def squared_relu_mlp(h, w1, w2):
    return jnp.square(jax.nn.relu(h @ w1)) @ w2

def second_inputs(seed: int = 0) -> dict:
    key = jax.random.key(seed)
    ks = jax.random.split(key, 16)
    f32 = jnp.float32
    nrm = lambda kk, shape, scale: jax.random.normal(kk, shape, f32) * scale
    x = nrm(ks[0], (BATCH, SEQ, D_MODEL), 1.0)
    norm_mix = 1.0 + nrm(ks[1], (DEPTH_2, D_MODEL), 0.02)
    norm_mlp = 1.0 + nrm(ks[2], (DEPTH_2, D_MODEL), 0.02)
    norm_final = 1.0 + nrm(ks[3], (D_MODEL,), 0.02)
    rel_bias = nrm(ks[4], (REL_BUCKETS, DSWA_HEADS), 0.2)
    gdn_w_in = nrm(ks[5], (N_LAYERS_A, D_MODEL, GDN_IN), D_MODEL ** -0.5)
    gdn_conv_w = nrm(ks[6], (N_LAYERS_A, GDN_CONV, 1, GDN_QKV), GDN_CONV ** -0.5)
    gdn_a_log = jnp.log(jax.random.uniform(ks[7], (N_LAYERS_A, 2, GDN_HEADS), f32, 1.0, 16.0))
    dt = jnp.exp(jax.random.uniform(ks[8], (N_LAYERS_A, 2, GDN_HEADS), f32,
                                    math.log(1e-3), math.log(1e-1)))
    gdn_dt_bias = dt + jnp.log(-jnp.expm1(-dt))
    gdn_norm_w = 1.0 + nrm(ks[9], (N_LAYERS_A, GDN_DV), 0.02)
    gdn_w_out = nrm(ks[10], (N_LAYERS_A, GDN_HEADS * GDN_DV, D_MODEL), (GDN_HEADS * GDN_DV) ** -0.5)
    dswa_w_in = nrm(ks[11], (N_LAYERS_B, D_MODEL, 3 * DSWA_WIDTH), D_MODEL ** -0.5)
    dswa_w_out = nrm(ks[12], (N_LAYERS_B, DSWA_WIDTH, D_MODEL), DSWA_WIDTH ** -0.5)
    mlp_w1 = nrm(ks[13], (DEPTH_2, D_MODEL, D_FF), D_MODEL ** -0.5)
    mlp_w2 = nrm(ks[14], (DEPTH_2, D_FF, D_MODEL), D_FF ** -0.5)
    return {'x': x, 'norm_mix': norm_mix, 'norm_mlp': norm_mlp, 'norm_final': norm_final,
            'rel_bias': rel_bias, 'gdn_w_in': gdn_w_in, 'gdn_conv_w': gdn_conv_w,
            'gdn_a_log': gdn_a_log, 'gdn_dt_bias': gdn_dt_bias, 'gdn_norm_w': gdn_norm_w,
            'gdn_w_out': gdn_w_out, 'dswa_w_in': dswa_w_in, 'dswa_w_out': dswa_w_out,
            'mlp_w1': mlp_w1, 'mlp_w2': mlp_w2}

def second_block(x, norm_mix, norm_mlp, norm_final, rel_bias, gdn_w_in, gdn_conv_w,
              gdn_a_log, gdn_dt_bias, gdn_norm_w, gdn_w_out, dswa_w_in, dswa_w_out,
              mlp_w1, mlp_w2):
    for i in range(DEPTH_2):
        h = rmsnorm_2(x, norm_mix[i])
        j = i // N_MIXERS
        if i % N_MIXERS == 0:
            y = gated_deltanet_bidir(h, gdn_w_in[j], gdn_conv_w[j], gdn_a_log[j],
                                     gdn_dt_bias[j], gdn_norm_w[j], gdn_w_out[j])
        else:
            y = dilated_window_attention(h, dswa_w_in[j], dswa_w_out[j], rel_bias)
        x = x + y
        h = rmsnorm_2(x, norm_mlp[i])
        x = x + squared_relu_mlp(h, mlp_w1[i], mlp_w2[i])
    return rmsnorm_2(x, norm_final)


def setup_inputs(seed=0):
    out = dict(first_inputs(seed))
    for name, value in second_inputs(seed + 1).items():
        if name != "x":
            out[name + "_2"] = value
    return out


def reference(
    x, mem, positions, g_mix, g_mem, w_in, gate_b, attn_sink, conv_w, conv_b, lru_wr, lru_br,
    lru_wi, lru_bi, lru_lambda, w_mem_kv, p_attn, p_lru, p_mem, w_out, g_ffn, w_peer_q,
    peer_sub_keys, peer_u, peer_v, g_final, norm_mix_2, norm_mlp_2, norm_final_2, rel_bias_2,
    gdn_w_in_2, gdn_conv_w_2, gdn_a_log_2, gdn_dt_bias_2, gdn_norm_w_2, gdn_w_out_2,
    dswa_w_in_2, dswa_w_out_2, mlp_w1_2, mlp_w2_2,
):
    x = first_block(
        x, mem, positions, g_mix, g_mem, w_in, gate_b, attn_sink, conv_w, conv_b, lru_wr,
        lru_br, lru_wi, lru_bi, lru_lambda, w_mem_kv, p_attn, p_lru, p_mem, w_out, g_ffn,
        w_peer_q, peer_sub_keys, peer_u, peer_v, g_final,
    )
    return second_block(
        x, norm_mix_2, norm_mlp_2, norm_final_2, rel_bias_2, gdn_w_in_2, gdn_conv_w_2,
        gdn_a_log_2, gdn_dt_bias_2, gdn_norm_w_2, gdn_w_out_2, dswa_w_in_2, dswa_w_out_2,
        mlp_w1_2, mlp_w2_2,
    )


_drawn_inputs = setup_inputs


def setup_inputs(seed=0):
    import zlib

    import numpy as np

    out = dict(_drawn_inputs(seed))
    spreads = {}
    factors = {'g_mix': 2.789,
     'g_mem': 7.456,
     'gate_b': 6.191,
     'attn_sink': 64.0,
     'lru_br': 8.0,
     'lru_bi': 6.516,
     'norm_mix_2': 3.122,
     'norm_final_2': 23.495,
     'rel_bias_2': 50.368,
     'gdn_norm_w_2': 16.45,
     'g_ffn': 8.0,
     'norm_mlp_2': 8.0,
     'dswa_w_in_2': 2.858,
     'dswa_w_out_2': 2.842}
    for name, (base, spread) in spreads.items():
        noise = np.random.default_rng([zlib.crc32(name.encode()), seed]).standard_normal(out[name].shape)
        drawn = base * np.exp(spread * noise) if base else spread * noise
        out[name] = __import__('jax').numpy.asarray(drawn.astype(out[name].dtype))
    for name, factor in factors.items():
        out[name] = (out[name] * factor).astype(out[name].dtype)
    return out
```

```python
from contextlib import ExitStack

import numpy as np

import concourse.bass as bass
from concourse import mybir

F32 = mybir.dt.float32
I32 = mybir.dt.int32
U32 = mybir.dt.uint32
F32R = mybir.dt.float32r
ALU = mybir.AluOpType
ACT = mybir.ActivationFunctionType
AX = mybir.AxisListType

P = 128
S = 256
TT = S // P
D = 1024
KC = D // P
RING = 4
UNIT = 2048
EPS = 1e-6
NEG = -1e30
BIG = 1e30

HEADS, KV_HEADS, MEM_HEADS = 6, 2, 4
GROUP = HEADS // KV_HEADS
SCALE = float(P) ** -0.5
LRU_B = 6
CONV = 4
FF = 4096
PEER_H, TOPK, KEYS = 8, 16, 128
GDN_H = 8
GDN_CONV = 5
DS_HEADS, DS_E, DS_PER = 18, 64, 6
DS_DIL = (1, 4, 16)
DS_HALF = 64
BUCKETS = 32
TWO_PI = 2.0 * np.pi

STREAM = [
    ("mem_k", 2), ("mem_v", 2), ("q", 3), ("k", 1), ("v", 1), ("mem_q", 2),
    ("lru_x", 3), ("lru_gate", 3), ("lru_w", 2), ("gates", 12),
    ("merge", 8), ("out", 4), ("peer_q", 8), ("peer", 128),
    ("gdn_qkv", 12), ("gdn_z", 4), ("gdn_out", 4), ("mlp1_0", 16), ("mlp2_0", 16),
    ("ds_in", 14), ("ds_out", 5), ("mlp1_1", 16), ("mlp2_1", 16),
]
FIRST = {}
_n = 0
for _name, _units in STREAM:
    FIRST[_name] = _n
    _n += _units
UNITS = _n

COLS = [
    ("g_mix", KC), ("g_mem", KC), ("g_ffn", KC), ("g_a", KC), ("g_mlp0", KC), ("g_b", KC),
    ("g_mlp1", KC), ("gate_b", 24), ("conv_w", CONV * LRU_B), ("conv_b", LRU_B),
    ("lru_b", 4 * LRU_B), ("lam", 2 * LRU_B), ("gdn_conv", GDN_CONV * 24), ("gdn_norm", 1),
]
COL = {}
_n = 0
for _name, _units in COLS:
    COL[_name] = _n
    _n += _units
NCOLS = _n
ROWS = {"sink": 0, "a_log": HEADS, "dt_bias": HEADS + 16}
NROWS = HEADS + 32

CONSTS = [
    ("ident", P), ("ones", P), ("iota", P), ("rot", P), ("inv_freq", 1), ("window", TT * S),
    ("cum", 2 * P), ("far_a", 4 * P), ("far_i", 4 * P), ("levels", 7 * 4 * P),
]
CON = {}
_n = 0
for _name, _units in CONSTS:
    CON[_name] = _n
    _n += _units
NCON = _n
DELTAS = 2 * S


def shape_constants():
    c = np.zeros((P, NCON), np.float32)

    def put(name, value):
        value = np.asarray(value, np.float32)
        c[:, CON[name]:CON[name] + value.shape[1]] = value

    i = np.arange(P)
    put("ident", np.eye(P))
    put("ones", np.ones((P, P)))
    put("iota", np.tile(i, (P, 1)))
    rot = np.zeros((P, P))
    for n in range(16):
        rot[n + 16, n] = -1.0
        rot[n, n + 16] = 1.0
    put("rot", rot)
    freq = np.zeros((P, 1), np.float32)
    inv = np.float32(500000.0) ** (-np.arange(0, 32, 2, dtype=np.float32) / np.float32(32))
    freq[0:16, 0] = inv
    freq[16:32, 0] = inv
    put("inv_freq", freq)
    q = np.arange(TT)[None, :, None] * P + i[:, None, None]
    k = np.arange(S)[None, None, :]
    put("window", np.where(np.abs(k - q) <= 128, 0.0, NEG).reshape(P, -1))
    before = (i[:, None] <= i[None, :]).astype(np.float32)
    put("cum", np.concatenate([before, before.T], 1))
    row, col = i[:, None], i[None, :]
    lower = row > col
    strict = [lower, lower, lower.T, lower.T]
    put("far_a", np.concatenate([np.where(m, 0.0, BIG) for m in strict], 1))
    incl = [row <= col, row <= col, row >= col, row >= col]
    put("far_i", np.concatenate([np.where(m, 0.0, -BIG) for m in incl], 1))
    levels = []
    for n in range(7):
        same = (row >> (n + 1)) == (col >> (n + 1))
        other = (row >> n) != (col >> n)
        low = same & other & lower
        levels.append(np.concatenate([low, low, low.T, low.T], 1))
    put("levels", np.concatenate(levels, 1))
    return c


def distance_constants():
    rel = np.arange(DELTAS) - (S - 1)
    n = np.abs(rel)
    half, exact = BUCKETS // 2, BUCKETS // 4
    nf = np.maximum(n, 1).astype(np.float32)
    large = exact + (np.log(nf / np.float32(exact)) / np.float32(np.log(1024 / exact))
                     * np.float32(half - exact)).astype(np.int32)
    bucket = np.where(rel > 0, half, 0) + np.where(n < exact, n, np.minimum(large, half - 1))
    hot = (np.arange(BUCKETS)[:, None] == bucket[None, :]).astype(np.float32)
    seen = np.zeros((DS_HEADS, DELTAS), np.float32)
    for h in range(DS_HEADS):
        d = DS_DIL[h // DS_PER]
        seen[h] = np.where((rel % d == 0) & (n <= DS_HALF * d), 0.0, NEG)
    return hot, seen


class Count:

    def __init__(self, sem):
        self.sem, self.n, self.turn = sem, 0, 0

    def up(self, instruction):
        instruction.then_inc(self.sem, 1)
        self.n += 1

    def settle(self, eng):
        eng.wait_ge(self.sem, self.turn + self.n)

    def enter(self, i, each):
        self.start, self.each, self.turn = self.n, each, i * each

    def leave(self, turns):
        assert self.n - self.start == self.each, (self.n - self.start, self.each)
        self.n, self.turn = self.start + turns * self.each, 0


class Kernel:
    pass


def carve(k, at, *dims):
    n = int(np.prod(dims))
    assert at + n <= k.ARENA, (at, n)
    v = k.arena[:, at:at + n]
    if len(dims) == 1:
        return v
    names = "abcd"[:len(dims)]
    return v.rearrange(f"p ({' '.join(names)}) -> p {' '.join(names)}",
                       **{x: d for x, d in zip(names[1:], dims[1:])})


class Layout:

    def __init__(self, k, at=0):
        self.k, self.at = k, at

    def take(self, *dims):
        v = carve(self.k, self.at, *dims)
        self.at += int(np.prod(dims))
        return v


def halves(ap):
    return ap.rearrange("p (a b) -> p a b", a=2)


def stream(k, sp, until):
    until = min(until, UNITS)
    u = k.issued

    def load(slot, unit):
        sp.dma_start(k.ring[:, slot, :], k.weights[bass.ds(unit, 1), :, :].rearrange("a p n -> p (a n)"))\
          .then_inc(k.w_loaded[slot], 16)

    while u < until:
        turns = (until - u) // RING
        if u % RING == 0 and u >= RING and turns >= 3:
            with sp.Fori(0, turns) as i:
                for s in range(RING):
                    sp.wait_ge(k.unit_done, i * RING + (u + s - RING + 1))
                    load(s, i * RING + (u + s))
            u += turns * RING
            continue
        if u >= RING:
            sp.wait_ge(k.unit_done, u - RING + 1)
        load(u % RING, u)
        u += 1
    k.issued = until


def loaded(k, pe, u, turn=0):
    pe.wait_ge(k.w_loaded[u % RING], 16 * (u // RING + 1) + turn * 16)


def slot(k, u):
    return k.ring[:, u % RING, :].rearrange("p (c n) -> p c n", c=8)


def unit_T(k, pe, u, srcT, out, turn=0):
    loaded(k, pe, u, turn)
    w = slot(k, u)
    for nb in range(2):
        for c in range(8):
            last = pe.matmul(out[:, nb * S:(nb + 1) * S], w[:, c, nb * P:(nb + 1) * P], srcT[:, c, :],
                             start=(c == 0), stop=(c == 7))
    last.then_inc(k.unit_done, 1)


def unit_N(k, pe, u, srcT, out, turn=0, first=True, final=True):
    loaded(k, pe, u, turn)
    w = slot(k, u)
    for tt in range(TT):
        for c in range(8):
            last = pe.matmul(out[tt], srcT[:, c, tt * P:(tt + 1) * P], w[:, c, :],
                             start=(first and c == 0), stop=(final and c == 7))
    last.then_inc(k.unit_done, 1)


def plain(ap):
    return ap.bitcast(F32)


def split_hi(k, act, u, turn=0, ring_turn=0):
    act.wait_ge(k.w_loaded[u % RING], 16 * (u // RING + 1) + ring_turn * 16)
    if u >= 2:
        act.wait_ge(k.unit_done, turn + (u - 1))
    act.activation(k.w_hi[:, u % 2, :], k.ring[:, u % RING, :], ACT.Copy).then_inc(k.hi_ready, 1)


def split_lo(k, dve, u, turn=0):
    dve.wait_ge(k.hi_ready, turn + (u - k.whole_units + 1))
    dve.tensor_tensor(k.ring_lo[:, u % RING, :], k.ring[:, u % RING, :], plain(k.w_hi[:, u % 2, :]), ALU.subtract).then_inc(k.lo_ready, 1)


def unit_parts(k, u):
    return [ap.rearrange("p (c n) -> p c n", c=8) for ap in (k.w_hi[:, u % 2, :], k.ring_lo[:, u % RING, :])]


def split_ready(k, pe, u, n, turn=0):
    if n == 0:
        pe.wait_ge(k.hi_ready, turn + (u - k.whole_units + 1))
    if n == 2:
        pe.wait_ge(k.lo_ready, turn + (u - k.whole_units + 1))


def unit_T_split(k, pe, u, h_hi, h_lo, out, turn=0):
    hi, lo = unit_parts(k, u)
    for nb in range(2):
        for n, (w, h) in enumerate(((hi, h_hi), (hi, h_lo), (lo, h_hi))):
            if nb == 0:
                split_ready(k, pe, u, n, turn)
            for c in range(8):
                last = pe.matmul(out[:, nb * S:(nb + 1) * S], w[:, c, nb * P:(nb + 1) * P], h(c),
                                 start=(n == 0 and c == 0), stop=(n == 2 and c == 7))
    last.then_inc(k.unit_done, 1)


def normalise(k, src, gcol, dstT, lay_at, split=False):
    nc = k.nc
    lay = Layout(k, lay_at)
    junk, xn = lay.take(TT, D), lay.take(TT, D)
    st = k.small[:, 0:8]
    n, m = k.norms, k.norms_T
    own = k.norm_steps
    with nc.Block() as block:
        @block.sync
        def _(sp):
            stream(k, sp, k.stream_to)

        @block.scalar
        def _(act):
            norm_roots(k, act, src, junk, st)
            if split:
                for j in range(4):
                    act.wait_ge(k.turned, 4 * m + j + 1)
                    for c in range(2):
                        last = act.activation(k.hT_hi[:, 2 * j + c, :], k.ps[j][:, c * S:(c + 1) * S],
                                              ACT.Copy, scale=gcol[:, 2 * j + c:2 * j + c + 1])
                    last.then_inc(k.rounded_out, 1)
                return
            for j in range(0, 4, 2):
                act.wait_ge(k.turned, 4 * m + j + 1)
                for c in range(2):
                    act.activation(dstT[:, 2 * j + c, :], k.ps[j][:, c * S:(c + 1) * S], ACT.Copy,
                                   scale=gcol[:, 2 * j + c:2 * j + c + 1])

        @block.vector
        def _(dve):
            norm_means(k, dve, own, st)
            for tt in range(TT):
                dve.tensor_scalar(xn[:, tt, :], src[:, tt, :], st[:, 6 + tt:7 + tt], None,
                                  ALU.mult).then_inc(k.scaled, 1)
            if split:
                for j in range(4):
                    dve.wait_ge(k.rounded_out, 4 * k.splits + j + 2)
                    for c in range(2):
                        n = 2 * j + c
                        dve.scalar_tensor_tensor(out=k.hT_lo[:, n, :], in0=k.ps[j][:, c * S:(c + 1) * S],
                                                 scalar=gcol[:, n:n + 1], in1=plain(k.hT_hi[:, n, :]), op0=ALU.mult,
                                                 op1=ALU.subtract)
                k.splits += 1
                return
            for j in range(1, 4, 2):
                dve.wait_ge(k.turned, 4 * m + j + 1)
                for c in range(2):
                    dve.tensor_scalar(dstT[:, 2 * j + c, :], k.ps[j][:, c * S:(c + 1) * S],
                                      gcol[:, 2 * j + c:2 * j + c + 1], None, ALU.mult)

        @block.tensor
        def _(pe):
            pe.wait_ge(k.scaled, TT * (m + 1))
            for j in range(4):
                for c in range(2):
                    for tt in range(TT):
                        last = pe.transpose(k.ps[j][:, c * S + tt * P:c * S + (tt + 1) * P],
                                            xn[:, tt, (2 * j + c) * P:(2 * j + c + 1) * P], k.ident)
                last.then_inc(k.turned, 1)
    k.norms, k.norms_T = n + 1, m + 1


def norm_roots(k, act, src, junk, st):
    for tt in range(TT):
        act.activation(junk[:, tt, :], src[:, tt, :], ACT.Square,
                       accum_out=st[:, tt:tt + 1]).then_inc(k.squares, 1)
    act.wait_ge(k.mean_ready, k.norms + 1)
    act.activation(st[:, 6:8], st[:, 4:6], ACT.Sqrt).then_inc(k.root_ready, 1)


def norm_means(k, dve, own, st):
    dve.wait_ge(k.squares, TT * (k.norms + 1))
    own.up(dve.tensor_scalar(st[:, 2:4], st[:, 0:2], 1.0 / D, EPS, ALU.mult, ALU.add))
    own.settle(dve)
    dve.reciprocal(st[:, 4:6], st[:, 2:4]).then_inc(k.mean_ready, 1)
    dve.wait_ge(k.root_ready, k.norms + 1)


def normalise_rows(k, src, g_dram, dst):
    st = k.small[:, 0:8]
    lay = Layout(k, 0)
    junk, g_rows = lay.take(TT, D), lay.take(D)
    with k.nc.Block() as block:
        @block.sync
        def _(sp):
            sp.dma_start(g_rows, g_dram.partition_broadcast(P)).then_inc(k.g_here, 16)
            stream(k, sp, k.stream_to)

        @block.scalar
        def _(act):
            norm_roots(k, act, src, junk, st)

        @block.vector
        def _(dve):
            norm_means(k, dve, k.norm_steps, st)
            k.rows_normed += 1
            dve.wait_ge(k.g_here, 16 * k.rows_normed)
            for tt in range(TT):
                dve.scalar_tensor_tensor(out=dst[:, tt, :], in0=src[:, tt, :], scalar=st[:, 6 + tt:7 + tt],
                                         in1=g_rows, op0=ALU.mult, op1=ALU.mult)
    k.norms += 1


def ctx_sem(k, name):
    return k.stack.enter_context(k.nc.semaphore(name))


def load_and_tables(k):
    lay = Layout(k, 24576)
    posi = lay.take(S).bitcast(I32)
    pos, ang = lay.take(S), lay.take(S)
    turns, red = lay.take(2, S), lay.take(2, S)
    here_a, steps, reduced = ctx_sem(k, "params_here"), Count(ctx_sem(k, "table_steps")), ctx_sem(k, "reduced")
    here = ctx_sem(k, "inputs_here")
    c = k.consts
    with k.nc.Block() as block:
        @block.sync
        def _(sp):
            sp.dma_start(k.x[:, :, :], k.x_dram.rearrange("(t p) d -> p t d", p=P)).then_inc(here, 16)
            sp.dma_start(k.mem_rows, k.mem_dram.rearrange("(t p) d -> p t d", p=P)).then_inc(here, 16)
            for s in range(RING):
                sp.dma_start(k.ring[:, s, :], k.weights[s]).then_inc(k.w_loaded[s], 16)
            k.issued = RING

        @block.scalar
        def _(act):
            act.dma_start(posi, k.pos_dram.partition_broadcast(P)).then_inc(here_a, 16)
            act.dma_start(k.consts[:, :], k.consts_dram[:, 0:CON["window"]]).then_inc(here_a, 16)
            act.dma_start(k.cols[:, :], k.cols_dram).then_inc(here_a, 16)
            act.dma_start(k.rows[:, :], k.rows_dram.partition_broadcast(P)).then_inc(here_a, 16)
            act.wait_ge(reduced, 1)
            act.activation(k.sin, red[:, 0, :], ACT.Sin)
            act.activation(k.cos, red[:, 1, :], ACT.Sin)

        @block.vector
        def _(dve):
            dve.wait_ge(here_a, 64)
            dve.wait_ge(here, 32)
            steps.up(dve.tensor_copy(pos, posi))
            steps.settle(dve)
            steps.up(dve.tensor_scalar(ang, pos, c[:, CON["inv_freq"]:CON["inv_freq"] + 1], None, ALU.mult))
            steps.settle(dve)
            magic = 12582912.0
            for n, ahead in enumerate((0.0, 0.25)):
                steps.up(dve.tensor_scalar(turns[:, n, :], ang, 1.0 / TWO_PI, ahead, ALU.mult, ALU.add))
                steps.settle(dve)
                steps.up(dve.tensor_scalar(turns[:, n, :], turns[:, n, :], magic, None, ALU.add))
                steps.settle(dve)
                steps.up(dve.tensor_scalar(turns[:, n, :], turns[:, n, :], -magic, None, ALU.add))
                steps.settle(dve)
                steps.up(dve.scalar_tensor_tensor(out=red[:, n, :], in0=turns[:, n, :], scalar=-6.28125,
                                                  in1=ang, op0=ALU.mult, op1=ALU.add))
                steps.settle(dve)
                steps.up(dve.scalar_tensor_tensor(out=red[:, n, :], in0=turns[:, n, :],
                                                  scalar=-(TWO_PI - 6.28125), in1=red[:, n, :],
                                                  op0=ALU.mult, op1=ALU.add))
                steps.settle(dve)
                steps.up(dve.tensor_scalar(red[:, n, :], red[:, n, :], n * np.pi / 2, 3.1415925,
                                           ALU.add, ALU.min))
                steps.settle(dve)
                last = dve.tensor_scalar(red[:, n, :], red[:, n, :], -3.1415925, None, ALU.max)
                if n == 0:
                    steps.up(last)
                    steps.settle(dve)
            last.then_inc(reduced, 1)



def col(k, name, n=1, at=0):
    return k.cols[:, COL[name] + at:COL[name] + at + n]


def over(ap, n):
    return ap.rearrange("p (a s) -> p a s", a=1).to_broadcast([P, n, ap.shape[1]])


def softplus(dve, own, x, out, tmp, abs_ready, exp_ready):
    _, e, t, t2, p = tmp
    dve.scalar_tensor_tensor(out=tmp[0], in0=x, scalar=-1.0, in1=x, op0=ALU.mult, op1=ALU.max).then_inc(abs_ready, 1)
    dve.wait_ge(exp_ready, 1)
    own.up(dve.tensor_scalar(p, e, 2.0, None, ALU.add))
    own.settle(dve)
    own.up(dve.reciprocal(t2, p))
    own.settle(dve)
    own.up(dve.tensor_tensor(t, e, t2, ALU.mult))
    own.settle(dve)
    own.up(dve.tensor_tensor(t2, t, t, ALU.mult))
    own.settle(dve)
    own.up(dve.tensor_scalar(p, t2, 1.0 / 15, None, ALU.mult))
    own.settle(dve)
    for c in (13, 11, 9, 7, 5, 3):
        own.up(dve.scalar_tensor_tensor(out=p, in0=p, scalar=1.0 / c, in1=t2, op0=ALU.add, op1=ALU.mult))
        own.settle(dve)
    own.up(dve.scalar_tensor_tensor(out=p, in0=p, scalar=1.0, in1=t, op0=ALU.add, op1=ALU.mult))
    own.settle(dve)
    own.up(dve.tensor_scalar(t, x, 0.0, 0.5, ALU.max, ALU.mult))
    own.settle(dve)
    own.up(dve.tensor_tensor(t2, p, t, ALU.add))
    own.settle(dve)
    own.up(dve.tensor_scalar(out, t2, 2.0, None, ALU.mult))
    own.settle(dve)


def done_mark(k, pe, sem):
    pe.matmul(k.ps[7][0:1, 511:512], k.ident[:, 0:1], k.ident[:, 0:1], start=True, stop=True).then_inc(sem, 1)


def mixer_layout(k):
    lay = Layout(k, 0)
    m = k.mix
    m.kmT = lay.take(MEM_HEADS, S)
    m.vm = lay.take(TT, MEM_HEADS * P)
    m.qkT = lay.take(HEADS + KV_HEADS, S)
    m.va = lay.take(TT, KV_HEADS * P)
    m.qmT = lay.take(MEM_HEADS, S)
    m.xl = lay.take(LRU_B, S + CONV - 1)
    m.gl = lay.take(LRU_B, S)
    m.xc = lay.take(LRU_B, S)
    k.gatesT = lay.take(24, S)
    k.branchT = lay.take(16, S)
    m.free = lay.at


def projections(k):
    m, ps, U = k.mix, k.ps, FIRST
    acc, rope_ps = [ps[0], ps[1]], ps[5]
    lay = Layout(k, m.free)
    k.memT = lay.take(KC, S)
    raw = lay.take(2, 2, S)
    rot1, rot2 = lay.take(2, S), lay.take(2, S)
    soft = [lay.take(2 * LRU_B) for _ in range(5)]
    neg_lam, m_soft = lay.take(2 * LRU_B), lay.take(2 * LRU_B)
    names = ("acc_out", "rot_ready", "rot_used", "lam_abs", "lam_exp")
    acc_out, rot_ready, rot_used, lam_abs, lam_exp = (ctx_sem(k, n) for n in names)
    own = Count(ctx_sem(k, "projections_dve"))
    parts = [
        ("mem_k", 2, True, k.memT, lambda n: m.kmT[:, 2 * n:2 * n + 2, :]),
        ("mem_v", 2, False, k.memT, lambda n: m.vm[:, :, n * S:(n + 1) * S]),
        ("q", 3, True, k.hT, lambda n: raw[:, n % 2, :, :]),
        ("k", 1, True, k.hT, lambda n: raw[:, 1, :, :]),
        ("v", 1, False, k.hT, lambda n: m.va[:, :, :]),
        ("mem_q", 2, True, k.hT, lambda n: m.qmT[:, 2 * n:2 * n + 2, :]),
        ("lru_x", 3, True, k.hT, lambda n: m.xl[:, 2 * n:2 * n + 2, 2:2 + S]),
        ("lru_gate", 3, True, k.hT, lambda n: m.gl[:, 2 * n:2 * n + 2, :]),
    ]
    FIRST_RAW = 4
    with k.nc.Block() as block:
        @block.sync
        def _(sp):
            stream(k, sp, U["lru_w"] + RING)

        @block.tensor
        def _(pe):
            def rotate(n):
                pe.wait_ge(acc_out, FIRST_RAW + n + 1)
                if n >= 1:
                    pe.wait_ge(rot_used, n)
                pe.matmul(rope_ps[:, :], k.rot, raw[:, n % 2, :, :].rearrange("p a s -> p (a s)"),
                          start=True, stop=True).then_inc(rot_ready, 1)

            use = 0
            for name, units, turned, src, _ in parts:
                for n in range(units):
                    bank = acc[use % 2]
                    if use >= 2:
                        pe.wait_ge(acc_out, use - 1)
                    if turned:
                        unit_T(k, pe, U[name] + n, src, bank)
                    else:
                        unit_N(k, pe, U[name] + n, src, [bank[:, 0:S], bank[:, S:2 * S]])
                    use += 1
                    if FIRST_RAW + 1 < use <= FIRST_RAW + 5:
                        rotate(use - FIRST_RAW - 2)

        @block.scalar
        def _(act):
            act.wait_ge(lam_abs, 1)
            act.activation(soft[1], soft[0], ACT.Exp, scale=-1.0).then_inc(lam_exp, 1)
            use = 0
            for name, units, _, _, dst in parts:
                for n in range(units):
                    act.wait_ge(k.unit_done, U[name] + n + 1)
                    if FIRST_RAW + 2 <= use < FIRST_RAW + 4:
                        act.wait_ge(rot_used, use - FIRST_RAW - 1)
                    func = ACT.Gelu_apprx_tanh if name == "lru_gate" else ACT.Copy
                    act.activation(dst(n), halves(acc[use % 2][:, :]), func).then_inc(acc_out, 1)
                    use += 1

        @block.vector
        def _(dve):
            own.up(dve.memset(m.xl[:, :, 0:2], 0.0))
            own.up(dve.memset(m.xl[:, :, 2 + S:3 + S], 0.0))
            own.up(dve.tensor_scalar(neg_lam, col(k, "lam", 2 * LRU_B), -1.0, None, ALU.mult))
            own.up(dve.tensor_scalar(k.half_b[:, 0:24], col(k, "gate_b", 24), 0.5, None, ALU.mult))
            own.up(dve.tensor_scalar(k.half_b[:, 24:48], col(k, "lru_b", 24), 0.5, None, ALU.mult))
            own.settle(dve)
            softplus(dve, own, neg_lam, m_soft, soft, lam_abs, lam_exp)
            own.up(dve.tensor_scalar(k.rate[:, :], m_soft, -4.0, None, ALU.mult))
            for n in range(4):
                dve.wait_ge(acc_out, FIRST_RAW + n + 1)
                own.up(dve.tensor_tensor(rot1, raw[:, n % 2, :, :], over(k.cos, 2), ALU.mult))
                dve.wait_ge(rot_ready, n + 1)
                own.up(dve.tensor_tensor(rot2, halves(rope_ps[:, :]), over(k.sin, 2), ALU.mult))
                own.settle(dve)
                dve.tensor_tensor(m.qkT[:, 2 * n:2 * n + 2, :], rot1, rot2, ALU.add).then_inc(rot_used, 1)
                dve.wait_ge(rot_used, n + 1)
            dve.wait_ge(acc_out, 14)
            w, b = col(k, "conv_w", CONV * LRU_B), col(k, "conv_b", LRU_B)
            for h in range(LRU_B):
                own.up(dve.tensor_scalar(m.xc[:, h, :], m.xl[:, h, 0:S], w[:, h:h + 1], b[:, h:h + 1],
                                         ALU.mult, ALU.add))
            for j in range(1, CONV):
                own.settle(dve)
                for h in range(LRU_B):
                    own.up(dve.scalar_tensor_tensor(out=m.xc[:, h, :], in0=m.xl[:, h, j:j + S],
                                                    scalar=w[:, LRU_B * j + h:LRU_B * j + h + 1],
                                                    in1=m.xc[:, h, :], op0=ALU.mult, op1=ALU.add))


def attention(k):
    m, ps, U = k.mix, k.ps, FIRST
    acc, score, pt, out_ps = [ps[0], ps[1]], [ps[2], ps[3]], ps[4], ps[6]
    lay = Layout(k, m.free)
    prob, ptS = lay.take(2, TT, S), lay.take(2, 2, S)
    th = lay.take(2, 2, LRU_B, S)
    twice, bx = lay.take(2, LRU_B, S), lay.take(2, LRU_B, S)
    window = lay.take(TT, S)
    stat = k.small[:, 16:48]
    HN, NG = HEADS + MEM_HEADS, 12
    names = ("gate_out", "lru_out", "window_here", "scores", "probs", "pt_ready", "pt_out", "pv_ready",
             "pv_out", "maxed", "exped", "lru_mm", "lru_log", "lru_exp", "lru_in", "lru_root")
    (gate_out, lru_out, window_here, scores, probs, pt_ready, pt_out, pv_ready, pv_out, maxed, exped,
     lru_mm, lru_log, lru_exp, lru_in, lru_root) = (ctx_sem(k, n) for n in names)
    own = Count(ctx_sem(k, "attention_dve"))
    gates_at = [1] * 9 + [2, 1]
    gate_unit = [U["gates"] + n for n in range(NG)]
    assert sum(gates_at) == NG

    def is_mem(t):
        return t < MEM_HEADS

    def exps_to(t):
        return 2 * (t + 1) + max(0, t + 1 - MEM_HEADS)

    def lru(pe):
        for n in range(2):
            u = U["lru_w"] + n
            loaded(k, pe, u)
            for b in range(16 if n == 0 else 8):
                blk = 16 * n + b
                pair, d = blk // 2, blk % 2
                if d == 0 and pair >= 2:
                    pe.wait_ge(lru_out, 2 * (pair - 1))
                last = pe.matmul(acc[pair % 2][:, d * S:(d + 1) * S], k.ring[:, u % RING, b * P:(b + 1) * P],
                                 m.xc[:, pair % LRU_B, :], start=True, stop=True)
                if d == 1:
                    last.then_inc(lru_mm, 1)
            done_mark(k, pe, k.unit_done)

    def pdhs(ap):
        return ap.rearrange("p d h s -> p (d h s)")

    with k.nc.Block() as block:
        @block.sync
        def _(sp):
            sp.dma_start(window, k.consts_dram[:, CON["window"]:CON["window"] + TT * S]
                         .rearrange("p (t s) -> p t s", t=TT)).then_inc(window_here, 16)
            stream(k, sp, U["merge"] + RING)

        @block.tensor
        def _(pe):
            def gate(n):
                if n >= 2:
                    pe.wait_ge(gate_out, 2 * (n - 1))
                if n < 2:
                    pe.wait_ge(lru_out, 24)
                unit_T(k, pe, gate_unit[n], k.hT, acc[n % 2])

            def score_mm(t):
                if t >= 2:
                    pe.wait_ge(exped, exps_to(t - 2))
                qT = m.qmT[:, t, :] if is_mem(t) else m.qkT[:, t - MEM_HEADS, :]
                kT = m.kmT[:, t, :] if is_mem(t) else m.qkT[:, HEADS + (t - MEM_HEADS) // GROUP, :]
                for tt in range(TT):
                    last = pe.matmul(score[t % 2][:, tt * S:(tt + 1) * S], qT[:, tt * P:(tt + 1) * P], kT,
                                     start=True, stop=True)
                last.then_inc(scores, 1)

            def turn_probs(t):
                pe.wait_ge(probs, t + 1)
                if t >= 1:
                    pe.wait_ge(pt_out, t)
                for kt in range(TT):
                    for tt in range(TT):
                        last = pe.transpose(pt[:, kt * S + tt * P:kt * S + (tt + 1) * P],
                                            prob[:, t % 2, tt, kt * P:(kt + 1) * P], k.ident)
                last.then_inc(pt_ready, 1)

            def weigh(t):
                pe.wait_ge(pt_out, t + 1)
                if t >= 1:
                    pe.wait_ge(pv_out, t)
                g = t if is_mem(t) else (t - MEM_HEADS) // GROUP
                v = (m.vm if is_mem(t) else m.va)[:, :, g * P:(g + 1) * P]
                for kt in range(TT):
                    last = pe.matmul(out_ps[:, 0:S], v[:, kt, :], ptS[:, t % 2, kt, :],
                                     start=(kt == 0), stop=(kt == TT - 1))
                last.then_inc(pv_ready, 1)

            at = 0
            for t in range(HN + 1):
                if t < HN:
                    score_mm(t)
                if t >= 1:
                    turn_probs(t - 1)
                if t == 0:
                    lru(pe)
                for n in range(gates_at[t]):
                    gate(at)
                    at += 1
                if t >= 1:
                    weigh(t - 1)

        @block.scalar
        def _(act):
            for pair in range(2 * LRU_B):
                g, h = pair // LRU_B, pair % LRU_B
                act.wait_ge(lru_mm, pair + 1)
                for d in range(2):
                    at = 24 + (2 * g + d) * LRU_B + h
                    act.activation(th[:, g, d, h, :], acc[pair % 2][:, d * S:(d + 1) * S], ACT.Tanh, scale=0.5,
                                   bias=k.half_b[:, at:at + 1]).then_inc(lru_out, 1)
            act.wait_ge(lru_log, 1)
            act.activation(pdhs(th[:, 1]), pdhs(th[:, 0]), ACT.Tanh, scale=-1.0).then_inc(lru_exp, 1)
            act.wait_ge(lru_exp, 1)
            act.activation(pdhs(th[:, 0]), pdhs(th[:, 0]), ACT.Exp).then_inc(lru_exp, 1)
            at = 0
            for t in range(HN + 1):
                if t >= 1:
                    act.wait_ge(pt_ready, t)
                    if t >= 3:
                        act.wait_ge(pv_ready, t - 2)
                    act.activation(ptS[:, (t - 1) % 2, :, :], halves(pt[:, :]), ACT.Copy).then_inc(pt_out, 1)
                if t < HN:
                    o = 16 * (t % 2)
                    act.wait_ge(maxed, t + 1)
                    if t >= 2 and is_mem(t):
                        act.wait_ge(pt_ready, t - 1)
                    for tt in range(TT):
                        src = score[t % 2][:, tt * S:(tt + 1) * S] if is_mem(t) else prob[:, t % 2, tt, :]
                        act.activation(prob[:, t % 2, tt, :], src, ACT.Exp,
                                       bias=stat[:, o + 2 + tt:o + 3 + tt], scale=SCALE if is_mem(t) else 1.0,
                                       accum_out=stat[:, o + 4 + tt:o + 5 + tt]).then_inc(exped, 1)
                    if not is_mem(t):
                        act.activation(stat[:, o + 8:o + 10], stat[:, o + 6:o + 8], ACT.Exp).then_inc(exped, 1)
                for n in range(gates_at[t]):
                    act.wait_ge(k.unit_done, gate_unit[at] + 1)
                    for b in range(2):
                        act.activation(k.gatesT[:, 2 * at + b, :], acc[at % 2][:, b * S:(b + 1) * S], ACT.Tanh,
                                       scale=0.5, bias=k.half_b[:, 2 * at + b:2 * at + b + 1]).then_inc(gate_out, 1)
                    at += 1
                if t >= 1:
                    act.wait_ge(pv_ready, t)
                    chunk = 12 + t - 1 if is_mem(t - 1) else t - 1 - MEM_HEADS
                    act.activation(k.branchT[:, chunk, :], out_ps[:, 0:S], ACT.Copy).then_inc(pv_out, 1)
                if t == 4:
                    act.wait_ge(lru_in, 1)
                    act.activation(pdhs(th[:, 1]), pdhs(th[:, 1]), ACT.Sqrt, scale=0.25).then_inc(lru_root, 1)

        @block.vector
        def _(dve):
            def softmax(t):
                o = 16 * (t % 2)
                dve.wait_ge(scores, t + 1)
                if is_mem(t):
                    own.up(dve.tensor_reduce(stat[:, o:o + 2], halves(score[t % 2][:, :]), AX.X, ALU.max))
                    own.settle(dve)
                    dve.tensor_scalar(stat[:, o + 2:o + 4], stat[:, o:o + 2], -SCALE, None, ALU.mult)\
                       .then_inc(maxed, 1)
                    dve.wait_ge(exped, exps_to(t))
                    total = stat[:, o + 4:o + 6]
                else:
                    h = t - MEM_HEADS
                    sink = k.rows[:, h:h + 1]
                    if h == 0:
                        dve.wait_ge(window_here, 16)
                    dve.wait_ge(pt_ready, t - 1)
                    own.up(dve.scalar_tensor_tensor(out=prob[:, t % 2, :, :], in0=halves(score[t % 2][:, :]),
                                                    scalar=SCALE, in1=window, op0=ALU.mult, op1=ALU.add))
                    own.settle(dve)
                    own.up(dve.tensor_reduce(stat[:, o:o + 2], prob[:, t % 2, :, :], AX.X, ALU.max))
                    own.settle(dve)
                    own.up(dve.tensor_scalar(stat[:, o + 2:o + 4], stat[:, o:o + 2], sink, -1.0,
                                             ALU.max, ALU.mult))
                    own.settle(dve)
                    dve.tensor_scalar(stat[:, o + 6:o + 8], stat[:, o + 2:o + 4], sink, None, ALU.add)\
                       .then_inc(maxed, 1)
                    dve.wait_ge(exped, exps_to(t))
                    total = stat[:, o + 10:o + 12]
                    own.up(dve.tensor_tensor(total, stat[:, o + 4:o + 6], stat[:, o + 8:o + 10], ALU.add))
                    own.settle(dve)
                own.up(dve.reciprocal(stat[:, o + 12:o + 14], total))
                own.settle(dve)
                for tt in range(TT):
                    last = dve.tensor_scalar(prob[:, t % 2, tt, :], prob[:, t % 2, tt, :],
                                             stat[:, o + 12 + tt:o + 13 + tt], None, ALU.mult)
                    if tt == 0:
                        own.up(last)
                last.then_inc(probs, 1)
                own.settle(dve)
                dve.wait_ge(probs, t + 1)

            a, om = th[:, 0], th[:, 1]
            dve.wait_ge(lru_out, 24)
            for d in range(2):
                for h in range(LRU_B):
                    own.up(dve.tensor_scalar(th[:, 0, d, h, :], th[:, 0, d, h, :], 1.0,
                                             k.rate[:, d * LRU_B + h:d * LRU_B + h + 1], ALU.add, ALU.mult))
            for d in range(2):
                last = dve.scalar_tensor_tensor(out=flat(twice[:, d]), in0=flat(th[:, 1, d]), scalar=1.0,
                                                in1=flat(m.xc), op0=ALU.add, op1=ALU.mult)
                if d == 0:
                    own.up(last)
                    own.settle(dve)
            last.then_inc(lru_log, 1)
            softmax(0)
            softmax(1)
            dve.wait_ge(lru_exp, 2)
            own.up(dve.tensor_tensor(pdhs(bx), pdhs(a), pdhs(a), ALU.mult))
            own.settle(dve)
            dve.scalar_tensor_tensor(out=pdhs(om), in0=pdhs(bx), scalar=1.0, in1=pdhs(om), op0=ALU.add,
                                     op1=ALU.mult).then_inc(lru_in, 1)
            for t in range(2, 6):
                softmax(t)
            dve.wait_ge(lru_root, 1)
            own.up(dve.tensor_tensor(pdhs(bx), pdhs(om), pdhs(twice), ALU.mult))
            own.settle(dve)
            for h in range(LRU_B):
                own.up(dve.tensor_tensor_scan(out=twice[:, 0, h, :], data0=a[:, 0, h, :], data1=bx[:, 0, h, :],
                                              initial=0.0, op0=ALU.mult, op1=ALU.add))
                own.up(dve.tensor_tensor_scan(out=twice[:, 1, h, ::-1], data0=a[:, 1, h, ::-1],
                                              data1=bx[:, 1, h, ::-1], initial=0.0, op0=ALU.mult, op1=ALU.add))
            own.settle(dve)
            own.up(dve.tensor_tensor(flat(twice[:, 0]), flat(twice[:, 0]), flat(twice[:, 1]), ALU.add))
            own.settle(dve)
            own.up(dve.tensor_tensor(flat(k.branchT[:, 6:12, :]), flat(twice[:, 0]), flat(m.gl), ALU.mult))
            for t in range(6, HN):
                softmax(t)


def flat(ap):
    return ap.rearrange("p h s -> p (h s)")


def merge(k):
    ps, U = k.ps, FIRST
    lay = Layout(k, 0)
    mergedT = lay.take(KC, S)
    part = lay.take(2, 3, S)
    own = Count(ctx_sem(k, "merge_dve"))
    merged, out_used = ctx_sem(k, "merged"), ctx_sem(k, "out_used")
    chunks = [(0, 6), (6, 12), (12, 16)]

    with k.nc.Block() as block:
        @block.sync
        def _(sp):
            stream(k, sp, k.stream_to)

        @block.tensor
        def _(pe):
            for nb in range(8):
                u = U["merge"] + nb
                loaded(k, pe, u)
                if nb >= 2:
                    pe.wait_ge(merged, nb - 1)
                w = k.ring[:, u % RING, :].rearrange("p (c n) -> p c n", c=16)
                for b, (lo, hi) in enumerate(chunks):
                    bank = ps[2 * (nb % 2) + b // 2][:, (b % 2) * S:(b % 2 + 1) * S]
                    for c in range(lo, hi):
                        last = pe.matmul(bank, w[:, c, :], k.branchT[:, c, :], start=(c == lo), stop=(c == hi - 1))
                last.then_inc(k.unit_done, 1)
            pe.wait_ge(merged, 8)
            for n in range(4):
                bank = ps[4 + n]
                unit_N(k, pe, U["out"] + n, mergedT, [bank[:, 0:S], bank[:, S:2 * S]])

        @block.vector
        def _(dve):
            g = flat(k.gatesT)
            own.up(dve.tensor_scalar(g, g, 0.5, 0.5, ALU.mult, ALU.add))
            own.settle(dve)
            gates = k.gatesT.rearrange("p (b n) s -> p b n s", b=3)
            for nb in range(8):
                dve.wait_ge(k.unit_done, U["merge"] + nb + 1)
                a, b = halves(ps[2 * (nb % 2)][:, :]), ps[2 * (nb % 2) + 1][:, 0:S]
                own.up(dve.tensor_tensor(part[:, nb % 2, 0:2, :], a, gates[:, 0:2, nb, :], ALU.mult))
                own.up(dve.tensor_tensor(part[:, nb % 2, 2, :], b, gates[:, 2, nb, :], ALU.mult))
                own.settle(dve)
                own.up(dve.tensor_tensor(part[:, nb % 2, 0, :], part[:, nb % 2, 0, :], part[:, nb % 2, 1, :], ALU.add))
                own.settle(dve)
                dve.tensor_tensor(mergedT[:, nb, :], part[:, nb % 2, 0, :], part[:, nb % 2, 2, :], ALU.add)\
                   .then_inc(merged, 1)
            for n in range(4):
                dve.wait_ge(k.unit_done, U["out"] + n + 1)
                xs = k.x[:, :, n * S:(n + 1) * S]
                own.up(dve.tensor_tensor(xs, xs, halves(ps[4 + n][:, :]), ALU.add))


def route(k):
    ps, U = k.ps, FIRST
    k.G = carve(k, 0, KEYS, S)
    lay = Layout(k, 0)
    qT = lay.take(2 * PEER_H, S)
    keys = lay.take(2 * PEER_H, KEYS)
    sc = lay.take(2, TT, 2, KEYS)
    best = lay.take(TT, 2 * PEER_H, TOPK)
    index = lay.take(TT, 2 * PEER_H, TOPK).bitcast(U32)
    index_f = lay.take(TT, 2 * PEER_H, TOPK)
    cand = lay.take(2, TT, TOPK * TOPK)
    top = lay.take(TT, PEER_H, TOPK)
    where = lay.take(TT, PEER_H * TOPK).bitcast(U32)
    half = [lay.take(TT, PEER_H * TOPK).bitcast(U32) for _ in range(2)]
    half_f = [lay.take(TT, PEER_H * TOPK) for _ in range(2)]
    equal = lay.take(PEER_H * TOPK, TOPK)
    chosen = lay.take(3, TT, PEER_H * TOPK)
    shifted, total, inverse = lay.take(TT, PEER_H, TOPK), lay.take(TT, PEER_H), lay.take(TT, PEER_H)
    k.slotsT = carve(k, KEYS * S, 3, S)
    names = ("keys_here", "q_out", "score_mm", "score_out", "head_done", "shift_ready", "exp_ready",
             "chosen_ready", "chosen_turned")
    (keys_here, q_out, score_mm, score_out, head_done, shift_ready, exp_ready, chosen_ready,
     chosen_turned) = (ctx_sem(k, n) for n in names)
    own = Count(ctx_sem(k, "route_dve"))

    with k.nc.Block() as block:
        @block.sync
        def _(sp):
            sp.dma_start(keys, k.args["sub_keys"].rearrange("p (n k) -> p n k", k=KEYS)).then_inc(keys_here, 16)
            stream(k, sp, k.stream_to)

        @block.tensor
        def _(pe):
            def score(h):
                pe.wait_ge(q_out, h + 1)
                if h == 0:
                    pe.wait_ge(keys_here, 16)
                if h >= 2:
                    pe.wait_ge(score_out, h - 1)
                for tt in range(TT):
                    for p in range(2):
                        o = (2 * tt + p) * KEYS
                        last = pe.matmul(ps[2 + h % 2][:, o:o + KEYS], qT[:, 2 * h + p, tt * P:(tt + 1) * P],
                                         keys[:, 2 * h + p, :], start=True, stop=True)
                last.then_inc(score_mm, 1)

            for h in range(PEER_H):
                if h >= 2:
                    pe.wait_ge(q_out, h - 1)
                unit_T(k, pe, U["peer_q"] + h, k.hT, ps[h % 2])
                if h >= 1:
                    score(h - 1)
            score(PEER_H - 1)
            pe.wait_ge(chosen_ready, 1)
            for n in range(3):
                for tt in range(TT):
                    o = (n % 2) * S + tt * P
                    last = pe.transpose(ps[4 + n // 2][:, o:o + P], chosen[:, n, tt, :], k.ident)
            last.then_inc(chosen_turned, 1)

        @block.scalar
        def _(act):
            for h in range(PEER_H + 1):
                if h < PEER_H:
                    act.wait_ge(k.unit_done, U["peer_q"] + h + 1)
                    act.activation(qT[:, 2 * h:2 * h + 2, :], halves(ps[h % 2][:, :]), ACT.Copy).then_inc(q_out, 1)
                if h >= 1:
                    act.wait_ge(score_mm, h)
                    if h >= 3:
                        act.wait_ge(head_done, h - 2)
                    act.activation(sc[:, (h - 1) % 2].rearrange("p t q k -> p (t q k)"), ps[2 + (h - 1) % 2][:, :],
                                   ACT.Copy).then_inc(score_out, 1)
            act.wait_ge(shift_ready, 1)
            act.activation(shifted, shifted, ACT.Exp).then_inc(exp_ready, 1)
            act.wait_ge(chosen_turned, 1)
            act.activation(k.slotsT[:, 0:2, :], halves(ps[4][:, :]), ACT.Copy)
            act.activation(k.slotsT[:, 2, :], ps[5][:, 0:S], ACT.Copy)

        @block.vector
        def _(dve):
            def top16(rows):
                for half_n in range(2):
                    at = slice(8 * half_n, 8 * half_n + 8)
                    for v, b, _ in rows:
                        own.up(dve.max(b[:, at], v))
                    own.settle(dve)
                    for v, b, i in rows:
                        own.up(dve.max_index(i[:, at], b[:, at], v))
                    own.settle(dve)
                    if half_n == 0:
                        for v, b, _ in rows:
                            own.up(dve.match_replace(v, b[:, at], v, -3e38))
                        own.settle(dve)

            for h in range(PEER_H):
                dve.wait_ge(score_out, h + 1)
                top16([(sc[:, h % 2, tt, p, :], best[:, tt, 2 * h + p, :], index[:, tt, 2 * h + p, :])
                       for tt in range(TT) for p in range(2)])
                for tt in range(TT):
                    a = best[:, tt, 2 * h, :].rearrange("p (a b) -> p a b", b=1).to_broadcast([P, TOPK, TOPK])
                    b = over(best[:, tt, 2 * h + 1, :], TOPK)
                    own.up(dve.tensor_tensor(cand[:, h % 2, tt, :].rearrange("p (a b) -> p a b", a=TOPK), a, b,
                                             ALU.add))
                own.settle(dve)
                top16([(cand[:, h % 2, tt, :], top[:, tt, h, :], where[:, tt, h * TOPK:(h + 1) * TOPK])
                       for tt in range(TT)])
                dve.tensor_scalar(half[1][:, :, h * TOPK:(h + 1) * TOPK], where[:, :, h * TOPK:(h + 1) * TOPK],
                                  TOPK - 1, None, ALU.bitwise_and).then_inc(head_done, 1)
            first = top[:, :, :, 0:1].to_broadcast([P, TT, PEER_H, TOPK])
            dve.tensor_tensor(shifted, top, first, ALU.subtract).then_inc(shift_ready, 1)
            own.up(dve.tensor_scalar(half[0], where, 4, None, ALU.logical_shift_right))
            own.up(dve.tensor_copy(index_f, index))
            own.settle(dve)
            dve.wait_ge(head_done, PEER_H)
            for n in range(2):
                own.up(dve.tensor_copy(half_f[n], half[n]))
            own.settle(dve)
            parts = index_f.rearrange("p t (h q) a -> p t h q a", q=2)
            for n in range(2):
                for tt in range(TT):
                    pos = half_f[n][:, tt, :].rearrange("p (j a) -> p j a", a=1).to_broadcast([P, PEER_H * TOPK, TOPK])
                    own.up(dve.tensor_tensor(equal, pos, over(k.iota[:, 0:TOPK], PEER_H * TOPK), ALU.is_equal))
                    own.settle(dve)
                    e = equal.rearrange("p (h j) a -> p h j a", h=PEER_H)
                    ind = parts[:, tt, :, n, :].rearrange("p h (j a) -> p h j a", j=1)\
                        .to_broadcast([P, PEER_H, TOPK, TOPK])
                    own.up(dve.tensor_tensor(e, e, ind, ALU.mult))
                    own.settle(dve)
                    own.up(dve.tensor_reduce(chosen[:, n, tt, :], equal, AX.X, ALU.add))
                    own.settle(dve)
            dve.wait_ge(exp_ready, 1)
            own.up(dve.tensor_reduce(total, shifted, AX.X, ALU.add))
            own.settle(dve)
            own.up(dve.reciprocal(inverse, total))
            own.settle(dve)
            inv = inverse.rearrange("p t (h j) -> p t h j", j=1).to_broadcast([P, TT, PEER_H, TOPK])
            gates = chosen[:, 2].rearrange("p t (h j) -> p t h j", h=PEER_H)
            dve.tensor_tensor(gates, shifted, inv, ALU.mult).then_inc(chosen_ready, 1)


def spread(k):
    GROUP_T, GROUPS, BUFS = 4, 4, 2
    TURNS = S // (GROUP_T * GROUPS)
    hot = carve(k, KEYS * S + 3 * S, BUFS, 2, GROUP_T, KEYS)
    hot_ready, spread_mm, spread_out = (ctx_sem(k, n) for n in ("hot_ready", "spread_mm", "spread_out"))
    ps = k.ps

    def turns(eng, body):
        body(0, True)
        with eng.Fori(1, TURNS) as i:
            body(i, False)

    with k.nc.Block() as block:
        @block.sync
        def _(sp):
            sp.dma_start(k.x_away, k.x.rearrange("p t d -> p (t d)")).then_inc(k.x_saved, 16)
            stream(k, sp, k.stream_to)
            sp.wait_ge(k.x_saved, 16)

        @block.vector
        def _(dve):
            def body(i, first):
                for g in range(GROUPS):
                    if not (first and g < BUFS):
                        dve.wait_ge(spread_mm, i * GROUPS + (g - BUFS + 1))
                    for n in range(GROUP_T):
                        t = i * (GROUP_T * GROUPS) + (g * GROUP_T + n)
                        i1, i2, gate = (k.slotsT[:, c, bass.ds(t, 1)] for c in range(3))
                        dve.tensor_scalar(hot[:, g % BUFS, 0, n, :], k.iota, i1, gate, ALU.is_equal, ALU.mult)
                        last = dve.tensor_scalar(hot[:, g % BUFS, 1, n, :], k.iota, i2, None, ALU.is_equal)
                    last.then_inc(hot_ready, 1)
            turns(dve, body)
            h = k.hT.rearrange("p c s -> p (c s)")
            dve.wait_ge(k.rounded_out, 1)
            dve.tensor_tensor(k.hT_lo.rearrange("p c s -> p (c s)"), h, plain(k.hT_hi.rearrange("p c s -> p (c s)")),
                              ALU.subtract)

        @block.tensor
        def _(pe):
            def body(i, first):
                for g in range(GROUPS):
                    pe.wait_ge(hot_ready, i * GROUPS + (g + 1))
                    if not first:
                        pe.wait_ge(spread_out, i * GROUPS + (g - GROUPS + 1))
                    for n in range(GROUP_T):
                        last = pe.matmul(ps[g][:, n * KEYS:(n + 1) * KEYS], hot[:, g % BUFS, 0, n, :],
                                         hot[:, g % BUFS, 1, n, :], start=True, stop=True)
                    last.then_inc(spread_mm, 1)
            turns(pe, body)

        @block.scalar
        def _(act):
            act.activation(k.hT_hi.rearrange("p c s -> p (c s)"), k.hT.rearrange("p c s -> p (c s)"),
                           ACT.Copy).then_inc(k.rounded_out, 1)

            def body(i, first):
                for g in range(GROUPS):
                    act.wait_ge(spread_mm, i * GROUPS + (g + 1))
                    t = i * (GROUP_T * GROUPS) + g * GROUP_T
                    act.activation(k.G[:, :, bass.ds(t, GROUP_T)],
                                   ps[g][:, :].rearrange("p (t n) -> p n t", t=GROUP_T), ACT.Copy)\
                       .then_inc(spread_out, 1)
            turns(act, body)


PAIRS = 64


def experts(k):
    ps = k.ps
    F = FIRST["peer"]
    room = k.x.rearrange("p t d -> p (t d)")
    gelu, weighted_lo, weighted_hi = (ap.rearrange("p (j b s) -> p j b s", j=2, b=2)
                                      for ap in (room[:, 0:4 * S], k.x_r[:, 0:4 * S], k.x_r[:, 4 * S:8 * S]))
    x_back = carve(k, 0, TT, D)
    gelu_out, weighted_whole, weighted_round, weighted_ready = (
        ctx_sem(k, n) for n in ("gelu_out", "weighted_whole", "weighted_round", "weighted_ready"))
    own = Count(ctx_sem(k, "experts_dve"))

    def u_unit(j):
        return F + (2 * j - 1 if j else 0)

    def v_unit(j):
        return F + min(2 * j + 2, 127)

    def steps(eng, body):
        body(0, 0)
        with eng.Fori(0, (PAIRS - 2) // 2) as i:
            for n in (1, 2):
                body(n, i)
        body(PAIRS - 1, 0)

    with k.nc.Block() as block:
        @block.sync
        def _(sp):
            stream(k, sp, k.stream_to)
            sp.wait_ge(weighted_whole, 4)
            sp.wait_ge(k.x_saved, 16)
            sp.dma_start(x_back.rearrange("p t d -> p (t d)"), k.x_away).then_inc(k.x_here, 16)

        @block.tensor
        def _(pe):
            def up(j0, i):
                unit_T_split(k, pe, u_unit(j0), lambda c: k.hT_hi[:, c, :],
                             lambda c: k.hT_lo[:, c, :], ps[j0 % 2], turn=i * 4)

            def down(j0, i):
                v = v_unit(j0)
                pe.wait_ge(weighted_ready, i * 2 + (j0 + 1))
                w_hi, w_lo = (w.rearrange("p (b d) -> p b d", b=2)
                              for w in (k.w_hi[:, v % 2, :], k.ring_lo[:, v % RING, :]))
                g_hi, g_lo = weighted_hi[:, j0 % 2], weighted_lo[:, j0 % 2]
                for n, (g, w) in enumerate(((g_hi, w_hi), (g_lo, w_hi), (g_hi, w_lo))):
                    split_ready(k, pe, v, n, turn=i * 4)
                    for b in range(2):
                        for tt in range(TT):
                            for dh in range(2):
                                last = pe.matmul(ps[4 + 2 * tt + dh][:, :], g[:, b, tt * P:(tt + 1) * P],
                                                 w[:, b, dh * 512:(dh + 1) * 512],
                                                 start=(j0 == 0 and n == 0 and b == 0),
                                                 stop=(j0 == PAIRS - 1 and n == 2 and b == 1))
                last.then_inc(k.unit_done, 1)

            def body(j0, i):
                if j0 == PAIRS - 1:
                    return down(j0, i)
                if j0 >= 1:
                    pe.wait_ge(gelu_out, i * 2 + j0)
                up(j0 + 1, i)
                down(j0, i)

            up(0, 0)
            steps(pe, body)

        @block.scalar
        def _(act):
            def body(j0, i):
                act.wait_ge(k.unit_done, i * 4 + (u_unit(j0) + 1))
                if j0 >= 2:
                    act.wait_ge(weighted_ready, i * 2 + (j0 - 1))
                act.activation(flat(gelu[:, j0 % 2]), ps[j0 % 2][:, :], ACT.Gelu_apprx_tanh).then_inc(gelu_out, 1)
                if 0 < j0 < PAIRS - 1:
                    split_hi(k, act, u_unit(j0 + 1), turn=i * 4, ring_turn=i)
                act.wait_ge(weighted_whole, i * 2 + (j0 + 1))
                act.activation(flat(weighted_hi[:, j0 % 2]), flat(gelu[:, j0 % 2]), ACT.Copy)\
                   .then_inc(weighted_round, 1)
                split_hi(k, act, v_unit(j0), turn=i * 4, ring_turn=i)

            split_hi(k, act, F)
            split_hi(k, act, F + 1)
            steps(act, body)

        @block.vector
        def _(dve):
            def body(j0, i):
                dve.wait_ge(gelu_out, i * 2 + (j0 + 1))
                g = gelu[:, j0 % 2]
                dve.tensor_tensor(g, g, k.G[:, bass.ds(i * 4 + 2 * j0, 2), :], ALU.mult).then_inc(weighted_whole, 1)
                if 0 < j0 < PAIRS - 1:
                    split_lo(k, dve, u_unit(j0 + 1), turn=i * 4)
                dve.wait_ge(weighted_round, i * 2 + (j0 + 1))
                dve.tensor_tensor(weighted_lo[:, j0 % 2], g, plain(weighted_hi[:, j0 % 2]), ALU.subtract).then_inc(weighted_ready, 1)
                split_lo(k, dve, v_unit(j0), turn=i * 4)

            split_lo(k, dve, F)
            split_lo(k, dve, F + 1)
            steps(dve, body)
            dve.wait_ge(k.unit_done, F + 128)
            dve.wait_ge(k.x_here, 16)
            for tt in range(TT):
                for dh in range(2):
                    at = slice(dh * 512, (dh + 1) * 512)
                    own.up(dve.tensor_tensor(k.x[:, tt, at], x_back[:, tt, at], ps[4 + 2 * tt + dh][:, :], ALU.add))


def gdn_layout(k):
    g = k.gdn = Kernel()
    lay = Layout(k, 0)
    H = GDN_H
    g.qkvT = lay.take(3 * H, S)
    g.zT = lay.take(H, S)
    g.A = lay.take(H, 4, P)
    g.intraT = lay.take(H, 4, P)
    g.bv = lay.take(H, 4, P)
    g.kdec = lay.take(H, 2, P)
    g.qdec = lay.take(H, 2, P)
    g.Y = lay.take(H, 4, P)
    g.X = lay.take(H, 4, P)
    g.levels = lay.take(7, 4, P)
    small = [lay.take(4, H) for _ in range(7)]
    g.g, g.beta, g.G, g.negG, g.eG, g.kd, g.nbe = small
    g.qT, g.kT, g.vT = (g.qkvT[:, n * H:(n + 1) * H, :] for n in range(3))
    g.at_A, g.at_Y, g.at_X, g.at_levels = 8 * 4 * S, 24 * 4 * S, 28 * 4 * S, 32 * 4 * S


def gdn_project(k):
    g, ps, U, H = k.gdn, k.ps, FIRST, GDN_H
    PAD = GDN_CONV // 2
    lay = Layout(k, g.at_A)
    padded = lay.take(2, 2, S + 2 * PAD)
    square = lay.take(2, 2, S)
    inv = lay.take(2 * H, S)
    ab_w = lay.take(KC, 32)
    x_a, m_soft = lay.take(TT * 16), lay.take(TT * 16)
    soft = [lay.take(TT * 16) for _ in range(5)]
    th, rate = lay.take(TT, 16), lay.take(16)
    names = ("ab_here", "ab_mm", "gdn_raw", "conv_ready", "silu_done", "square_ready", "norm_mm",
             "norm_read", "inv_ready", "inv_root", "dt_abs", "dt_exp", "ab_act")
    (ab_here, ab_mm, gdn_raw, conv_ready, silu_done, square_ready, norm_mm, norm_read, inv_ready,
     inv_root, dt_abs, dt_exp, ab_act) = (ctx_sem(k, n) for n in names)
    own = Count(ctx_sem(k, "gdn_project_dve"))
    ab_ps = ps[6]
    a_of = ab_ps[:, 0:64].rearrange("p (t n) -> p t n", t=TT)[:, :, 0:16]
    b_of = ab_ps[:, 0:64].rearrange("p (t n) -> p t n", t=TT)[:, :, 16:32]

    pads_ready = ctx_sem(k, "pads_ready")

    def silu(act, n):
        act.wait_ge(conv_ready, n + 1)
        pair = flat(g.qkvT[:, 2 * n:2 * n + 2, :])
        act.activation(pair, pair, ACT.Silu).then_inc(silu_done, 1)

    def read_norm(dve, n):
        dve.wait_ge(norm_mm, n + 1)
        dve.tensor_scalar(flat(inv[:, 2 * n:2 * n + 2, :]), ps[2 + n % 2][:, :], EPS, None, ALU.add)\
           .then_inc(norm_read, 1)

    def th_view(ap):
        return ap.rearrange("p (t d h) -> p t d h", t=TT, d=2)

    def by_system(ap):
        return ap.rearrange("p (d t) h -> p t d h", d=2)

    with k.nc.Block() as block:
        @block.sync
        def _(sp):
            sp.dma_start(ab_w, k.args["ab"].rearrange("p (c n) -> p c n", c=KC)).then_inc(ab_here, 16)
            sp.dma_start(g.levels, k.consts_dram[:, CON["levels"]:CON["levels"] + 28 * P]
                         .rearrange("p (l s n) -> p l s n", l=7, s=4)).then_inc(k.levels_here, 16)
            stream(k, sp, k.stream_to)

        @block.tensor
        def _(pe):
            pe.wait_ge(ab_here, 16)
            for tt in range(TT):
                for c in range(KC):
                    last = pe.matmul(ab_ps[:, tt * 32:(tt + 1) * 32], k.hT[:, c, tt * P:(tt + 1) * P], ab_w[:, c, :],
                                     start=(c == 0), stop=(c == KC - 1))
            last.then_inc(ab_mm, 1)
            for n in range(16):
                if n >= 2:
                    pe.wait_ge(gdn_raw, n - 1)
                unit_T(k, pe, U["gdn_qkv"] + n, k.hT, ps[n % 2])
                if 2 <= n < 10:
                    pe.wait_ge(square_ready, n - 1)
                    if n >= 4:
                        pe.wait_ge(norm_read, n - 3)
                    pe.matmul(ps[2 + n % 2][:, :], k.ones, flat(square[:, n % 2]), start=True, stop=True)\
                      .then_inc(norm_mm, 1)

        @block.scalar
        def _(act):
            act.wait_ge(ab_mm, 1)
            act.activation(th, b_of, ACT.Tanh, scale=0.5).then_inc(ab_act, 1)
            act.activation(rate, k.rows[:, ROWS["a_log"]:ROWS["a_log"] + 16], ACT.Exp).then_inc(ab_act, 1)
            act.wait_ge(dt_abs, 1)
            act.activation(soft[1], soft[0], ACT.Exp, scale=-1.0).then_inc(dt_exp, 1)
            for n in range(16):
                act.wait_ge(k.unit_done, U["gdn_qkv"] + n + 1)
                if n < 12:
                    if n >= 2:
                        act.wait_ge(conv_ready, n - 1)
                    else:
                        act.wait_ge(pads_ready, 1)
                    act.activation(padded[:, n % 2, :, PAD:PAD + S], halves(ps[n % 2][:, :]), ACT.Copy)\
                       .then_inc(gdn_raw, 1)
                    if n >= 1:
                        silu(act, n - 1)
                    if n == 11:
                        silu(act, 11)
                else:
                    act.activation(g.zT[:, 2 * (n - 12):2 * (n - 11), :], halves(ps[n % 2][:, :]), ACT.Silu)\
                       .then_inc(gdn_raw, 1)
            act.wait_ge(inv_ready, 1)
            act.activation(flat(inv), flat(inv), ACT.Sqrt).then_inc(inv_root, 1)

        @block.vector
        def _(dve):
            own.up(dve.memset(padded[:, :, :, 0:PAD], 0.0))
            own.settle(dve)
            dve.memset(padded[:, :, :, PAD + S:PAD + S + PAD], 0.0).then_inc(pads_ready, 1)
            dve.wait_ge(ab_act, 1)
            own.up(dve.tensor_tensor(x_a.rearrange("p (t n) -> p t n", t=TT), a_of,
                                     over(k.rows[:, ROWS["dt_bias"]:ROWS["dt_bias"] + 16], TT), ALU.add))
            own.settle(dve)
            softplus(dve, own, x_a, m_soft, soft, dt_abs, dt_exp)
            dve.wait_ge(ab_act, 2)
            own.up(dve.scalar_tensor_tensor(out=soft[0].rearrange("p (t n) -> p t n", t=TT),
                                            in0=m_soft.rearrange("p (t n) -> p t n", t=TT), scalar=-1.0,
                                            in1=over(rate, TT), op0=ALU.mult, op1=ALU.mult))
            own.settle(dve)
            own.up(dve.tensor_copy(by_system(g.g), th_view(soft[0])))
            own.up(dve.tensor_scalar(by_system(g.beta), th_view(th.rearrange("p t n -> p (t n)")), 0.5, 0.5,
                                     ALU.mult, ALU.add))
            w = col(k, "gdn_conv", GDN_CONV * 24)
            for n in range(12):
                dve.wait_ge(gdn_raw, n + 1)
                for j in range(GDN_CONV):
                    for b in range(2):
                        tap = w[:, 24 * j + 2 * n + b:24 * j + 2 * n + b + 1]
                        src, dst = padded[:, n % 2, b, j:j + S], g.qkvT[:, 2 * n + b, :]
                        if j == 0:
                            last = dve.tensor_scalar(dst, src, tap, None, ALU.mult)
                        else:
                            last = dve.scalar_tensor_tensor(out=dst, in0=src, scalar=tap, in1=dst,
                                                            op0=ALU.mult, op1=ALU.add)
                        if (j, b) != (GDN_CONV - 1, 1):
                            own.up(last)
                    if j < GDN_CONV - 1:
                        own.settle(dve)
                last.then_inc(conv_ready, 1)
                if 2 <= n < 10:
                    read_norm(dve, n - 2)
                if 1 <= n < 9:
                    dve.wait_ge(silu_done, n)
                    pair = flat(g.qkvT[:, 2 * n - 2:2 * n, :])
                    dve.tensor_tensor(flat(square[:, (n - 1) % 2]), pair, pair, ALU.mult).then_inc(square_ready, 1)
            own.settle(dve)
            dve.wait_ge(norm_read, 8)
            dve.reciprocal(flat(inv), flat(inv)).then_inc(inv_ready, 1)
            dve.wait_ge(silu_done, 8)
            dve.wait_ge(inv_root, 1)
            own.up(dve.scalar_tensor_tensor(out=flat(g.qT), in0=flat(g.qT), scalar=SCALE, in1=flat(inv[:, 0:H]),
                                            op0=ALU.mult, op1=ALU.mult))
            own.up(dve.tensor_tensor(flat(g.kT), flat(g.kT), flat(inv[:, H:2 * H]), ALU.mult))


def gdn_build(k):
    g, ps, H = k.gdn, k.ps, GDN_H
    lay = Layout(k, g.at_Y)
    gm, dA, dI = lay.take(2, 4, P), lay.take(2, 4, P), lay.take(2, 4, P)
    row_e = lay.take(2, 2, P)
    lay = Layout(k, g.at_X)
    cum, far_a, far_i = lay.take(2, P), lay.take(4, P), lay.take(4, P)
    lay = Layout(k, g.at_X + 2048)
    total = lay.take(4, H)
    names = ("masks_here", "sums_mm", "sums_ready", "sums_exp", "gm_ready", "build_mm", "decays_ready",
             "head_built", "natural_out", "scales_ready")
    (masks_here, sums_mm, sums_ready, sums_exp, gm_ready, build_mm, decays_ready, head_built,
     natural_out, scales_ready) = (ctx_sem(k, n) for n in names)
    own = Count(ctx_sem(k, "gdn_build_dve"))
    KQ, RA, RI, RU, NAT = ps[0], ps[1], ps[2], ps[3], [ps[4], ps[5]]

    with k.nc.Block() as block:
        @block.sync
        def _(sp):
            sp.dma_start(cum, k.consts_dram[:, CON["cum"]:CON["cum"] + 2 * P].rearrange("p (d n) -> p d n", d=2))\
              .then_inc(masks_here, 16)
            sp.dma_start(far_a, k.consts_dram[:, CON["far_a"]:CON["far_a"] + 4 * P]
                         .rearrange("p (s n) -> p s n", s=4)).then_inc(masks_here, 16)
            sp.dma_start(far_i, k.consts_dram[:, CON["far_i"]:CON["far_i"] + 4 * P]
                         .rearrange("p (s n) -> p s n", s=4)).then_inc(masks_here, 16)
            stream(k, sp, k.stream_to)

        @block.tensor
        def _(pe):
            pe.wait_ge(masks_here, 48)
            for d in range(2):
                pe.matmul(ps[6][:, d * 16:(d + 1) * 16], cum[:, d, :], g.g[:, 2 * d:2 * d + 2, :]
                          .rearrange("p s h -> p (s h)"), start=True, stop=True)
            pe.matmul(ps[6][:, 32:64], k.ones, g.g.rearrange("p s h -> p (s h)"), start=True, stop=True)\
              .then_inc(sums_mm, 1)
            for h in range(H):
                if h >= 1:
                    pe.wait_ge(head_built, h)
                    pe.wait_ge(decays_ready, 9 * h)
                for tt in range(TT):
                    c = slice(tt * P, (tt + 1) * P)
                    pe.matmul(KQ[:, tt * P:(tt + 1) * P], g.kT[:, h, c], g.kT[:, h, c], start=True, stop=True)
                    pe.matmul(KQ[:, (2 + tt) * P:(3 + tt) * P], g.kT[:, h, c], g.qT[:, h, c], start=True, stop=True)
                pe.wait_ge(gm_ready, h + 1)
                rows = gm[:, h % 2].rearrange("p s n -> p (s n)")
                pe.matmul(RA[:, :], k.ones, rows, start=True, stop=False)
                pe.matmul(RA[:, :], k.ident, far_a.rearrange("p s n -> p (s n)"), start=False, stop=True)
                pe.matmul(RI[:, :], k.ones, rows, start=True, stop=False)
                pe.matmul(RI[:, :], k.ident, far_i.rearrange("p s n -> p (s n)"), start=False, stop=True)
                pe.matmul(RU[:, 0:2 * P], k.ones, gm[:, h % 2, 1:3, :].rearrange("p s n -> p (s n)"),
                          start=True, stop=True)
                if h >= 2:
                    pe.wait_ge(natural_out, 6 * (h - 1))
                for n, src in enumerate((g.kT, g.vT)):
                    for tt in range(TT):
                        last = pe.transpose(NAT[h % 2][:, (2 * n + tt) * P:(2 * n + tt + 1) * P],
                                            src[:, h, tt * P:(tt + 1) * P], k.ident)
                last.then_inc(build_mm, 1)

        @block.scalar
        def _(act):
            act.wait_ge(sums_ready, 2)
            act.activation(g.eG, g.G, ACT.Exp).then_inc(sums_exp, 1)
            act.activation(g.kd, g.kd, ACT.Exp).then_inc(sums_exp, 1)
            act.wait_ge(sums_exp, 2)
            for h in range(H):
                act.wait_ge(build_mm, h + 1)
                if h >= 2:
                    act.wait_ge(head_built, h - 1)
                for s in range(4):
                    c = slice(s * P, (s + 1) * P)
                    act.activation(dA[:, h % 2, s, :], RA[:, c], ACT.Exp, scale=-1.0, bias=g.G[:, s, h:h + 1])\
                       .then_inc(decays_ready, 1)
                    act.activation(dI[:, h % 2, s, :], RI[:, c], ACT.Exp, bias=g.negG[:, s, h:h + 1])\
                       .then_inc(decays_ready, 1)
                act.activation(row_e[:, h % 2], RU[:, 0:2 * P].rearrange("p (d n) -> p d n", d=2), ACT.Exp)\
                   .then_inc(decays_ready, 1)
                nat = NAT[h % 2]
                for tt in range(TT):
                    act.activation(g.kdec[:, h, tt, :], nat[:, tt * P:(tt + 1) * P], ACT.Copy,
                                   scale=g.kd[:, 3 * tt, h:h + 1]).then_inc(natural_out, 1)
                for s in range(4):
                    act.activation(g.bv[:, h, s, :], nat[:, (2 + s % 2) * P:(3 + s % 2) * P], ACT.Copy,
                                   scale=g.beta[:, s, h:h + 1]).then_inc(natural_out, 1)

        @block.vector
        def _(dve):
            dve.wait_ge(masks_here, 48)

            def running(h):
                if h >= 2:
                    dve.wait_ge(build_mm, h - 1)
                for s in range(4):
                    last = dve.tensor_scalar(gm[:, h % 2, s, :], cum[:, s // 2, :], g.g[:, s, h:h + 1], None, ALU.mult)
                    if s < 3:
                        own.up(last)
                last.then_inc(gm_ready, 1)

            running(0)
            dve.wait_ge(sums_mm, 1)
            sums = ps[6][:, 0:32].rearrange("p (s h) -> p s h", s=4)
            own.up(dve.tensor_copy(g.G, sums))
            own.up(dve.tensor_copy(total, ps[6][:, 32:64].rearrange("p (s h) -> p s h", s=4)))
            own.settle(dve)
            dve.tensor_scalar(g.negG, g.G, -1.0, None, ALU.mult).then_inc(sums_ready, 1)
            dve.tensor_tensor(g.kd, total, g.G, ALU.subtract).then_inc(sums_ready, 1)
            dve.wait_ge(sums_exp, 1)
            own.up(dve.scalar_tensor_tensor(out=g.nbe, in0=g.eG, scalar=-1.0, in1=g.beta, op0=ALU.mult,
                                            op1=ALU.mult))
            for h in range(H):
                if h + 1 < H:
                    running(h + 1)
                dve.wait_ge(decays_ready, 9 * (h + 1))
                both = lambda n: KQ[:, 2 * n * P:2 * (n + 1) * P].rearrange("p (d s) -> p d s", d=1)\
                    .to_broadcast([P, 2, 2 * P])
                pair = lambda ap: ap.rearrange("p (d t) n -> p d (t n)", d=2)
                own.up(dve.tensor_tensor(pair(dA[:, h % 2]), pair(dA[:, h % 2]), both(0), ALU.mult))
                own.up(dve.tensor_tensor(pair(g.intraT[:, h]), pair(dI[:, h % 2]), both(1), ALU.mult))
                own.up(dve.tensor_tensor(g.qdec[:, h, 0, :], g.qT[:, h, P:2 * P], row_e[:, h % 2, 0, :], ALU.mult))
                own.up(dve.tensor_tensor(g.qdec[:, h, 1, :], g.qT[:, h, 0:P], row_e[:, h % 2, 1, :], ALU.mult))
                own.settle(dve)
                beta = g.beta[:, :, h:h + 1].to_broadcast([P, 4, P])
                dve.tensor_tensor(g.A[:, h], dA[:, h % 2], beta, ALU.mult).then_inc(head_built, 1)


def gdn_invert(k):
    g, ps, H = k.gdn, k.ps, GDN_H
    lay = Layout(k, 0)
    am, zs = lay.take(2, 4, P), lay.take(2, 4, P)
    names = ("level_ready", "z_mm", "z_out", "delta_mm", "y_ready", "x_ready")
    level_ready, z_mm, z_out, delta_mm, y_ready, x_ready = (ctx_sem(k, n) for n in names)
    LEVELS = 7

    def order():
        n = 0
        for h2 in range(0, H, 2):
            for level in range(LEVELS):
                for h in (h2, h2 + 1):
                    yield n, h, level
                    n += 1

    def all4(ap):
        return ap.rearrange("p s n -> p (s n)")

    with k.nc.Block() as block:
        @block.sync
        def _(sp):
            stream(k, sp, k.stream_to)

        @block.gpsimd
        def _(pool):
            pool.wait_ge(k.levels_here, 16)
            for n, h, level in order():
                if n >= 2:
                    pool.wait_ge(z_mm, n - 1)
                if level == 1:
                    pool.wait_ge(x_ready, n - 1)
                pool.tensor_tensor(all4(am[:, h % 2]), all4(g.A[:, h]), all4(g.levels[:, level]), ALU.mult)\
                    .then_inc(level_ready, 1)

        @block.tensor
        def _(pe):
            def delta(n, h, level):
                pe.wait_ge(z_out, n + 1 - (n // (2 * LEVELS) * 2 + min(2, n % (2 * LEVELS))))
                for s in range(4):
                    pe.matmul(ps[2 + h % 2][:, s * P:(s + 1) * P], g.X[:, h, s, :], zs[:, h % 2, s, :],
                              start=True, stop=True)
                for s in range(4):
                    last = pe.matmul(ps[4 + h % 2][:, s * P:(s + 1) * P], zs[:, h % 2, s, :], g.X[:, h, s, :],
                                     start=True, stop=True)
                last.then_inc(delta_mm, 1)

            before = None
            for n, h, level in order():
                pe.wait_ge(level_ready, n + 1)
                if level == 0:
                    if n >= 2:
                        pe.wait_ge(y_ready, n - 1)
                    for s in range(4):
                        last = pe.matmul(ps[h % 2][:, s * P:(s + 1) * P], am[:, h % 2, s, :], k.ident,
                                         start=True, stop=True)
                else:
                    pe.wait_ge(y_ready, n - 1)
                    pe.wait_ge(x_ready, n - 1)
                    for s in range(4):
                        last = pe.matmul(ps[h % 2][:, s * P:(s + 1) * P], am[:, h % 2, s, :], g.Y[:, h, s, :],
                                         start=True, stop=True)
                last.then_inc(z_mm, 1)
                if before is not None:
                    delta(*before)
                before = (n, h, level) if level > 0 else None
            delta(*before)

        @block.scalar
        def _(act):
            for n, h, level in order():
                if level == 0:
                    continue
                act.wait_ge(z_mm, n + 1)
                act.activation(all4(zs[:, h % 2]), ps[h % 2][:, :], ACT.Copy).then_inc(z_out, 1)

        @block.vector
        def _(dve):
            def apply(n, h, level):
                if level == 0:
                    dve.wait_ge(z_mm, n + 1)
                    eye = k.ident.rearrange("p (s n) -> p s n", s=1).to_broadcast([P, 4, P])
                    dve.tensor_tensor(g.Y[:, h], eye, ps[h % 2][:, :].rearrange("p (s n) -> p s n", s=4),
                                      ALU.subtract).then_inc(y_ready, 1)
                    dve.tensor_tensor(g.X[:, h], eye, am[:, h % 2], ALU.subtract).then_inc(x_ready, 1)
                    return
                done = n + 1 - (n // (2 * LEVELS) * 2 + min(2, n % (2 * LEVELS)))
                dve.wait_ge(delta_mm, done)
                dve.tensor_tensor(all4(g.Y[:, h]), all4(g.Y[:, h]), ps[2 + h % 2][:, :], ALU.subtract)\
                   .then_inc(y_ready, 1)
                dve.tensor_tensor(all4(g.X[:, h]), all4(g.X[:, h]), ps[4 + h % 2][:, :], ALU.subtract)\
                   .then_inc(x_ready, 1)

            for n, h, level in order():
                apply(n, h, level)


def gdn_recur(k):
    g, ps, U, H = k.gdn, k.ps, FIRST, GDN_H
    lay = Layout(k, g.at_A)
    v1, state = lay.take(2 * H, P), lay.take(2 * H, P)
    lay = Layout(k, g.at_X)
    rhs, v2 = lay.take(2 * H, P), lay.take(2 * H, P)
    oT = carve(k, 0, H, S)
    square = carve(k, 2 * H * S, H, S)
    inv = carve(k, g.at_levels, H, S)
    names = ("v1_mm", "v1_out", "state_mm", "state_out", "ks_mm", "rhs_ready", "v2_mm", "v2_out", "o_mm",
             "o_out", "o_square", "o_norm_mm", "o_mean", "o_root", "o_gated")
    (v1_mm, v1_out, state_mm, state_out, ks_mm, rhs_ready, v2_mm, v2_out, o_mm, o_out, o_square,
     o_norm_mm, o_mean, o_root, o_gated) = (ctx_sem(k, n) for n in names)
    own = Count(ctx_sem(k, "gdn_recur_dve"))
    GROUPS = H // 2
    first_s, second_s = (0, 3), (1, 2)
    members = [[(2 * q + hh, d) for hh in range(2) for d in range(2)] for q in range(GROUPS)]

    def group(ap, q):
        return ap[:, 4 * q:4 * q + 4, :].rearrange("p c n -> p (c n)")

    with k.nc.Block() as block:
        @block.sync
        def _(sp):
            stream(k, sp, k.stream_to)

        @block.tensor
        def _(pe):
            def products(q, bank, lhs, rhs_of, done):
                for c, (h, d) in enumerate(members[q]):
                    last = pe.matmul(bank[:, c * P:(c + 1) * P], lhs(h, d), rhs_of(h, d), start=True, stop=True)
                last.then_inc(done, 1)

            for q in range(GROUPS):
                products(q, ps[q], lambda h, d: g.Y[:, h, first_s[d], :], lambda h, d: g.bv[:, h, first_s[d], :], v1_mm)
            for q in range(GROUPS):
                pe.wait_ge(v1_out, q + 1)
                products(q, ps[4 + q], lambda h, d: g.kdec[:, h, d, :], lambda h, d: v1[:, 2 * h + d, :], state_mm)
            for q in range(GROUPS):
                pe.wait_ge(state_out, q + 1)
                products(q, ps[q], lambda h, d: g.kT[:, h, (1 - d) * P:(2 - d) * P],
                         lambda h, d: state[:, 2 * h + d, :], ks_mm)
            for q in range(GROUPS):
                pe.wait_ge(rhs_ready, q + 1)
                products(q, ps[4 + q], lambda h, d: g.Y[:, h, second_s[d], :], lambda h, d: rhs[:, 2 * h + d, :], v2_mm)
            for q in range(GROUPS):
                pe.wait_ge(v2_out, q + 1)
                for hh in range(2):
                    h = 2 * q + hh
                    for tt in range(TT):
                        f, s = tt, 1 - tt
                        out = ps[q][:, hh * S + tt * P:hh * S + (tt + 1) * P]
                        pe.matmul(out, v1[:, 2 * h + f, :], g.intraT[:, h, first_s[f], :], start=True, stop=False)
                        pe.matmul(out, v2[:, 2 * h + s, :], g.intraT[:, h, second_s[s], :], start=False, stop=False)
                        last = pe.matmul(out, state[:, 2 * h + s, :], g.qdec[:, h, s, :], start=False, stop=True)
                last.then_inc(o_mm, 1)
            for q in range(GROUPS):
                pe.wait_ge(o_square, q + 1)
                pe.matmul(ps[4 + q][:, :], k.ones, flat(square[:, 2 * q:2 * q + 2, :]), start=True, stop=True)\
                  .then_inc(o_norm_mm, 1)
            pe.wait_ge(o_gated, 1)
            for n in range(4):
                unit_N(k, pe, U["gdn_out"] + n, oT, [ps[n][:, 0:S], ps[n][:, S:2 * S]])

        @block.scalar
        def _(act):
            for mm, out, dst, bank in ((v1_mm, v1_out, v1, 0), (state_mm, state_out, state, 4),
                                       (v2_mm, v2_out, v2, 4)):
                for q in range(GROUPS):
                    act.wait_ge(mm, q + 1)
                    act.activation(group(dst, q), ps[bank + q][:, :], ACT.Copy).then_inc(out, 1)
            for q in range(GROUPS):
                act.wait_ge(o_mm, q + 1)
                act.activation(oT[:, 2 * q:2 * q + 2, :], halves(ps[q][:, :]), ACT.Copy).then_inc(o_out, 1)
            act.wait_ge(o_mean, 1)
            act.activation(flat(inv), flat(inv), ACT.Sqrt).then_inc(o_root, 1)

        @block.vector
        def _(dve):
            for q in range(GROUPS):
                dve.wait_ge(ks_mm, q + 1)
                for c, (h, d) in enumerate(members[q]):
                    s = second_s[d]
                    last = dve.scalar_tensor_tensor(out=rhs[:, 2 * h + d, :], in0=ps[q][:, c * P:(c + 1) * P],
                                                    scalar=g.nbe[:, s, h:h + 1], in1=g.bv[:, h, s, :],
                                                    op0=ALU.mult, op1=ALU.add)
                    if c < 3:
                        own.up(last)
                last.then_inc(rhs_ready, 1)
            for q in range(GROUPS):
                dve.wait_ge(o_out, q + 1)
                o = flat(oT[:, 2 * q:2 * q + 2, :])
                dve.tensor_tensor(flat(square[:, 2 * q:2 * q + 2, :]), o, o, ALU.mult).then_inc(o_square, 1)
            for q in range(GROUPS):
                dve.wait_ge(o_norm_mm, q + 1)
                own.up(dve.tensor_scalar(flat(inv[:, 2 * q:2 * q + 2, :]), ps[4 + q][:, :], 1.0 / P, EPS,
                                         ALU.mult, ALU.add))
            own.settle(dve)
            dve.reciprocal(flat(inv), flat(inv)).then_inc(o_mean, 1)
            own.up(dve.scalar_tensor_tensor(out=flat(oT), in0=flat(oT), scalar=col(k, "gdn_norm"), in1=flat(g.zT),
                                            op0=ALU.mult, op1=ALU.mult))
            own.settle(dve)
            dve.wait_ge(o_root, 1)
            dve.tensor_tensor(flat(oT), flat(oT), flat(inv), ALU.mult).then_inc(o_gated, 1)
            for n in range(4):
                dve.wait_ge(k.unit_done, U["gdn_out"] + n + 1)
                xs = k.x[:, :, n * S:(n + 1) * S]
                own.up(dve.tensor_tensor(xs, xs, halves(ps[n][:, :]), ALU.add))


def mlp(k, layer):
    ps, F1, F2 = k.ps, FIRST[f"mlp1_{layer}"], FIRST[f"mlp2_{layer}"]
    mid_hi, mid_lo = k.mid_r[:, 0], k.mid_r[:, 1]
    mid = carve(k, 2 * FF // P * S, 2, 2, S)
    relu_out, square_ready, mid_round, mid_ready, sum_out = (
        ctx_sem(k, f"{n}_{layer}") for n in ("relu_out", "mid_square", "mid_round", "mid_ready", "sum_out"))
    own = Count(ctx_sem(k, f"mlp_dve_{layer}"))
    N1 = FF // 256

    def add(dve, j):
        dve.wait_ge(k.unit_done, F2 + 4 * j + 4)
        for tt in range(TT):
            xs = k.x[:, tt, j * S:(j + 1) * S]
            last = dve.tensor_tensor(xs, xs, ps[4 + 2 * (j % 2) + tt][:, 0:S], ALU.add)
            if tt == 0:
                own.up(last)
        last.then_inc(sum_out, 1)

    with k.nc.Block() as block:
        @block.sync
        def _(sp):
            stream(k, sp, k.stream_to)

        @block.tensor
        def _(pe):
            def up(i, first):
                for n in range(RING):
                    if not first:
                        pe.wait_ge(relu_out, i * RING + (n - RING + 1))
                    unit_T_split(k, pe, F1 + n, lambda c: k.hT_hi[:, c, :],
                                 lambda c: k.hT_lo[:, c, :], ps[n], turn=i * RING)

            up(0, True)
            with pe.Fori(1, N1 // RING) as i:
                up(i, False)
            for j in range(4):
                if j >= 2:
                    pe.wait_ge(sum_out, j - 1)
                for q in range(4):
                    u = F2 + 4 * j + q
                    hi, lo = unit_parts(k, u)
                    for n, (m, w) in enumerate(((mid_hi, hi), (mid_lo, hi), (mid_hi, lo))):
                        split_ready(k, pe, u, n)
                        if j == 0 and n == 0:
                            pe.wait_ge(mid_ready, 4 * (q + 1))
                        for tt in range(TT):
                            for c in range(8):
                                last = pe.matmul(ps[4 + 2 * (j % 2) + tt][:, 0:S],
                                                 m[:, 8 * q + c, tt * P:(tt + 1) * P], w[:, c, :],
                                                 start=(q == 0 and n == 0 and c == 0),
                                                 stop=(q == 3 and n == 2 and c == 7))
                    last.then_inc(k.unit_done, 1)

        @block.scalar
        def _(act):
            def turn(i, first):
                for n in range(RING):
                    act.wait_ge(k.unit_done, i * RING + (F1 + n + 1))
                    if not (first and n < 2):
                        act.wait_ge(mid_ready, i * RING + (n - 1))
                    act.activation(flat(mid[:, n % 2]), ps[n][:, :], ACT.Relu).then_inc(relu_out, 1)
                    split_hi(k, act, F1 + n + 2, turn=i * RING, ring_turn=i)
                    act.wait_ge(square_ready, i * RING + (n + 1))
                    act.activation(mid_hi[:, bass.ds(i * (2 * RING) + 2 * n, 2), :], mid[:, n % 2], ACT.Copy)\
                       .then_inc(mid_round, 1)

            split_hi(k, act, F1)
            split_hi(k, act, F1 + 1)
            turn(0, True)
            with act.Fori(1, N1 // RING) as i:
                turn(i, False)
            for u in range(F2 + 2, F2 + RING):
                split_hi(k, act, u)
            with act.Fori(0, 3) as i:
                for n in range(RING):
                    split_hi(k, act, F2 + RING + n, turn=i * RING, ring_turn=i)

        @block.vector
        def _(dve):
            split_lo(k, dve, F1)
            split_lo(k, dve, F1 + 1)
            with dve.Fori(0, N1 // RING) as i:
                for n in range(RING):
                    dve.wait_ge(relu_out, i * RING + (n + 1))
                    m = mid[:, n % 2]
                    dve.tensor_tensor(m, m, m, ALU.mult).then_inc(square_ready, 1)
                    split_lo(k, dve, F1 + n + 2, turn=i * RING)
                    dve.wait_ge(mid_round, i * RING + (n + 1))
                    at = bass.ds(i * (2 * RING) + 2 * n, 2)
                    dve.tensor_tensor(mid_lo[:, at, :], m, plain(mid_hi[:, at, :]), ALU.subtract).then_inc(mid_ready, 1)
            for j in range(4):
                for q in range(4):
                    if 4 * j + q >= 2:
                        split_lo(k, dve, F2 + 4 * j + q)
                    if j >= 1 and q == 1:
                        add(dve, j - 1)
            add(dve, 3)


def ds_project(k):
    ps, F = k.ps, FIRST["ds_in"]
    d = k.ds = Kernel()
    lay = Layout(k, 0)
    d.qkT = lay.take(18, S)
    d.v = lay.take(TT, 5 * S)
    d.oT = lay.take(9, S)
    d.at = lay.at
    rel, hot, seen, table = (lay.take(n) for n in (DS_HEADS, DELTAS, DELTAS, DELTAS))
    names = ("ds_out_of", "bias_here", "bias_mm", "bias_ready")
    ds_out, bias_here, bias_mm, bias_ready = (ctx_sem(k, n) for n in names)
    with k.nc.Block() as block:
        @block.sync
        def _(sp):
            sp.dma_start(rel[0:BUCKETS, :], k.args["rel_bias"]).then_inc(bias_here, 16)
            sp.dma_start(hot[0:BUCKETS, :], k.args["hot"]).then_inc(bias_here, 16)
            sp.dma_start(seen[0:DS_HEADS, :], k.args["seen"]).then_inc(bias_here, 16)
            sp.wait_ge(bias_ready, 1)
            rows = table[0:DS_HEADS, :].rearrange("h (c n) -> h c n", c=1).to_broadcast([DS_HEADS, P, DELTAS])
            sp.dma_start(k.bias_dram, rows).then_inc(k.bias_stored, 16)
            stream(k, sp, k.stream_to)

        @block.tensor
        def _(pe):
            pe.wait_ge(bias_here, 48)
            pe.matmul(ps[2][0:DS_HEADS, :], rel[0:BUCKETS, :], hot[0:BUCKETS, :], start=True, stop=True)\
              .then_inc(bias_mm, 1)
            for n in range(14):
                bank = ps[n % 2]
                if n >= 2:
                    pe.wait_ge(ds_out, n - 1)
                if n < 9:
                    unit_T(k, pe, F + n, k.hT, bank)
                else:
                    unit_N(k, pe, F + n, k.hT, [bank[:, 0:S], bank[:, S:2 * S]])

        @block.scalar
        def _(act):
            for n in range(14):
                act.wait_ge(k.unit_done, F + n + 1)
                dst = d.qkT[:, 2 * n:2 * n + 2, :] if n < 9 else d.v[:, :, (n - 9) * S:(n - 8) * S]
                act.activation(dst, halves(ps[n % 2][:, :]), ACT.Copy).then_inc(ds_out, 1)

        @block.vector
        def _(dve):
            dve.wait_ge(bias_mm, 1)
            dve.tensor_tensor(table[0:DS_HEADS, :], ps[2][0:DS_HEADS, :], seen[0:DS_HEADS, :], ALU.add)\
               .then_inc(bias_ready, 1)


def ds_attend(k):
    ps, F, d = k.ps, FIRST["ds_out"], k.ds
    G = len(DS_DIL)
    E = DS_E
    lay = Layout(k, d.at)
    bias = lay.take(2, G, TT * S)
    sc = lay.take(2, G, TT, S)
    ptS = lay.take(2, G, 2, S)
    stat = k.small[:, 16:48]
    names = ("ds_bias_here0", "ds_bias_here1", "ds_scores", "ds_scaled", "ds_maxed", "ds_exped", "ds_probs",
             "ds_turned", "ds_pt_out", "ds_pv", "ds_pv_out")
    (here0, here1, scores, scaled, maxed, exped, probs, turned, pt_out, pv, pv_out) = (ctx_sem(k, n) for n in names)
    here = [here0, here1]
    own = Count(ctx_sem(k, "ds_dve"))
    J = DS_PER

    with k.nc.Block() as block:
        @block.sync
        def _(sp):
            sp.wait_ge(k.bias_stored, 16)
            for j in range(J):
                if j >= 2:
                    sp.wait_ge(scaled, G * (j - 1))
                for tt in range(TT):
                    src = bass.AP(k.bias_dram.tensor, j * P * DELTAS + S - 1 - tt * P,
                                  [[DELTAS - 1, P], [DS_PER * P * DELTAS, G], [1, S]])
                    sp.dma_start(bias[:, j % 2, :, tt * S:(tt + 1) * S], src).then_inc(here[j % 2], 16)
            stream(k, sp, k.stream_to)

        @block.tensor
        def _(pe):
            def score(j):
                rows = slice(E * (j % 2), E * (j % 2) + E)
                if j >= 1:
                    pe.wait_ge(scaled, G * j)
                for g in range(G):
                    c = (DS_PER * g + j) // 2
                    for tt in range(TT):
                        last = pe.matmul(ps[g][:, tt * S:(tt + 1) * S], d.qkT[rows, c, tt * P:(tt + 1) * P],
                                         d.qkT[rows, 9 + c, :], start=True, stop=True)
                    last.then_inc(scores, 1)

            def turn(j):
                pe.wait_ge(probs, j + 1)
                if j >= 1:
                    pe.wait_ge(pt_out, G * j)
                for g in range(G):
                    for kt in range(TT):
                        for tt in range(TT):
                            last = pe.transpose(ps[3 + g][:, kt * S + tt * P:kt * S + (tt + 1) * P],
                                                sc[:, j % 2, g, tt, kt * P:(kt + 1) * P], k.ident)
                    last.then_inc(turned, 1)

            def weigh(j):
                rows = slice(E * (j % 2), E * (j % 2) + E)
                if j >= 1:
                    pe.wait_ge(pv_out, 2 * j)
                for g in range(G):
                    pe.wait_ge(pt_out, G * j + g + 1)
                    h = DS_PER * g + j
                    out = ps[6 + g // 2][rows, (g % 2) * S:(g % 2 + 1) * S]
                    for kt in range(TT):
                        last = pe.matmul(out, d.v[:, kt, E * h:E * h + E], ptS[:, j % 2, g, kt, :],
                                         start=(kt == 0), stop=(kt == TT - 1))
                last.then_inc(pv, 1)

            for j in range(J + 1):
                if j < J:
                    score(j)
                if j >= 1:
                    turn(j - 1)
                    weigh(j - 1)
            pe.wait_ge(pv_out, 2 * J)
            for n in range(4):
                for u in (F + 9 * n // 8, F + (9 * n + 8) // 8):
                    loaded(k, pe, u)
                for tt in range(TT):
                    for c in range(9):
                        i = 9 * n + c
                        w = slot(k, F + i // 8)[:, i % 8, :]
                        last = pe.matmul(ps[n][:, tt * S:(tt + 1) * S], d.oT[:, c, tt * P:(tt + 1) * P], w,
                                         start=(c == 0), stop=(c == 8))
                last.then_inc(k.unit_done, 1)
            done_mark(k, pe, k.unit_done)

        @block.scalar
        def _(act):
            for j in range(J + 1):
                if j < J:
                    o = 16 * (j % 2)
                    act.wait_ge(maxed, j + 1)
                    for tt in range(TT):
                        act.activation(sc[:, j % 2, :, tt, :], sc[:, j % 2, :, tt, :], ACT.Exp,
                                       bias=stat[:, o + 2 + tt:o + 3 + tt],
                                       accum_out=stat[:, o + 4 + tt:o + 5 + tt]).then_inc(exped, 1)
                if j >= 1:
                    rows = slice(E * ((j - 1) % 2), E * ((j - 1) % 2) + E)
                    if j >= 3:
                        act.wait_ge(pv, j - 2)
                    for g in range(G):
                        act.wait_ge(turned, G * (j - 1) + g + 1)
                        act.activation(ptS[:, (j - 1) % 2, g], halves(ps[3 + g][:, :]), ACT.Copy).then_inc(pt_out, 1)
                    act.wait_ge(pv, j)
                    c = (j - 1) // 2
                    act.activation(d.oT[rows, c:c + 4:3, :], halves(ps[6][rows, :]), ACT.Copy).then_inc(pv_out, 1)
                    act.activation(d.oT[rows, c + 6, :], ps[7][rows, 0:S], ACT.Copy).then_inc(pv_out, 1)

        @block.vector
        def _(dve):
            for j in range(J):
                o = 16 * (j % 2)
                dve.wait_ge(here[j % 2], 16 * TT * (j // 2 + 1))
                if j >= 2:
                    dve.wait_ge(turned, G * (j - 1))
                for g in range(G):
                    dve.wait_ge(scores, G * j + g + 1)
                    dve.scalar_tensor_tensor(out=sc[:, j % 2, g].rearrange("p t s -> p (t s)"), in0=ps[g][:, :],
                                             scalar=E ** -0.5, in1=bias[:, j % 2, g, :], op0=ALU.mult,
                                             op1=ALU.add).then_inc(scaled, 1)
                dve.wait_ge(scaled, G * (j + 1))
                own.up(dve.tensor_reduce(stat[:, o:o + 2], sc[:, j % 2].rearrange("p g t s -> p t g s"), AX.XY,
                                         ALU.max))
                own.settle(dve)
                dve.tensor_scalar(stat[:, o + 2:o + 4], stat[:, o:o + 2], -1.0, None, ALU.mult).then_inc(maxed, 1)
                dve.wait_ge(exped, 2 * (j + 1))
                own.up(dve.reciprocal(stat[:, o + 6:o + 8], stat[:, o + 4:o + 6]))
                own.settle(dve)
                for tt in range(TT):
                    last = dve.tensor_scalar(sc[:, j % 2, :, tt, :], sc[:, j % 2, :, tt, :],
                                             stat[:, o + 6 + tt:o + 7 + tt], None, ALU.mult)
                    if tt == 0:
                        own.up(last)
                last.then_inc(probs, 1)
                own.settle(dve)
            for n in range(4):
                dve.wait_ge(k.unit_done, F + n + 1)
                xs = k.x[:, :, n * S:(n + 1) * S]
                own.up(dve.tensor_tensor(xs, xs, halves(ps[n][:, :]), ALU.add))


def build(nc, args, out):
    k = Kernel()
    k.nc, k.mix = nc, Kernel()
    k.ARENA = 36864
    k.weights, k.consts_dram, k.cols_dram = args["weights"], args["consts"], args["cols"]
    k.x_dram, k.mem_dram, k.pos_dram, k.rows_dram = args["x"], args["mem"], args["pos"], args["rows"]
    k.args, k.out = args, out
    with ExitStack() as stack:
        k.stack = stack

        def sb(name, shape, dt=F32):
            return stack.enter_context(nc.sbuf_tensor("s_" + name, shape, dt))

        with ExitStack() as first:
            def low(name, *dims):
                return first.enter_context(nc.sbuf_tensor("s_" + name, [P, *dims], F32R))

            k.ring_lo = low("ring_lo", RING, UNIT)
            k.x_r = low("x_r", TT * D)
            k.hT_lo = low("hT_lo", KC, S)
            k.mid_r = low("mid_r", 2, FF // P, S)
            low("between", k.ARENA - 2 * FF // P * S - 2 * UNIT)
            k.w_hi = low("w_hi", 2, UNIT)
        k.ring = sb("ring", [P, RING, UNIT])
        k.x = sb("x", [P, TT, D])
        k.hT = sb("hT", [P, KC, S])
        k.arena = sb("arena", [P, k.ARENA])
        k.hT_hi = sb("hT_hi", [P, KC, S], F32R)
        k.consts = sb("consts", [P, CON["window"]])
        k.cols = sb("cols", [P, NCOLS])
        k.rows = sb("rows", [P, NROWS])
        k.small = sb("small", [P, 64])
        k.half_b = sb("half_b", [P, 48])
        k.rate = sb("rate", [P, 2 * LRU_B])
        k.ps = [stack.enter_context(nc.psum_tensor(f"bank{n}", [P, 512], F32)) for n in range(8)]
        k.ident = k.consts[:, CON["ident"]:CON["ident"] + P]
        k.ones = k.consts[:, CON["ones"]:CON["ones"] + P]
        k.iota = k.consts[:, CON["iota"]:CON["iota"] + P]
        k.rot = k.consts[:, CON["rot"]:CON["rot"] + P]
        k.w_loaded = [ctx_sem(k, f"weights_loaded{s}") for s in range(RING)]
        k.unit_done = ctx_sem(k, "unit_done")
        k.squares, k.mean_ready, k.root_ready = (ctx_sem(k, n) for n in ("squares", "mean_ready", "root_ready"))
        k.scaled, k.turned, k.norm_steps = ctx_sem(k, "scaled"), ctx_sem(k, "turned"), Count(ctx_sem(k, "norm_steps"))
        k.g_here, k.levels_here, k.bias_stored = (ctx_sem(k, n) for n in ("g_rows_here", "levels_here", "bias_stored"))
        k.hi_ready, k.lo_ready, k.rounded_out = (ctx_sem(k, n) for n in ("hi_ready", "lo_ready", "rounded_out"))
        k.x_saved, k.x_here = ctx_sem(k, "x_saved"), ctx_sem(k, "x_here")
        k.x_away = nc.dram_tensor("x_away", (P, TT * D), F32, kind="Internal").ap()
        k.norms = k.norms_T = k.rows_normed = k.splits = 0
        k.bias_dram = nc.dram_tensor("bias_by_distance", (DS_HEADS, P, DELTAS), F32, kind="Internal").ap()
        program(k)


def program(k):
    mixer_layout(k)
    high = Layout(k, k.ARENA - TT * D - 2 * S)
    k.mem_rows = high.take(TT, D)
    k.sin, k.cos = high.take(S), high.take(S)
    load_and_tables(k)
    k.stream_to = RING
    memT = carve(k, k.mix.free, KC, S)
    normalise(k, k.mem_rows, col(k, "g_mem", KC), memT, k.mix.free + KC * S)
    normalise(k, k.x, col(k, "g_mix", KC), k.hT, k.mix.free + KC * S)
    projections(k)
    attention(k)
    k.stream_to = FIRST["peer_q"] + RING
    merge(k)
    normalise(k, k.x, col(k, "g_ffn", KC), k.hT, 0)
    k.stream_to = FIRST["peer"] + RING
    route(k)
    spread(k)
    k.stream_to = FIRST["gdn_qkv"] + RING
    k.whole_units = FIRST["peer"]
    experts(k)
    normalise_rows(k, k.x, k.args["g_final"], k.x)
    normalise(k, k.x, col(k, "g_a", KC), k.hT, 0)
    k.stream_to = FIRST["gdn_out"] + RING
    gdn_layout(k)
    gdn_project(k)
    gdn_build(k)
    gdn_invert(k)
    k.stream_to = FIRST["mlp1_0"] + RING
    gdn_recur(k)
    normalise(k, k.x, col(k, "g_mlp0", KC), k.hT, 0, split=True)
    k.whole_units += FIRST["mlp1_0"] - FIRST["gdn_qkv"]
    k.stream_to = FIRST["ds_in"] + RING
    mlp(k, 0)
    normalise(k, k.x, col(k, "g_b", KC), k.hT, 0)
    k.stream_to = FIRST["ds_out"] + RING
    ds_project(k)
    k.stream_to = FIRST["mlp1_1"] + RING
    ds_attend(k)
    normalise(k, k.x, col(k, "g_mlp1", KC), k.hT, 0, split=True)
    k.whole_units += FIRST["mlp1_1"] - FIRST["ds_in"]
    k.stream_to = UNITS
    mlp(k, 1)
    normalise_rows(k, k.x, k.args["norm_final"], k.x)
    store(k, k.x)


def store(k, src):
    done = ctx_sem(k, "stored")
    with k.nc.Block() as block:
        @block.sync
        def _(sp):
            sp.dma_start(k.out.rearrange("(t p) d -> p t d", p=P), src[:, :, :]).then_inc(done, 16)
            sp.wait_ge(done, 16)


def columns(w):
    n = w.shape[1] // 256
    return w.reshape(8, P, n, 256).transpose(2, 1, 0, 3).reshape(n, P, UNIT)


def lay_out(i):
    w_in = i["w_in"][0]
    at = np.cumsum([0, HEADS * P, KV_HEADS * P, KV_HEADS * P, 768, 768, MEM_HEADS * P, 3 * D])
    q, kk, v, lx, lg, mq, gates = (w_in[:, a:b] for a, b in zip(at[:-1], at[1:]))
    mem = i["w_mem_kv"][0]
    branches = np.concatenate([i["p_attn"][0], i["p_lru"][0], i["p_mem"][0]], 0)
    lru = np.stack([i["lru_wr"][0], i["lru_wi"][0]])
    lru = lru.transpose(0, 2, 1, 3, 4).reshape(24, P, P).transpose(1, 0, 2).reshape(P, 24 * P)
    lru = np.concatenate([lru, np.zeros((P, 8 * P), np.float32)], 1).reshape(P, 2, UNIT).transpose(1, 0, 2)
    units = {
        "mem_k": columns(mem[:, :512]), "mem_v": columns(mem[:, 512:]), "q": columns(q), "k": columns(kk),
        "v": columns(v), "mem_q": columns(mq), "lru_x": columns(lx), "lru_gate": columns(lg), "lru_w": lru,
        "gates": columns(gates),
        "merge": branches.reshape(16, P, 8, P).transpose(2, 1, 0, 3).reshape(8, P, UNIT),
        "out": columns(i["w_out"][0]), "peer_q": columns(i["w_peer_q"][0]),
    }
    u = i["peer_u"][0].reshape(KEYS, 64, 2, 8, P).transpose(1, 4, 3, 2, 0).reshape(64, P, UNIT)
    v = i["peer_v"][0].reshape(KEYS, 64, 2, D).transpose(1, 0, 2, 3).reshape(64, P, UNIT)
    units["peer"] = np.concatenate([u[:1], np.stack([u[1:], v[:-1]], 1).reshape(126, P, UNIT), v[-1:]], 0)
    g = i["gdn_w_in_2"][0]
    units["gdn_qkv"], units["gdn_z"] = columns(g[:, :3 * D]), columns(g[:, 3 * D:4 * D])
    units["gdn_out"] = columns(i["gdn_w_out_2"][0])
    for n in range(2):
        units[f"mlp1_{n}"] = columns(i["mlp_w1_2"][n])
        w2 = i["mlp_w2_2"][n]
        units[f"mlp2_{n}"] = w2.reshape(4, 8, P, 4, 256).transpose(3, 0, 2, 1, 4).reshape(16, P, UNIT)
    ds = np.concatenate([i["dswa_w_in_2"][0], np.zeros((D, P), np.float32)], 1)
    units["ds_in"] = columns(ds)
    out = i["dswa_w_out_2"][0].reshape(9, P, 4, 256).transpose(2, 0, 1, 3).reshape(36, P, 256)
    out = np.concatenate([out, np.zeros((4, P, 256), np.float32)], 0)
    units["ds_out"] = out.reshape(5, 8, P, 256).transpose(0, 2, 1, 3).reshape(5, P, UNIT)
    for name, n in STREAM:
        assert units[name].shape == (n, P, UNIT), (name, units[name].shape)
    weights = np.concatenate([units[name] for name, _ in STREAM], 0)

    def cols(a):
        return np.asarray(a, np.float32).reshape(-1, P).T

    parts = {
        "g_mix": i["g_mix"][0], "g_mem": i["g_mem"][0], "g_ffn": i["g_ffn"][0], "g_a": i["norm_mix_2"][0],
        "g_mlp0": i["norm_mlp_2"][0], "g_b": i["norm_mix_2"][1], "g_mlp1": i["norm_mlp_2"][1],
        "gate_b": i["gate_b"][0], "conv_w": i["conv_w"][0], "conv_b": i["conv_b"][0],
        "lru_b": np.stack([i["lru_br"][0], i["lru_bi"][0]]), "lam": i["lru_lambda"][0],
        "gdn_conv": i["gdn_conv_w_2"][0], "gdn_norm": i["gdn_norm_w_2"][0],
    }
    packed = np.concatenate([cols(parts[name]) for name, _ in COLS], 1)
    assert packed.shape == (P, NCOLS)
    rows = np.concatenate([i["attn_sink"][0], i["gdn_a_log_2"][0].ravel(), i["gdn_dt_bias_2"][0].ravel()])
    ab = i["gdn_w_in_2"][0][:, 4 * D:].reshape(8, P, 32).transpose(1, 0, 2).reshape(P, 256)
    hot, seen = distance_constants()
    sub_keys = i["peer_sub_keys"][0].reshape(16, KEYS, P).transpose(2, 0, 1).reshape(P, UNIT)
    arrays = {
        "sub_keys": sub_keys,
        "weights": weights, "cols": packed, "rows": rows, "consts": shape_constants(), "x": i["x"][0],
        "mem": i["mem"][0], "pos": i["positions"][0], "ab": ab, "rel_bias": i["rel_bias_2"],
        "g_final": i["g_final"], "norm_final": i["norm_final_2"], "hot": hot, "seen": seen,
    }
    return {n: np.ascontiguousarray(a) for n, a in arrays.items()}


def kernel(**inputs):
    from concourse import bacc
    from concourse.bass_utils import run_bass_kernel_spmd

    arrays = lay_out({n: np.asarray(a) for n, a in inputs.items()})
    nc = bacc.Bacc("TRN2", target_bir_lowering=False, num_devices=1)
    args = {n: nc.dram_tensor(n, a.shape, mybir.dt.from_np(a.dtype), kind="ExternalInput").ap()
            for n, a in arrays.items()}
    out = nc.dram_tensor("out", (S, D), F32, kind="ExternalOutput").ap()
    build(nc, args, out)
    r = run_bass_kernel_spmd(nc, [arrays], core_ids=[0])
    return r.results[0]["out"].reshape(1, S, D)
```

```python
from contextlib import ExitStack

import numpy as np

import concourse.bass as bass
from concourse import mybir

F32 = mybir.dt.float32
I32 = mybir.dt.int32
U32 = mybir.dt.uint32
F32R = mybir.dt.float32r
ALU = mybir.AluOpType
ACT = mybir.ActivationFunctionType
AX = mybir.AxisListType

P = 128
S = 256
TT = S // P
D = 1024
KC = D // P
RING = 4
UNIT = 2048
EPS = 1e-6
NEG = -1e30
BIG = 1e30

HEADS, KV_HEADS, MEM_HEADS = 6, 2, 4
GROUP = HEADS // KV_HEADS
SCALE = float(P) ** -0.5
LRU_B = 6
CONV = 4
FF = 4096
PEER_H, TOPK, KEYS = 8, 16, 128
GDN_H = 8
GDN_CONV = 5
DS_HEADS, DS_E, DS_PER = 18, 64, 6
DS_DIL = (1, 4, 16)
DS_HALF = 64
BUCKETS = 32
TWO_PI = 2.0 * np.pi

STREAM = [
    ("mem_k", 2), ("mem_v", 2), ("q", 3), ("k", 1), ("v", 1), ("mem_q", 2),
    ("lru_x", 3), ("lru_gate", 3), ("lru_w", 2), ("gates", 12),
    ("merge", 8), ("out", 4), ("peer_q", 8), ("peer", 128),
    ("gdn_qkv", 12), ("gdn_z", 4), ("gdn_out", 4), ("mlp1_0", 16), ("mlp2_0", 16),
    ("ds_in", 14), ("ds_out", 5), ("mlp1_1", 16), ("mlp2_1", 16),
]
FIRST = {}
_n = 0
for _name, _units in STREAM:
    FIRST[_name] = _n
    _n += _units
UNITS = _n

COLS = [
    ("g_mix", KC), ("g_mem", KC), ("g_ffn", KC), ("g_a", KC), ("g_mlp0", KC), ("g_b", KC),
    ("g_mlp1", KC), ("gate_b", 24), ("conv_w", CONV * LRU_B), ("conv_b", LRU_B),
    ("lru_b", 4 * LRU_B), ("lam", 2 * LRU_B), ("gdn_conv", GDN_CONV * 24), ("gdn_norm", 1),
]
COL = {}
_n = 0
for _name, _units in COLS:
    COL[_name] = _n
    _n += _units
NCOLS = _n
ROWS = {"sink": 0, "a_log": HEADS, "dt_bias": HEADS + 16}
NROWS = HEADS + 32

CONSTS = [
    ("ident", P), ("ones", P), ("iota", P), ("rot", P), ("inv_freq", 1), ("window", TT * S),
    ("cum", 2 * P), ("far_a", 4 * P), ("far_i", 4 * P), ("levels", 7 * 4 * P),
]
CON = {}
_n = 0
for _name, _units in CONSTS:
    CON[_name] = _n
    _n += _units
NCON = _n
DELTAS = 2 * S


def shape_constants():
    c = np.zeros((P, NCON), np.float32)

    def put(name, value):
        value = np.asarray(value, np.float32)
        c[:, CON[name]:CON[name] + value.shape[1]] = value

    i = np.arange(P)
    put("ident", np.eye(P))
    put("ones", np.ones((P, P)))
    put("iota", np.tile(i, (P, 1)))
    rot = np.zeros((P, P))
    for n in range(16):
        rot[n + 16, n] = -1.0
        rot[n, n + 16] = 1.0
    put("rot", rot)
    freq = np.zeros((P, 1), np.float32)
    inv = np.float32(500000.0) ** (-np.arange(0, 32, 2, dtype=np.float32) / np.float32(32))
    freq[0:16, 0] = inv
    freq[16:32, 0] = inv
    put("inv_freq", freq)
    q = np.arange(TT)[None, :, None] * P + i[:, None, None]
    k = np.arange(S)[None, None, :]
    put("window", np.where(np.abs(k - q) <= 128, 0.0, NEG).reshape(P, -1))
    before = (i[:, None] <= i[None, :]).astype(np.float32)
    put("cum", np.concatenate([before, before.T], 1))
    row, col = i[:, None], i[None, :]
    lower = row > col
    strict = [lower, lower, lower.T, lower.T]
    put("far_a", np.concatenate([np.where(m, 0.0, BIG) for m in strict], 1))
    incl = [row <= col, row <= col, row >= col, row >= col]
    put("far_i", np.concatenate([np.where(m, 0.0, -BIG) for m in incl], 1))
    levels = []
    for n in range(7):
        same = (row >> (n + 1)) == (col >> (n + 1))
        other = (row >> n) != (col >> n)
        low = same & other & lower
        levels.append(np.concatenate([low, low, low.T, low.T], 1))
    put("levels", np.concatenate(levels, 1))
    return c


def distance_constants():
    rel = np.arange(DELTAS) - (S - 1)
    n = np.abs(rel)
    half, exact = BUCKETS // 2, BUCKETS // 4
    nf = np.maximum(n, 1).astype(np.float32)
    large = exact + (np.log(nf / np.float32(exact)) / np.float32(np.log(1024 / exact))
                     * np.float32(half - exact)).astype(np.int32)
    bucket = np.where(rel > 0, half, 0) + np.where(n < exact, n, np.minimum(large, half - 1))
    hot = (np.arange(BUCKETS)[:, None] == bucket[None, :]).astype(np.float32)
    seen = np.zeros((DS_HEADS, DELTAS), np.float32)
    for h in range(DS_HEADS):
        d = DS_DIL[h // DS_PER]
        seen[h] = np.where((rel % d == 0) & (n <= DS_HALF * d), 0.0, NEG)
    return hot, seen


class Count:

    def __init__(self, sem):
        self.sem, self.n, self.turn = sem, 0, 0

    def up(self, instruction):
        instruction.then_inc(self.sem, 1)
        self.n += 1

    def settle(self, eng):
        eng.wait_ge(self.sem, self.turn + self.n)

    def enter(self, i, each):
        self.start, self.each, self.turn = self.n, each, i * each

    def leave(self, turns):
        assert self.n - self.start == self.each, (self.n - self.start, self.each)
        self.n, self.turn = self.start + turns * self.each, 0


class Kernel:
    pass


def carve(k, at, *dims):
    n = int(np.prod(dims))
    assert at + n <= k.ARENA, (at, n)
    v = k.arena[:, at:at + n]
    if len(dims) == 1:
        return v
    names = "abcd"[:len(dims)]
    return v.rearrange(f"p ({' '.join(names)}) -> p {' '.join(names)}",
                       **{x: d for x, d in zip(names[1:], dims[1:])})


class Layout:

    def __init__(self, k, at=0):
        self.k, self.at = k, at

    def take(self, *dims):
        v = carve(self.k, self.at, *dims)
        self.at += int(np.prod(dims))
        return v


def halves(ap):
    return ap.rearrange("p (a b) -> p a b", a=2)


def stream(k, sp, until):
    until = min(until, UNITS)
    u = k.issued

    def load(slot, unit):
        sp.dma_start(k.ring[:, slot, :], k.weights[bass.ds(unit, 1), :, :].rearrange("a p n -> p (a n)"))\
          .then_inc(k.w_loaded[slot], 16)

    while u < until:
        turns = (until - u) // RING
        if u % RING == 0 and u >= RING and turns >= 3:
            with sp.Fori(0, turns) as i:
                for s in range(RING):
                    sp.wait_ge(k.unit_done, i * RING + (u + s - RING + 1))
                    load(s, i * RING + (u + s))
            u += turns * RING
            continue
        if u >= RING:
            sp.wait_ge(k.unit_done, u - RING + 1)
        load(u % RING, u)
        u += 1
    k.issued = until


def loaded(k, pe, u, turn=0):
    pe.wait_ge(k.w_loaded[u % RING], 16 * (u // RING + 1) + turn * 16)


def slot(k, u):
    return k.ring[:, u % RING, :].rearrange("p (c n) -> p c n", c=8)


def unit_T(k, pe, u, srcT, out, turn=0):
    loaded(k, pe, u, turn)
    w = slot(k, u)
    for nb in range(2):
        for c in range(8):
            last = pe.matmul(out[:, nb * S:(nb + 1) * S], w[:, c, nb * P:(nb + 1) * P], srcT[:, c, :],
                             start=(c == 0), stop=(c == 7))
    last.then_inc(k.unit_done, 1)


def unit_N(k, pe, u, srcT, out, turn=0, first=True, final=True):
    loaded(k, pe, u, turn)
    w = slot(k, u)
    for tt in range(TT):
        for c in range(8):
            last = pe.matmul(out[tt], srcT[:, c, tt * P:(tt + 1) * P], w[:, c, :],
                             start=(first and c == 0), stop=(final and c == 7))
    last.then_inc(k.unit_done, 1)


def plain(ap):
    return ap.bitcast(F32)


def split_hi(k, act, u, turn=0, ring_turn=0):
    act.wait_ge(k.w_loaded[u % RING], 16 * (u // RING + 1) + ring_turn * 16)
    if u >= 2:
        act.wait_ge(k.unit_done, turn + (u - 1))
    act.activation(k.w_hi[:, u % 2, :], k.ring[:, u % RING, :], ACT.Copy).then_inc(k.hi_ready, 1)


def split_lo(k, dve, u, turn=0):
    dve.wait_ge(k.hi_ready, turn + (u - k.whole_units + 1))
    dve.tensor_tensor(k.ring_lo[:, u % RING, :], k.ring[:, u % RING, :], plain(k.w_hi[:, u % 2, :]), ALU.subtract).then_inc(k.lo_ready, 1)


def unit_parts(k, u):
    return [ap.rearrange("p (c n) -> p c n", c=8) for ap in (k.w_hi[:, u % 2, :], k.ring_lo[:, u % RING, :])]


def split_ready(k, pe, u, n, turn=0):
    if n == 0:
        pe.wait_ge(k.hi_ready, turn + (u - k.whole_units + 1))
    if n == 2:
        pe.wait_ge(k.lo_ready, turn + (u - k.whole_units + 1))


def unit_N_split(k, pe, u, h, out):
    hi, lo = unit_parts(k, u)
    for tt in range(TT):
        for n, (m, w) in enumerate(((h[0], hi), (h[1], hi), (h[0], lo))):
            if tt == 0:
                split_ready(k, pe, u, n)
            for c in range(8):
                last = pe.matmul(out[tt], m[:, c, tt * P:(tt + 1) * P], w[:, c, :],
                                 start=(n == 0 and c == 0), stop=(n == 2 and c == 7))
    last.then_inc(k.unit_done, 1)


def unit_T_split(k, pe, u, h_hi, h_lo, out, turn=0):
    hi, lo = unit_parts(k, u)
    for nb in range(2):
        for n, (w, h) in enumerate(((hi, h_hi), (hi, h_lo), (lo, h_hi))):
            if nb == 0:
                split_ready(k, pe, u, n, turn)
            for c in range(8):
                last = pe.matmul(out[:, nb * S:(nb + 1) * S], w[:, c, nb * P:(nb + 1) * P], h[:, c, :],
                                 start=(n == 0 and c == 0), stop=(n == 2 and c == 7))
    last.then_inc(k.unit_done, 1)


def normalise(k, src, gcol, dstT, lay_at, split=None):
    nc = k.nc
    lay = Layout(k, lay_at)
    junk, xn = lay.take(TT, D), lay.take(TT, D)
    st = k.small[:, 0:8]
    n, m = k.norms, k.norms_T
    own = k.norm_steps
    with nc.Block() as block:
        @block.sync
        def _(sp):
            stream(k, sp, k.stream_to)

        @block.scalar
        def _(act):
            norm_roots(k, act, src, junk, st)
            if split:
                split_hi(k, act, split[2])
                for j in range(4):
                    act.wait_ge(k.turned, 4 * m + j + 1)
                    for c in range(2):
                        last = act.activation(split[0][:, 2 * j + c, :], k.ps[j][:, c * S:(c + 1) * S],
                                              ACT.Copy, scale=gcol[:, 2 * j + c:2 * j + c + 1])
                    last.then_inc(k.rounded_out, 1)
                return
            for j in range(0, 4, 2):
                act.wait_ge(k.turned, 4 * m + j + 1)
                for c in range(2):
                    act.activation(dstT[:, 2 * j + c, :], k.ps[j][:, c * S:(c + 1) * S], ACT.Copy,
                                   scale=gcol[:, 2 * j + c:2 * j + c + 1])

        @block.vector
        def _(dve):
            norm_means(k, dve, own, st)
            for tt in range(TT):
                dve.tensor_scalar(xn[:, tt, :], src[:, tt, :], st[:, 6 + tt:7 + tt], None,
                                  ALU.mult).then_inc(k.scaled, 1)
            if split:
                split_lo(k, dve, split[2])
                for j in range(4):
                    dve.wait_ge(k.rounded_out, k.rounds + j + 1)
                    for c in range(2):
                        n = 2 * j + c
                        dve.scalar_tensor_tensor(out=split[1][:, n, :], in0=k.ps[j][:, c * S:(c + 1) * S],
                                                 scalar=gcol[:, n:n + 1], in1=plain(split[0][:, n, :]), op0=ALU.mult,
                                                 op1=ALU.subtract)
                k.rounds += 4
                return
            for j in range(1, 4, 2):
                dve.wait_ge(k.turned, 4 * m + j + 1)
                for c in range(2):
                    dve.tensor_scalar(dstT[:, 2 * j + c, :], k.ps[j][:, c * S:(c + 1) * S],
                                      gcol[:, 2 * j + c:2 * j + c + 1], None, ALU.mult)

        @block.tensor
        def _(pe):
            pe.wait_ge(k.scaled, TT * (m + 1))
            for j in range(4):
                for c in range(2):
                    for tt in range(TT):
                        last = pe.transpose(k.ps[j][:, c * S + tt * P:c * S + (tt + 1) * P],
                                            xn[:, tt, (2 * j + c) * P:(2 * j + c + 1) * P], k.ident)
                last.then_inc(k.turned, 1)
    k.norms, k.norms_T = n + 1, m + 1


def norm_roots(k, act, src, junk, st):
    for tt in range(TT):
        act.activation(junk[:, tt, :], src[:, tt, :], ACT.Square,
                       accum_out=st[:, tt:tt + 1]).then_inc(k.squares, 1)
    act.wait_ge(k.mean_ready, k.norms + 1)
    act.activation(st[:, 6:8], st[:, 4:6], ACT.Sqrt).then_inc(k.root_ready, 1)


def norm_means(k, dve, own, st):
    dve.wait_ge(k.squares, TT * (k.norms + 1))
    own.up(dve.tensor_scalar(st[:, 2:4], st[:, 0:2], 1.0 / D, EPS, ALU.mult, ALU.add))
    own.settle(dve)
    dve.reciprocal(st[:, 4:6], st[:, 2:4]).then_inc(k.mean_ready, 1)
    dve.wait_ge(k.root_ready, k.norms + 1)


def normalise_rows(k, src, g_dram, dst):
    st = k.small[:, 0:8]
    lay = Layout(k, 0)
    junk, g_rows = lay.take(TT, D), lay.take(D)
    with k.nc.Block() as block:
        @block.sync
        def _(sp):
            sp.dma_start(g_rows, g_dram.partition_broadcast(P)).then_inc(k.g_here, 16)
            stream(k, sp, k.stream_to)

        @block.scalar
        def _(act):
            norm_roots(k, act, src, junk, st)

        @block.vector
        def _(dve):
            norm_means(k, dve, k.norm_steps, st)
            k.rows_normed += 1
            dve.wait_ge(k.g_here, 16 * k.rows_normed)
            for tt in range(TT):
                dve.scalar_tensor_tensor(out=dst[:, tt, :], in0=src[:, tt, :], scalar=st[:, 6 + tt:7 + tt],
                                         in1=g_rows, op0=ALU.mult, op1=ALU.mult)
    k.norms += 1


def ctx_sem(k, name):
    return k.stack.enter_context(k.nc.semaphore(name))


def load_and_tables(k):
    lay = Layout(k, 24576)
    posi = lay.take(S).bitcast(I32)
    pos, ang = lay.take(S), lay.take(S)
    turns, red = lay.take(2, S), lay.take(2, S)
    here_a, steps, reduced = ctx_sem(k, "params_here"), Count(ctx_sem(k, "table_steps")), ctx_sem(k, "reduced")
    here = ctx_sem(k, "inputs_here")
    c = k.consts
    with k.nc.Block() as block:
        @block.sync
        def _(sp):
            sp.dma_start(k.x[:, :, :], k.x_dram.rearrange("(t p) d -> p t d", p=P)).then_inc(here, 16)
            sp.dma_start(k.mem_rows, k.mem_dram.rearrange("(t p) d -> p t d", p=P)).then_inc(here, 16)
            sp.wait_ge(here_a, 64)
            sp.wait_ge(here, 32)
            for s in range(RING):
                sp.dma_start(k.ring[:, s, :], k.weights[s]).then_inc(k.w_loaded[s], 16)
            k.issued = RING

        @block.scalar
        def _(act):
            act.dma_start(posi, k.pos_dram.partition_broadcast(P)).then_inc(here_a, 16)
            act.dma_start(k.consts[:, :], k.consts_dram[:, 0:CON["window"]]).then_inc(here_a, 16)
            act.dma_start(k.cols[:, :], k.cols_dram).then_inc(here_a, 16)
            act.dma_start(k.rows[:, :], k.rows_dram.partition_broadcast(P)).then_inc(here_a, 16)
            act.wait_ge(reduced, 1)
            act.activation(k.sin, red[:, 0, :], ACT.Sin)
            act.activation(k.cos, red[:, 1, :], ACT.Sin)

        @block.vector
        def _(dve):
            dve.wait_ge(here_a, 64)
            steps.up(dve.tensor_copy(pos, posi))
            steps.settle(dve)
            steps.up(dve.tensor_scalar(ang, pos, c[:, CON["inv_freq"]:CON["inv_freq"] + 1], None, ALU.mult))
            steps.settle(dve)
            magic = 12582912.0
            for n, ahead in enumerate((0.0, 0.25)):
                steps.up(dve.tensor_scalar(turns[:, n, :], ang, 1.0 / TWO_PI, ahead, ALU.mult, ALU.add))
                steps.settle(dve)
                steps.up(dve.tensor_scalar(turns[:, n, :], turns[:, n, :], magic, None, ALU.add))
                steps.settle(dve)
                steps.up(dve.tensor_scalar(turns[:, n, :], turns[:, n, :], -magic, None, ALU.add))
                steps.settle(dve)
                steps.up(dve.scalar_tensor_tensor(out=red[:, n, :], in0=turns[:, n, :], scalar=-6.28125,
                                                  in1=ang, op0=ALU.mult, op1=ALU.add))
                steps.settle(dve)
                steps.up(dve.scalar_tensor_tensor(out=red[:, n, :], in0=turns[:, n, :],
                                                  scalar=-(TWO_PI - 6.28125), in1=red[:, n, :],
                                                  op0=ALU.mult, op1=ALU.add))
                steps.settle(dve)
                steps.up(dve.tensor_scalar(red[:, n, :], red[:, n, :], n * np.pi / 2, 3.1415925,
                                           ALU.add, ALU.min))
                steps.settle(dve)
                last = dve.tensor_scalar(red[:, n, :], red[:, n, :], -3.1415925, None, ALU.max)
                if n == 0:
                    steps.up(last)
                    steps.settle(dve)
            last.then_inc(reduced, 1)
            dve.wait_ge(here, 32)


def col(k, name, n=1, at=0):
    return k.cols[:, COL[name] + at:COL[name] + at + n]


def over(ap, n):
    return ap.rearrange("p (a s) -> p a s", a=1).to_broadcast([P, n, ap.shape[1]])


def softplus(dve, own, x, out, tmp, abs_ready, exp_ready):
    _, e, t, t2, p = tmp
    dve.scalar_tensor_tensor(out=tmp[0], in0=x, scalar=-1.0, in1=x, op0=ALU.mult, op1=ALU.max).then_inc(abs_ready, 1)
    dve.wait_ge(exp_ready, 1)
    own.up(dve.tensor_scalar(p, e, 2.0, None, ALU.add))
    own.settle(dve)
    own.up(dve.reciprocal(t2, p))
    own.settle(dve)
    own.up(dve.tensor_tensor(t, e, t2, ALU.mult))
    own.settle(dve)
    own.up(dve.tensor_tensor(t2, t, t, ALU.mult))
    own.settle(dve)
    own.up(dve.tensor_scalar(p, t2, 1.0 / 15, None, ALU.mult))
    own.settle(dve)
    for c in (13, 11, 9, 7, 5, 3):
        own.up(dve.scalar_tensor_tensor(out=p, in0=p, scalar=1.0 / c, in1=t2, op0=ALU.add, op1=ALU.mult))
        own.settle(dve)
    own.up(dve.scalar_tensor_tensor(out=p, in0=p, scalar=1.0, in1=t, op0=ALU.add, op1=ALU.mult))
    own.settle(dve)
    own.up(dve.tensor_scalar(t, x, 0.0, 0.5, ALU.max, ALU.mult))
    own.settle(dve)
    own.up(dve.tensor_tensor(t2, p, t, ALU.add))
    own.settle(dve)
    own.up(dve.tensor_scalar(out, t2, 2.0, None, ALU.mult))
    own.settle(dve)


def done_mark(k, pe, sem):
    pe.matmul(k.ps[7][0:1, 511:512], k.ident[:, 0:1], k.ident[:, 0:1], start=True, stop=True).then_inc(sem, 1)


def mixer_layout(k):
    lay = Layout(k, 0)
    m = k.mix
    m.kmT = lay.take(MEM_HEADS, S)
    m.vm = lay.take(TT, MEM_HEADS * P)
    m.qkT = lay.take(HEADS + KV_HEADS, S)
    m.va = lay.take(TT, KV_HEADS * P)
    m.qmT = lay.take(MEM_HEADS, S)
    m.at_xl = lay.at
    m.xl = lay.take(LRU_B, S + CONV - 1)
    m.gl = lay.take(LRU_B, S)
    m.xc = lay.take(LRU_B, S)
    k.gatesT = lay.take(24, S)
    k.branchT = lay.take(16, S)
    m.free = lay.at
    start = 2 * FF // P * S
    at = -(-m.free // P) * P - start
    m.memT = [k.spare_r[:, at + n * KC * S:at + (n + 1) * KC * S].rearrange("p (c s) -> p c s", c=KC)
              for n in range(2)]
    m.branch_r = [k.spare_r[:, at + n * 16 * S:at + (n + 1) * 16 * S].rearrange("p (c s) -> p c s", c=16)
                  for n in range(2)]
    m.free_f = start + at + 2 * KC * S


def projections(k):
    m, ps, U = k.mix, k.ps, FIRST
    acc, rope_ps = [ps[0], ps[1]], ps[5]
    lay = Layout(k, m.free_f)
    h_parts = (k.hT_hi, k.hT_lo)
    raw = lay.take(2, 2, S)
    rot1, rot2 = lay.take(2, S), lay.take(2, S)
    soft = [lay.take(2 * LRU_B) for _ in range(5)]
    neg_lam, m_soft = lay.take(2 * LRU_B), lay.take(2 * LRU_B)
    names = ("acc_out", "rot_ready", "rot_used", "lam_abs", "lam_exp")
    acc_out, rot_ready, rot_used, lam_abs, lam_exp = (ctx_sem(k, n) for n in names)
    own = Count(ctx_sem(k, "projections_dve"))
    parts = [
        ("mem_k", 2, True, m.memT, lambda n: m.kmT[:, 2 * n:2 * n + 2, :]),
        ("mem_v", 2, False, m.memT, lambda n: m.vm[:, :, n * S:(n + 1) * S]),
        ("q", 3, True, h_parts, lambda n: raw[:, n % 2, :, :]),
        ("k", 1, True, h_parts, lambda n: raw[:, 1, :, :]),
        ("v", 1, False, h_parts, lambda n: m.va[:, :, :]),
        ("mem_q", 2, True, h_parts, lambda n: m.qmT[:, 2 * n:2 * n + 2, :]),
        ("lru_x", 3, True, h_parts, lambda n: m.xl[:, 2 * n:2 * n + 2, 2:2 + S]),
        ("lru_gate", 3, True, h_parts, lambda n: m.gl[:, 2 * n:2 * n + 2, :]),
    ]
    FIRST_RAW = 4
    with k.nc.Block() as block:
        @block.sync
        def _(sp):
            stream(k, sp, U["lru_w"] + RING)

        @block.tensor
        def _(pe):
            def rotate(n):
                pe.wait_ge(acc_out, FIRST_RAW + n + 1)
                if n >= 1:
                    pe.wait_ge(rot_used, n)
                pe.matmul(rope_ps[:, :], k.rot, raw[:, n % 2, :, :].rearrange("p a s -> p (a s)"),
                          start=True, stop=True).then_inc(rot_ready, 1)

            use = 0
            for name, units, turned, src, _ in parts:
                for n in range(units):
                    bank = acc[use % 2]
                    if use >= 2:
                        pe.wait_ge(acc_out, use - 1)
                    if turned:
                        unit_T_split(k, pe, U[name] + n, *src, bank)
                    else:
                        unit_N_split(k, pe, U[name] + n, src, [bank[:, 0:S], bank[:, S:2 * S]])
                    use += 1
                    if FIRST_RAW + 1 < use <= FIRST_RAW + 5:
                        rotate(use - FIRST_RAW - 2)

        @block.scalar
        def _(act):
            act.wait_ge(lam_abs, 1)
            act.activation(soft[1], soft[0], ACT.Exp, scale=-1.0).then_inc(lam_exp, 1)
            use = 0
            for name, units, _, _, dst in parts:
                for n in range(units):
                    act.wait_ge(k.unit_done, U[name] + n + 1)
                    if FIRST_RAW + 2 <= use < FIRST_RAW + 4:
                        act.wait_ge(rot_used, use - FIRST_RAW - 1)
                    func = ACT.Gelu_apprx_tanh if name == "lru_gate" else ACT.Copy
                    act.activation(dst(n), halves(acc[use % 2][:, :]), func).then_inc(acc_out, 1)
                    if use + 2 < U["lru_w"]:
                        split_hi(k, act, use + 2)
                    use += 1

        @block.vector
        def _(dve):
            own.up(dve.memset(m.xl[:, :, 0:2], 0.0))
            own.up(dve.memset(m.xl[:, :, 2 + S:3 + S], 0.0))
            own.up(dve.tensor_scalar(neg_lam, col(k, "lam", 2 * LRU_B), -1.0, None, ALU.mult))
            own.up(dve.tensor_scalar(k.half_b[:, 0:24], col(k, "gate_b", 24), 0.5, None, ALU.mult))
            own.up(dve.tensor_scalar(k.half_b[:, 24:48], col(k, "lru_b", 24), 0.5, None, ALU.mult))
            own.settle(dve)
            softplus(dve, own, neg_lam, m_soft, soft, lam_abs, lam_exp)
            own.up(dve.tensor_scalar(k.rate[:, :], m_soft, -4.0, None, ALU.mult))
            for use in range(U["lru_w"]):
                if use + 2 < U["lru_w"]:
                    split_lo(k, dve, use + 2)
                n = use - FIRST_RAW
                if not 0 <= n < 4:
                    continue
                dve.wait_ge(acc_out, FIRST_RAW + n + 1)
                own.up(dve.tensor_tensor(rot1, raw[:, n % 2, :, :], over(k.cos, 2), ALU.mult))
                dve.wait_ge(rot_ready, n + 1)
                own.up(dve.tensor_tensor(rot2, halves(rope_ps[:, :]), over(k.sin, 2), ALU.mult))
                own.settle(dve)
                dve.tensor_tensor(m.qkT[:, 2 * n:2 * n + 2, :], rot1, rot2, ALU.add).then_inc(rot_used, 1)
                dve.wait_ge(rot_used, n + 1)
            dve.wait_ge(acc_out, 14)
            w, b = col(k, "conv_w", CONV * LRU_B), col(k, "conv_b", LRU_B)
            for h in range(LRU_B):
                own.up(dve.tensor_scalar(m.xc[:, h, :], m.xl[:, h, 0:S], w[:, h:h + 1], b[:, h:h + 1],
                                         ALU.mult, ALU.add))
            for j in range(1, CONV):
                own.settle(dve)
                for h in range(LRU_B):
                    own.up(dve.scalar_tensor_tensor(out=m.xc[:, h, :], in0=m.xl[:, h, j:j + S],
                                                    scalar=w[:, LRU_B * j + h:LRU_B * j + h + 1],
                                                    in1=m.xc[:, h, :], op0=ALU.mult, op1=ALU.add))


def attention(k):
    m, ps, U = k.mix, k.ps, FIRST
    acc, score, pt, out_ps = [ps[0], ps[1]], [ps[2], ps[3]], ps[4], ps[6]
    lay = Layout(k, m.free)
    ptS = lay.take(2, 2, S)
    th = lay.take(2, 2, LRU_B, S)
    twice, square = lay.take(2, LRU_B, S), lay.take(LRU_B, S)
    over_xl = Layout(k, m.at_xl)
    prob, window = over_xl.take(2, TT, S), over_xl.take(TT, S)
    stat = k.small[:, 16:48]
    HN, NG = HEADS + MEM_HEADS, 12
    names = ("gate_out", "lru_out", "window_here", "scores", "probs", "pt_ready", "pt_out", "pv_ready",
             "pv_out", "maxed", "exped", "lru_mm", "lru_log", "lru_exp", "lru_in", "lru_root")
    (gate_out, lru_out, window_here, scores, probs, pt_ready, pt_out, pv_ready, pv_out, maxed, exped,
     lru_mm, lru_log, lru_exp, lru_in, lru_root) = (ctx_sem(k, n) for n in names)
    own = Count(ctx_sem(k, "attention_dve"))
    gates_at = [1] * 9 + [2, 1]
    gate_unit = [U["gates"] + n for n in range(NG)]
    assert sum(gates_at) == NG

    def is_mem(t):
        return t < MEM_HEADS

    def exps_to(t):
        return 2 * (t + 1) + max(0, t + 1 - MEM_HEADS)

    def lru(pe):
        for n in range(2):
            u = U["lru_w"] + n
            loaded(k, pe, u)
            for b in range(16 if n == 0 else 8):
                blk = 16 * n + b
                pair, d = blk // 2, blk % 2
                if d == 0 and pair >= 2:
                    pe.wait_ge(lru_out, 2 * (pair - 1))
                last = pe.matmul(acc[pair % 2][:, d * S:(d + 1) * S], k.ring[:, u % RING, b * P:(b + 1) * P],
                                 m.xc[:, pair % LRU_B, :], start=True, stop=True)
                if d == 1:
                    last.then_inc(lru_mm, 1)
            done_mark(k, pe, k.unit_done)

    def pdhs(ap):
        return ap.rearrange("p d h s -> p (d h s)")

    with k.nc.Block() as block:
        @block.sync
        def _(sp):
            sp.dma_start(window, k.consts_dram[:, CON["window"]:CON["window"] + TT * S]
                         .rearrange("p (t s) -> p t s", t=TT)).then_inc(window_here, 16)
            stream(k, sp, U["merge"] + RING)

        @block.tensor
        def _(pe):
            def gate(n):
                if n >= 2:
                    pe.wait_ge(gate_out, 2 * (n - 1))
                if n < 2:
                    pe.wait_ge(lru_out, 24)
                unit_T_split(k, pe, gate_unit[n], k.hT_hi, k.hT_lo, acc[n % 2])

            def score_mm(t):
                if t >= 2:
                    pe.wait_ge(exped, exps_to(t - 2))
                qT = m.qmT[:, t, :] if is_mem(t) else m.qkT[:, t - MEM_HEADS, :]
                kT = m.kmT[:, t, :] if is_mem(t) else m.qkT[:, HEADS + (t - MEM_HEADS) // GROUP, :]
                for tt in range(TT):
                    last = pe.matmul(score[t % 2][:, tt * S:(tt + 1) * S], qT[:, tt * P:(tt + 1) * P], kT,
                                     start=True, stop=True)
                last.then_inc(scores, 1)

            def turn_probs(t):
                pe.wait_ge(probs, t + 1)
                if t >= 1:
                    pe.wait_ge(pt_out, t)
                for kt in range(TT):
                    for tt in range(TT):
                        last = pe.transpose(pt[:, kt * S + tt * P:kt * S + (tt + 1) * P],
                                            prob[:, t % 2, tt, kt * P:(kt + 1) * P], k.ident)
                last.then_inc(pt_ready, 1)

            def weigh(t):
                pe.wait_ge(pt_out, t + 1)
                if t >= 1:
                    pe.wait_ge(pv_out, t)
                g = t if is_mem(t) else (t - MEM_HEADS) // GROUP
                v = (m.vm if is_mem(t) else m.va)[:, :, g * P:(g + 1) * P]
                for kt in range(TT):
                    last = pe.matmul(out_ps[:, 0:S], v[:, kt, :], ptS[:, t % 2, kt, :],
                                     start=(kt == 0), stop=(kt == TT - 1))
                last.then_inc(pv_ready, 1)

            at = 0
            for t in range(HN + 1):
                if t < HN:
                    score_mm(t)
                if t >= 1:
                    turn_probs(t - 1)
                if t == 0:
                    lru(pe)
                for n in range(gates_at[t]):
                    gate(at)
                    at += 1
                if t >= 1:
                    weigh(t - 1)

        @block.gpsimd
        def _(pool):
            for u in gate_unit:
                split_lo(k, pool, u)

        @block.scalar
        def _(act):
            for pair in range(2 * LRU_B):
                g, h = pair // LRU_B, pair % LRU_B
                act.wait_ge(lru_mm, pair + 1)
                for d in range(2):
                    at = 24 + (2 * g + d) * LRU_B + h
                    act.activation(th[:, g, d, h, :], acc[pair % 2][:, d * S:(d + 1) * S], ACT.Tanh, scale=0.5,
                                   bias=k.half_b[:, at:at + 1]).then_inc(lru_out, 1)
            split_hi(k, act, gate_unit[0])
            split_hi(k, act, gate_unit[1])
            act.wait_ge(lru_log, 1)
            act.activation(pdhs(th[:, 1]), pdhs(th[:, 0]), ACT.Tanh, scale=-1.0).then_inc(lru_exp, 1)
            act.wait_ge(lru_exp, 1)
            act.activation(pdhs(th[:, 0]), pdhs(th[:, 0]), ACT.Exp).then_inc(lru_exp, 1)
            at = 0
            for t in range(HN + 1):
                if t >= 1:
                    act.wait_ge(pt_ready, t)
                    if t >= 3:
                        act.wait_ge(pv_ready, t - 2)
                    act.activation(ptS[:, (t - 1) % 2, :, :], halves(pt[:, :]), ACT.Copy).then_inc(pt_out, 1)
                if t < HN:
                    o = 16 * (t % 2)
                    act.wait_ge(maxed, t + 1)
                    if t >= 2 and is_mem(t):
                        act.wait_ge(pt_ready, t - 1)
                    for tt in range(TT):
                        src = score[t % 2][:, tt * S:(tt + 1) * S] if is_mem(t) else prob[:, t % 2, tt, :]
                        act.activation(prob[:, t % 2, tt, :], src, ACT.Exp,
                                       bias=stat[:, o + 2 + tt:o + 3 + tt], scale=SCALE if is_mem(t) else 1.0,
                                       accum_out=stat[:, o + 4 + tt:o + 5 + tt]).then_inc(exped, 1)
                    if not is_mem(t):
                        act.activation(stat[:, o + 8:o + 10], stat[:, o + 6:o + 8], ACT.Exp).then_inc(exped, 1)
                for n in range(gates_at[t]):
                    act.wait_ge(k.unit_done, gate_unit[at] + 1)
                    for b in range(2):
                        act.activation(k.gatesT[:, 2 * at + b, :], acc[at % 2][:, b * S:(b + 1) * S], ACT.Tanh,
                                       scale=0.5, bias=k.half_b[:, 2 * at + b:2 * at + b + 1]).then_inc(gate_out, 1)
                    if at + 2 < NG:
                        split_hi(k, act, gate_unit[at + 2])
                    at += 1
                if t >= 1:
                    act.wait_ge(pv_ready, t)
                    chunk = 12 + t - 1 if is_mem(t - 1) else t - 1 - MEM_HEADS
                    act.activation(k.branchT[:, chunk, :], out_ps[:, 0:S], ACT.Copy).then_inc(pv_out, 1)
                if t == 4:
                    act.wait_ge(lru_in, 1)
                    act.activation(pdhs(th[:, 1]), pdhs(th[:, 1]), ACT.Sqrt, scale=0.25).then_inc(lru_root, 1)

        @block.vector
        def _(dve):
            def softmax(t):
                o = 16 * (t % 2)
                dve.wait_ge(scores, t + 1)
                if is_mem(t):
                    own.up(dve.tensor_reduce(stat[:, o:o + 2], halves(score[t % 2][:, :]), AX.X, ALU.max))
                    own.settle(dve)
                    dve.tensor_scalar(stat[:, o + 2:o + 4], stat[:, o:o + 2], -SCALE, None, ALU.mult)\
                       .then_inc(maxed, 1)
                    dve.wait_ge(exped, exps_to(t))
                    total = stat[:, o + 4:o + 6]
                else:
                    h = t - MEM_HEADS
                    sink = k.rows[:, h:h + 1]
                    if h == 0:
                        dve.wait_ge(window_here, 16)
                    dve.wait_ge(pt_ready, t - 1)
                    own.up(dve.scalar_tensor_tensor(out=prob[:, t % 2, :, :], in0=halves(score[t % 2][:, :]),
                                                    scalar=SCALE, in1=window, op0=ALU.mult, op1=ALU.add))
                    own.settle(dve)
                    own.up(dve.tensor_reduce(stat[:, o:o + 2], prob[:, t % 2, :, :], AX.X, ALU.max))
                    own.settle(dve)
                    own.up(dve.tensor_scalar(stat[:, o + 2:o + 4], stat[:, o:o + 2], sink, -1.0,
                                             ALU.max, ALU.mult))
                    own.settle(dve)
                    dve.tensor_scalar(stat[:, o + 6:o + 8], stat[:, o + 2:o + 4], sink, None, ALU.add)\
                       .then_inc(maxed, 1)
                    dve.wait_ge(exped, exps_to(t))
                    total = stat[:, o + 10:o + 12]
                    own.up(dve.tensor_tensor(total, stat[:, o + 4:o + 6], stat[:, o + 8:o + 10], ALU.add))
                    own.settle(dve)
                own.up(dve.reciprocal(stat[:, o + 12:o + 14], total))
                own.settle(dve)
                for tt in range(TT):
                    last = dve.tensor_scalar(prob[:, t % 2, tt, :], prob[:, t % 2, tt, :],
                                             stat[:, o + 12 + tt:o + 13 + tt], None, ALU.mult)
                    if tt == 0:
                        own.up(last)
                last.then_inc(probs, 1)
                own.settle(dve)
                dve.wait_ge(probs, t + 1)

            a, om = th[:, 0], th[:, 1]
            dve.wait_ge(lru_out, 24)
            for d in range(2):
                for h in range(LRU_B):
                    own.up(dve.tensor_scalar(th[:, 0, d, h, :], th[:, 0, d, h, :], 1.0,
                                             k.rate[:, d * LRU_B + h:d * LRU_B + h + 1], ALU.add, ALU.mult))
            for d in range(2):
                last = dve.scalar_tensor_tensor(out=flat(twice[:, d]), in0=flat(th[:, 1, d]), scalar=1.0,
                                                in1=flat(m.xc), op0=ALU.add, op1=ALU.mult)
                if d == 0:
                    own.up(last)
                    own.settle(dve)
            last.then_inc(lru_log, 1)
            softmax(0)
            softmax(1)
            dve.wait_ge(lru_exp, 2)
            for d in range(2):
                own.up(dve.tensor_tensor(flat(square), flat(a[:, d]), flat(a[:, d]), ALU.mult))
                own.settle(dve)
                last = dve.scalar_tensor_tensor(out=flat(om[:, d]), in0=flat(square), scalar=1.0, in1=flat(om[:, d]),
                                                op0=ALU.add, op1=ALU.mult)
                if d == 0:
                    own.up(last)
                    own.settle(dve)
            last.then_inc(lru_in, 1)
            for t in range(2, 6):
                softmax(t)
            dve.wait_ge(lru_root, 1)
            bx = om
            own.up(dve.tensor_tensor(pdhs(bx), pdhs(om), pdhs(twice), ALU.mult))
            own.settle(dve)
            for h in range(LRU_B):
                own.up(dve.tensor_tensor_scan(out=twice[:, 0, h, :], data0=a[:, 0, h, :], data1=bx[:, 0, h, :],
                                              initial=0.0, op0=ALU.mult, op1=ALU.add))
                own.up(dve.tensor_tensor_scan(out=twice[:, 1, h, ::-1], data0=a[:, 1, h, ::-1],
                                              data1=bx[:, 1, h, ::-1], initial=0.0, op0=ALU.mult, op1=ALU.add))
            own.settle(dve)
            own.up(dve.tensor_tensor(flat(twice[:, 0]), flat(twice[:, 0]), flat(twice[:, 1]), ALU.add))
            own.settle(dve)
            own.up(dve.tensor_tensor(flat(k.branchT[:, 6:12, :]), flat(twice[:, 0]), flat(m.gl), ALU.mult))
            for t in range(6, HN):
                softmax(t)


def flat(ap):
    return ap.rearrange("p h s -> p (h s)")


def merge(k):
    ps, U = k.ps, FIRST
    lay = Layout(k, 0)
    mergedT = lay.take(KC, S)
    part = lay.take(2, 3, S)
    merged_r = (k.mid_r[:, 0, 16:24, :], k.mid_r[:, 0, 24:32, :])
    branch_hi, branch_lo = k.mix.branch_r
    own = Count(ctx_sem(k, "merge_dve"))
    merged, merged_round, merged_split, branch_round, branch_split = (
        ctx_sem(k, n) for n in ("merged", "merged_round", "merged_split", "branch_round", "branch_split"))
    chunks = [(0, 6), (6, 12), (12, 16)]
    F = U["merge"]

    with k.nc.Block() as block:
        @block.sync
        def _(sp):
            stream(k, sp, k.stream_to)

        @block.tensor
        def _(pe):
            for nb in range(8):
                u = F + nb
                if nb >= 2:
                    pe.wait_ge(merged, nb - 1)
                hi, lo_part = (ap.rearrange("p (c n) -> p c n", c=16)
                               for ap in (k.w_hi[:, u % 2, :], k.ring_lo[:, u % RING, :]))
                for b, (lo, end) in enumerate(chunks):
                    bank = ps[2 * (nb % 2) + b // 2][:, (b % 2) * S:(b % 2 + 1) * S]
                    for n, (w, h) in enumerate(((hi, branch_hi), (hi, branch_lo), (lo_part, branch_hi))):
                        if b == 0:
                            split_ready(k, pe, u, n)
                        if nb == 0 and n < 2:
                            pe.wait_ge((branch_round, branch_split)[n], b + 1)
                        for c in range(lo, end):
                            last = pe.matmul(bank, w[:, c, :], h[:, c, :], start=(n == 0 and c == lo),
                                             stop=(n == 2 and c == end - 1))
                last.then_inc(k.unit_done, 1)
            pe.wait_ge(merged_split, 8)
            for n in range(4):
                bank = ps[4 + n]
                unit_N_split(k, pe, U["out"] + n, merged_r, [bank[:, 0:S], bank[:, S:2 * S]])

        @block.scalar
        def _(act):
            split_hi(k, act, F)
            for lo, end in chunks:
                act.activation(branch_hi[:, lo:end, :], k.branchT[:, lo:end, :], ACT.Copy).then_inc(branch_round, 1)
            split_hi(k, act, F + 1)
            for nb in range(12):
                if nb + 2 < 12:
                    split_hi(k, act, F + nb + 2)
                if nb < 8:
                    act.wait_ge(merged, nb + 1)
                    act.activation(merged_r[0][:, nb, :], mergedT[:, nb, :], ACT.Copy).then_inc(merged_round, 1)

        @block.vector
        def _(dve):
            def split_branch(b):
                lo, end = chunks[b]
                dve.wait_ge(branch_round, b + 1)
                dve.tensor_tensor(branch_lo[:, lo:end, :], k.branchT[:, lo:end, :], plain(branch_hi[:, lo:end, :]),
                                  ALU.subtract).then_inc(branch_split, 1)

            split_branch(0)
            split_lo(k, dve, F)
            split_branch(1)
            split_branch(2)
            split_lo(k, dve, F + 1)
            gates = k.gatesT.rearrange("p (b n) s -> p b n s", b=3)
            for nb in range(8):
                dve.wait_ge(k.unit_done, F + nb + 1)
                a, b = halves(ps[2 * (nb % 2)][:, :]), ps[2 * (nb % 2) + 1][:, 0:S]
                own.up(dve.scalar_tensor_tensor(out=part[:, nb % 2, 0:2, :], in0=gates[:, 0:2, nb, :], scalar=1.0,
                                                in1=a, op0=ALU.add, op1=ALU.mult))
                own.up(dve.scalar_tensor_tensor(out=part[:, nb % 2, 2, :], in0=gates[:, 2, nb, :], scalar=1.0,
                                                in1=b, op0=ALU.add, op1=ALU.mult))
                own.settle(dve)
                own.up(dve.tensor_tensor(part[:, nb % 2, 0, :], part[:, nb % 2, 0, :], part[:, nb % 2, 1, :], ALU.add))
                own.settle(dve)
                dve.tensor_tensor(mergedT[:, nb, :], part[:, nb % 2, 0, :], part[:, nb % 2, 2, :], ALU.add)\
                   .then_inc(merged, 1)
                split_lo(k, dve, F + nb + 2)
                dve.wait_ge(merged_round, nb + 1)
                dve.tensor_tensor(merged_r[1][:, nb, :], mergedT[:, nb, :], plain(merged_r[0][:, nb, :]),
                                  ALU.subtract).then_inc(merged_split, 1)
            split_lo(k, dve, F + 10)
            split_lo(k, dve, F + 11)
            for n in range(4):
                dve.wait_ge(k.unit_done, U["out"] + n + 1)
                xs = k.x[:, :, n * S:(n + 1) * S]
                own.up(dve.scalar_tensor_tensor(out=xs, in0=halves(ps[4 + n][:, :]), scalar=0.5, in1=xs,
                                                op0=ALU.mult, op1=ALU.add))


def route(k):
    ps, U = k.ps, FIRST
    k.G = carve(k, 0, KEYS, S)
    lay = Layout(k, 0)
    qT = lay.take(2 * PEER_H, S)
    keys = lay.take(2 * PEER_H, KEYS)
    sc = lay.take(2, TT, 2, KEYS)
    best = lay.take(TT, 2 * PEER_H, TOPK)
    index = lay.take(TT, 2 * PEER_H, TOPK).bitcast(U32)
    index_f = lay.take(TT, 2 * PEER_H, TOPK)
    cand = lay.take(2, TT, TOPK * TOPK)
    top = lay.take(TT, PEER_H, TOPK)
    where = lay.take(TT, PEER_H * TOPK).bitcast(U32)
    half = [lay.take(TT, PEER_H * TOPK).bitcast(U32) for _ in range(2)]
    half_f = [lay.take(TT, PEER_H * TOPK) for _ in range(2)]
    equal = lay.take(PEER_H * TOPK, TOPK)
    chosen = lay.take(3, TT, PEER_H * TOPK)
    shifted, total, inverse = lay.take(TT, PEER_H, TOPK), lay.take(TT, PEER_H), lay.take(TT, PEER_H)
    k.slotsT = carve(k, KEYS * S, 3, S)
    names = ("keys_here", "q_out", "score_mm", "score_out", "head_done", "shift_ready", "exp_ready",
             "chosen_ready", "chosen_turned")
    (keys_here, q_out, score_mm, score_out, head_done, shift_ready, exp_ready, chosen_ready,
     chosen_turned) = (ctx_sem(k, n) for n in names)
    own = Count(ctx_sem(k, "route_dve"))

    with k.nc.Block() as block:
        @block.sync
        def _(sp):
            sp.dma_start(keys, k.args["sub_keys"].rearrange("p (n k) -> p n k", k=KEYS)).then_inc(keys_here, 16)
            stream(k, sp, k.stream_to)

        @block.tensor
        def _(pe):
            def score(h):
                pe.wait_ge(q_out, h + 1)
                if h == 0:
                    pe.wait_ge(keys_here, 16)
                if h >= 2:
                    pe.wait_ge(score_out, h - 1)
                for tt in range(TT):
                    for p in range(2):
                        o = (2 * tt + p) * KEYS
                        last = pe.matmul(ps[2 + h % 2][:, o:o + KEYS], qT[:, 2 * h + p, tt * P:(tt + 1) * P],
                                         keys[:, 2 * h + p, :], start=True, stop=True)
                last.then_inc(score_mm, 1)

            for h in range(PEER_H):
                if h >= 2:
                    pe.wait_ge(q_out, h - 1)
                unit_T(k, pe, U["peer_q"] + h, k.hT, ps[h % 2])
                if h >= 1:
                    score(h - 1)
            score(PEER_H - 1)
            pe.wait_ge(chosen_ready, 1)
            for n in range(3):
                for tt in range(TT):
                    o = (n % 2) * S + tt * P
                    last = pe.transpose(ps[4 + n // 2][:, o:o + P], chosen[:, n, tt, :], k.ident)
            last.then_inc(chosen_turned, 1)

        @block.scalar
        def _(act):
            for h in range(PEER_H + 1):
                if h < PEER_H:
                    act.wait_ge(k.unit_done, U["peer_q"] + h + 1)
                    act.activation(qT[:, 2 * h:2 * h + 2, :], halves(ps[h % 2][:, :]), ACT.Copy).then_inc(q_out, 1)
                if h >= 1:
                    act.wait_ge(score_mm, h)
                    if h >= 3:
                        act.wait_ge(head_done, h - 2)
                    act.activation(sc[:, (h - 1) % 2].rearrange("p t q k -> p (t q k)"), ps[2 + (h - 1) % 2][:, :],
                                   ACT.Copy).then_inc(score_out, 1)
            act.wait_ge(shift_ready, 1)
            act.activation(shifted, shifted, ACT.Exp).then_inc(exp_ready, 1)
            act.wait_ge(chosen_turned, 1)
            act.activation(k.slotsT[:, 0:2, :], halves(ps[4][:, :]), ACT.Copy)
            act.activation(k.slotsT[:, 2, :], ps[5][:, 0:S], ACT.Copy)

        @block.vector
        def _(dve):
            def top16(rows):
                for half_n in range(2):
                    at = slice(8 * half_n, 8 * half_n + 8)
                    for v, b, _ in rows:
                        own.up(dve.max(b[:, at], v))
                    own.settle(dve)
                    for v, b, i in rows:
                        own.up(dve.max_index(i[:, at], b[:, at], v))
                    own.settle(dve)
                    if half_n == 0:
                        for v, b, _ in rows:
                            own.up(dve.match_replace(v, b[:, at], v, -3e38))
                        own.settle(dve)

            for h in range(PEER_H):
                dve.wait_ge(score_out, h + 1)
                top16([(sc[:, h % 2, tt, p, :], best[:, tt, 2 * h + p, :], index[:, tt, 2 * h + p, :])
                       for tt in range(TT) for p in range(2)])
                for tt in range(TT):
                    a = best[:, tt, 2 * h, :].rearrange("p (a b) -> p a b", b=1).to_broadcast([P, TOPK, TOPK])
                    b = over(best[:, tt, 2 * h + 1, :], TOPK)
                    own.up(dve.tensor_tensor(cand[:, h % 2, tt, :].rearrange("p (a b) -> p a b", a=TOPK), a, b,
                                             ALU.add))
                own.settle(dve)
                top16([(cand[:, h % 2, tt, :], top[:, tt, h, :], where[:, tt, h * TOPK:(h + 1) * TOPK])
                       for tt in range(TT)])
                dve.tensor_scalar(half[1][:, :, h * TOPK:(h + 1) * TOPK], where[:, :, h * TOPK:(h + 1) * TOPK],
                                  TOPK - 1, None, ALU.bitwise_and).then_inc(head_done, 1)
            first = top[:, :, :, 0:1].to_broadcast([P, TT, PEER_H, TOPK])
            dve.tensor_tensor(shifted, top, first, ALU.subtract).then_inc(shift_ready, 1)
            own.up(dve.tensor_scalar(half[0], where, 4, None, ALU.logical_shift_right))
            own.up(dve.tensor_copy(index_f, index))
            own.settle(dve)
            dve.wait_ge(head_done, PEER_H)
            for n in range(2):
                own.up(dve.tensor_copy(half_f[n], half[n]))
            own.settle(dve)
            parts = index_f.rearrange("p t (h q) a -> p t h q a", q=2)
            for n in range(2):
                for tt in range(TT):
                    pos = half_f[n][:, tt, :].rearrange("p (j a) -> p j a", a=1).to_broadcast([P, PEER_H * TOPK, TOPK])
                    own.up(dve.tensor_tensor(equal, pos, over(k.iota[:, 0:TOPK], PEER_H * TOPK), ALU.is_equal))
                    own.settle(dve)
                    e = equal.rearrange("p (h j) a -> p h j a", h=PEER_H)
                    ind = parts[:, tt, :, n, :].rearrange("p h (j a) -> p h j a", j=1)\
                        .to_broadcast([P, PEER_H, TOPK, TOPK])
                    own.up(dve.tensor_tensor(e, e, ind, ALU.mult))
                    own.settle(dve)
                    own.up(dve.tensor_reduce(chosen[:, n, tt, :], equal, AX.X, ALU.add))
                    own.settle(dve)
            dve.wait_ge(exp_ready, 1)
            own.up(dve.tensor_reduce(total, shifted, AX.X, ALU.add))
            own.settle(dve)
            own.up(dve.reciprocal(inverse, total))
            own.settle(dve)
            inv = inverse.rearrange("p t (h j) -> p t h j", j=1).to_broadcast([P, TT, PEER_H, TOPK])
            gates = chosen[:, 2].rearrange("p t (h j) -> p t h j", h=PEER_H)
            dve.tensor_tensor(gates, shifted, inv, ALU.mult).then_inc(chosen_ready, 1)


def spread(k):
    GROUP_T, GROUPS, BUFS = 4, 4, 2
    TURNS = S // (GROUP_T * GROUPS)
    hot = carve(k, KEYS * S + 3 * S, BUFS, 2, GROUP_T, KEYS)
    hot_ready, spread_mm, spread_out = (ctx_sem(k, n) for n in ("hot_ready", "spread_mm", "spread_out"))
    ps = k.ps

    def turns(eng, body):
        body(0, True)
        with eng.Fori(1, TURNS) as i:
            body(i, False)

    with k.nc.Block() as block:
        @block.sync
        def _(sp):
            sp.dma_start(k.x_away, k.x.rearrange("p t d -> p (t d)")).then_inc(k.x_saved, 16)
            stream(k, sp, k.stream_to)
            sp.wait_ge(k.x_saved, 16)

        @block.vector
        def _(dve):
            def body(i, first):
                for g in range(GROUPS):
                    if not (first and g < BUFS):
                        dve.wait_ge(spread_mm, i * GROUPS + (g - BUFS + 1))
                    for n in range(GROUP_T):
                        t = i * (GROUP_T * GROUPS) + (g * GROUP_T + n)
                        i1, gate = (k.slotsT[:, c, bass.ds(t, 1)] for c in (0, 2))
                        dve.tensor_scalar(hot[:, g % BUFS, 0, n, :], k.iota, i1, gate, ALU.is_equal, ALU.mult)
                    t = i * (GROUP_T * GROUPS) + g * GROUP_T
                    i2 = k.slotsT[:, 1, bass.ds(t, GROUP_T)].rearrange("p (t n) -> p t n", n=1)\
                        .to_broadcast([P, GROUP_T, KEYS])
                    dve.tensor_tensor(hot[:, g % BUFS, 1, :, :], over(k.iota, GROUP_T), i2, ALU.is_equal)\
                       .then_inc(hot_ready, 1)
            turns(dve, body)
            h = k.hT.rearrange("p c s -> p (c s)")
            dve.wait_ge(k.rounded_out, k.rounds + 1)
            k.rounds += 1
            dve.tensor_tensor(k.hT_lo.rearrange("p c s -> p (c s)"), h, plain(k.hT_hi.rearrange("p c s -> p (c s)")),
                              ALU.subtract)

        @block.tensor
        def _(pe):
            def body(i, first):
                for g in range(GROUPS):
                    pe.wait_ge(hot_ready, i * GROUPS + (g + 1))
                    if not first:
                        pe.wait_ge(spread_out, i * GROUPS + (g - GROUPS + 1))
                    for n in range(GROUP_T):
                        last = pe.matmul(ps[g][:, n * KEYS:(n + 1) * KEYS], hot[:, g % BUFS, 0, n, :],
                                         hot[:, g % BUFS, 1, n, :], start=True, stop=True)
                    last.then_inc(spread_mm, 1)
            turns(pe, body)

        @block.scalar
        def _(act):
            act.activation(k.hT_hi.rearrange("p c s -> p (c s)"), k.hT.rearrange("p c s -> p (c s)"),
                           ACT.Copy).then_inc(k.rounded_out, 1)

            def body(i, first):
                for g in range(GROUPS):
                    act.wait_ge(spread_mm, i * GROUPS + (g + 1))
                    t = i * (GROUP_T * GROUPS) + g * GROUP_T
                    act.activation(k.G[:, :, bass.ds(t, GROUP_T)],
                                   ps[g][:, :].rearrange("p (t n) -> p n t", t=GROUP_T), ACT.Copy)\
                       .then_inc(spread_out, 1)
            turns(act, body)


PAIRS = 64


def experts(k):
    ps = k.ps
    F = FIRST["peer"]
    room = k.x.rearrange("p t d -> p (t d)")
    gelu, weighted_lo, weighted_hi = (ap.rearrange("p (j b s) -> p j b s", j=2, b=2)
                                      for ap in (room[:, 0:4 * S], k.x_r[:, 0:4 * S], k.x_r[:, 4 * S:8 * S]))
    x_back = carve(k, 0, TT, D)
    gelu_out, weighted_whole, weighted_round, weighted_ready = (
        ctx_sem(k, n) for n in ("gelu_out", "weighted_whole", "weighted_round", "weighted_ready"))
    own = Count(ctx_sem(k, "experts_dve"))

    def u_unit(j):
        return F + (2 * j - 1 if j else 0)

    def v_unit(j):
        return F + min(2 * j + 2, 127)

    def steps(eng, body):
        body(0, 0)
        with eng.Fori(0, (PAIRS - 2) // 2) as i:
            for n in (1, 2):
                body(n, i)
        body(PAIRS - 1, 0)

    with k.nc.Block() as block:
        @block.sync
        def _(sp):
            stream(k, sp, k.stream_to)
            sp.wait_ge(weighted_whole, 4)
            sp.wait_ge(k.x_saved, 16)
            sp.dma_start(x_back.rearrange("p t d -> p (t d)"), k.x_away).then_inc(k.x_here, 16)

        @block.tensor
        def _(pe):
            def up(j0, i):
                unit_T_split(k, pe, u_unit(j0), k.hT_hi, k.hT_lo, ps[j0 % 2], turn=i * 4)

            def down(j0, i):
                v = v_unit(j0)
                pe.wait_ge(weighted_ready, i * 2 + (j0 + 1))
                w_hi, w_lo = (w.rearrange("p (b d) -> p b d", b=2)
                              for w in (k.w_hi[:, v % 2, :], k.ring_lo[:, v % RING, :]))
                g_hi, g_lo = weighted_hi[:, j0 % 2], weighted_lo[:, j0 % 2]
                for n, (g, w) in enumerate(((g_hi, w_hi), (g_lo, w_hi), (g_hi, w_lo))):
                    split_ready(k, pe, v, n, turn=i * 4)
                    for b in range(2):
                        for tt in range(TT):
                            for dh in range(2):
                                last = pe.matmul(ps[4 + 2 * tt + dh][:, :], g[:, b, tt * P:(tt + 1) * P],
                                                 w[:, b, dh * 512:(dh + 1) * 512],
                                                 start=(j0 == 0 and n == 0 and b == 0),
                                                 stop=(j0 == PAIRS - 1 and n == 2 and b == 1))
                last.then_inc(k.unit_done, 1)

            def body(j0, i):
                if j0 == PAIRS - 1:
                    return down(j0, i)
                if j0 >= 1:
                    pe.wait_ge(gelu_out, i * 2 + j0)
                up(j0 + 1, i)
                down(j0, i)

            up(0, 0)
            steps(pe, body)

        @block.scalar
        def _(act):
            def body(j0, i):
                act.wait_ge(k.unit_done, i * 4 + (u_unit(j0) + 1))
                if j0 >= 2:
                    act.wait_ge(weighted_ready, i * 2 + (j0 - 1))
                act.activation(flat(gelu[:, j0 % 2]), ps[j0 % 2][:, :], ACT.Gelu_apprx_tanh).then_inc(gelu_out, 1)
                if 0 < j0 < PAIRS - 1:
                    split_hi(k, act, u_unit(j0 + 1), turn=i * 4, ring_turn=i)
                act.wait_ge(weighted_whole, i * 2 + (j0 + 1))
                act.activation(flat(weighted_hi[:, j0 % 2]), flat(gelu[:, j0 % 2]), ACT.Copy)\
                   .then_inc(weighted_round, 1)
                split_hi(k, act, v_unit(j0), turn=i * 4, ring_turn=i)

            split_hi(k, act, F)
            split_hi(k, act, F + 1)
            steps(act, body)

        @block.vector
        def _(dve):
            def body(j0, i):
                dve.wait_ge(gelu_out, i * 2 + (j0 + 1))
                g = gelu[:, j0 % 2]
                dve.tensor_tensor(g, g, k.G[:, bass.ds(i * 4 + 2 * j0, 2), :], ALU.mult).then_inc(weighted_whole, 1)
                if 0 < j0 < PAIRS - 1:
                    split_lo(k, dve, u_unit(j0 + 1), turn=i * 4)
                dve.wait_ge(weighted_round, i * 2 + (j0 + 1))
                dve.tensor_tensor(weighted_lo[:, j0 % 2], g, plain(weighted_hi[:, j0 % 2]), ALU.subtract).then_inc(weighted_ready, 1)
                split_lo(k, dve, v_unit(j0), turn=i * 4)

            split_lo(k, dve, F)
            split_lo(k, dve, F + 1)
            steps(dve, body)
            dve.wait_ge(k.unit_done, F + 128)
            dve.wait_ge(k.x_here, 16)
            for tt in range(TT):
                for dh in range(2):
                    at = slice(dh * 512, (dh + 1) * 512)
                    own.up(dve.tensor_tensor(k.x[:, tt, at], x_back[:, tt, at], ps[4 + 2 * tt + dh][:, :], ALU.add))


def gdn_layout(k):
    g = k.gdn = Kernel()
    lay = Layout(k, 0)
    H = GDN_H
    g.qkvT = lay.take(3 * H, S)
    g.zT = lay.take(H, S)
    g.A = lay.take(H, 4, P)
    g.intraT = lay.take(H, 4, P)
    g.bv = lay.take(H, 4, P)
    g.kdec = lay.take(H, 2, P)
    g.qdec = lay.take(H, 2, P)
    g.Y = lay.take(H, 4, P)
    g.X = lay.take(H, 4, P)
    g.levels = lay.take(7, 4, P)
    small = [k.gdn_small[:, n] for n in range(7)]
    g.g, g.beta, g.G, g.negG, g.eG, g.kd, g.nbe = small
    g.qT, g.kT, g.vT = (g.qkvT[:, n * H:(n + 1) * H, :] for n in range(3))
    g.at_v = 2 * H * S
    g.at_A, g.at_Y, g.at_X, g.at_levels = 8 * 4 * S, 24 * 4 * S, 28 * 4 * S, 32 * 4 * S


def gdn_project(k):
    g, ps, U, H = k.gdn, k.ps, FIRST, GDN_H
    PAD = GDN_CONV // 2
    lay = Layout(k, g.at_A)
    padded = lay.take(2, 2, S + 2 * PAD)
    square = lay.take(2, 2, S)
    inv = lay.take(2 * H, S)
    ab_w = lay.take(KC, 32)
    x_a, m_soft = lay.take(TT * 16), lay.take(TT * 16)
    soft = [lay.take(TT * 16) for _ in range(5)]
    th, rate = lay.take(TT, 16), lay.take(16)
    ab_hi, ab_lo = (k.spare_r[:, n * 256:(n + 1) * 256].rearrange("p (c n) -> p c n", c=KC) for n in range(2))
    names = ("ab_here", "ab_mm", "gdn_raw", "conv_ready", "silu_done", "square_ready", "norm_mm",
             "norm_read", "inv_ready", "inv_root", "dt_abs", "dt_exp", "ab_act", "ab_round",
             "ab_split")
    (ab_here, ab_mm, gdn_raw, conv_ready, silu_done, square_ready, norm_mm, norm_read, inv_ready,
     inv_root, dt_abs, dt_exp, ab_act, ab_round, ab_split) = (ctx_sem(k, n) for n in names)
    own = Count(ctx_sem(k, "gdn_project_dve"))
    ab_ps = ps[6]
    a_of = ab_ps[:, 0:64].rearrange("p (t n) -> p t n", t=TT)[:, :, 0:16]
    b_of = ab_ps[:, 0:64].rearrange("p (t n) -> p t n", t=TT)[:, :, 16:32]

    pads_ready = ctx_sem(k, "pads_ready")

    def silu(act, n):
        act.wait_ge(conv_ready, n + 1)
        pair = flat(g.qkvT[:, 2 * n:2 * n + 2, :])
        act.activation(pair, pair, ACT.Silu).then_inc(silu_done, 1)

    def read_norm(dve, n):
        dve.wait_ge(norm_mm, n + 1)
        dve.tensor_scalar(flat(inv[:, 2 * n:2 * n + 2, :]), ps[2 + n % 2][:, :], EPS, None, ALU.add)\
           .then_inc(norm_read, 1)

    def th_view(ap):
        return ap.rearrange("p (t d h) -> p t d h", t=TT, d=2)

    def by_system(ap):
        return ap.rearrange("p (d t) h -> p t d h", d=2)

    with k.nc.Block() as block:
        @block.sync
        def _(sp):
            sp.dma_start(ab_w, k.args["ab"].rearrange("p (c n) -> p c n", c=KC)).then_inc(ab_here, 16)
            stream(k, sp, k.stream_to)

        @block.tensor
        def _(pe):
            pe.wait_ge(ab_split, 1)
            for tt in range(TT):
                for n, (h, w) in enumerate(((k.hT_hi, ab_hi), (k.hT_lo, ab_hi), (k.hT_hi, ab_lo))):
                    for c in range(KC):
                        last = pe.matmul(ab_ps[:, tt * 32:(tt + 1) * 32], h[:, c, tt * P:(tt + 1) * P], w[:, c, :],
                                         start=(n == 0 and c == 0), stop=(n == 2 and c == KC - 1))
            last.then_inc(ab_mm, 1)
            for n in range(16):
                if n >= 2:
                    pe.wait_ge(gdn_raw, n - 1)
                unit_T_split(k, pe, U["gdn_qkv"] + n, k.hT_hi, k.hT_lo, ps[n % 2])
                if 2 <= n < 10:
                    pe.wait_ge(square_ready, n - 1)
                    if n >= 4:
                        pe.wait_ge(norm_read, n - 3)
                    pe.matmul(ps[2 + n % 2][:, :], k.ones, flat(square[:, n % 2]), start=True, stop=True)\
                      .then_inc(norm_mm, 1)

        @block.gpsimd
        def _(pool):
            for n in range(1, 16):
                split_lo(k, pool, U["gdn_qkv"] + n)

        @block.scalar
        def _(act):
            split_hi(k, act, U["gdn_qkv"] + 1)
            act.wait_ge(ab_here, 16)
            act.activation(ab_hi, ab_w, ACT.Copy).then_inc(ab_round, 1)
            act.wait_ge(ab_mm, 1)
            act.activation(th, b_of, ACT.Tanh, scale=0.5).then_inc(ab_act, 1)
            act.activation(rate, k.rows[:, ROWS["a_log"]:ROWS["a_log"] + 16], ACT.Exp).then_inc(ab_act, 1)
            act.wait_ge(dt_abs, 1)
            act.activation(soft[1], soft[0], ACT.Exp, scale=-1.0).then_inc(dt_exp, 1)
            for n in range(16):
                act.wait_ge(k.unit_done, U["gdn_qkv"] + n + 1)
                if n + 2 < 16:
                    split_hi(k, act, U["gdn_qkv"] + n + 2)
                if n < 12:
                    if n >= 2:
                        act.wait_ge(conv_ready, n - 1)
                    else:
                        act.wait_ge(pads_ready, 1)
                    act.activation(padded[:, n % 2, :, PAD:PAD + S], halves(ps[n % 2][:, :]), ACT.Copy)\
                       .then_inc(gdn_raw, 1)
                    if n >= 1:
                        silu(act, n - 1)
                    if n == 11:
                        silu(act, 11)
                else:
                    act.activation(g.zT[:, 2 * (n - 12):2 * (n - 11), :], halves(ps[n % 2][:, :]), ACT.Silu)\
                       .then_inc(gdn_raw, 1)
            act.wait_ge(inv_ready, 1)
            act.activation(flat(inv), flat(inv), ACT.Sqrt).then_inc(inv_root, 1)

        @block.vector
        def _(dve):
            dve.wait_ge(ab_round, 1)
            dve.tensor_tensor(ab_lo, ab_w, plain(ab_hi), ALU.subtract).then_inc(ab_split, 1)
            own.up(dve.memset(padded[:, :, :, 0:PAD], 0.0))
            own.settle(dve)
            dve.memset(padded[:, :, :, PAD + S:PAD + S + PAD], 0.0).then_inc(pads_ready, 1)
            dve.wait_ge(ab_act, 1)
            own.up(dve.tensor_tensor(x_a.rearrange("p (t n) -> p t n", t=TT), a_of,
                                     over(k.rows[:, ROWS["dt_bias"]:ROWS["dt_bias"] + 16], TT), ALU.add))
            own.settle(dve)
            softplus(dve, own, x_a, m_soft, soft, dt_abs, dt_exp)
            dve.wait_ge(ab_act, 2)
            own.up(dve.scalar_tensor_tensor(out=soft[0].rearrange("p (t n) -> p t n", t=TT),
                                            in0=m_soft.rearrange("p (t n) -> p t n", t=TT), scalar=-1.0,
                                            in1=over(rate, TT), op0=ALU.mult, op1=ALU.mult))
            own.settle(dve)
            own.up(dve.tensor_copy(by_system(g.g), th_view(soft[0])))
            own.up(dve.tensor_scalar(by_system(g.beta), th_view(th.rearrange("p t n -> p (t n)")), 0.5, 0.5,
                                     ALU.mult, ALU.add))
            w = col(k, "gdn_conv", GDN_CONV * 24)
            for n in range(12):
                dve.wait_ge(gdn_raw, n + 1)
                for j in range(GDN_CONV):
                    for b in range(2):
                        tap = w[:, 24 * j + 2 * n + b:24 * j + 2 * n + b + 1]
                        src, dst = padded[:, n % 2, b, j:j + S], g.qkvT[:, 2 * n + b, :]
                        if j == 0:
                            last = dve.tensor_scalar(dst, src, tap, None, ALU.mult)
                        else:
                            last = dve.scalar_tensor_tensor(out=dst, in0=src, scalar=tap, in1=dst,
                                                            op0=ALU.mult, op1=ALU.add)
                        if (j, b) != (GDN_CONV - 1, 1):
                            own.up(last)
                    if j < GDN_CONV - 1:
                        own.settle(dve)
                last.then_inc(conv_ready, 1)
                if 2 <= n < 10:
                    read_norm(dve, n - 2)
                if 1 <= n < 9:
                    dve.wait_ge(silu_done, n)
                    pair = flat(g.qkvT[:, 2 * n - 2:2 * n, :])
                    dve.tensor_tensor(flat(square[:, (n - 1) % 2]), pair, pair, ALU.mult).then_inc(square_ready, 1)
            own.settle(dve)
            dve.wait_ge(norm_read, 8)
            dve.reciprocal(flat(inv), flat(inv)).then_inc(inv_ready, 1)
            dve.wait_ge(silu_done, 8)
            dve.wait_ge(inv_root, 1)
            own.up(dve.scalar_tensor_tensor(out=flat(g.qT), in0=flat(g.qT), scalar=SCALE, in1=flat(inv[:, 0:H]),
                                            op0=ALU.mult, op1=ALU.mult))
            own.up(dve.tensor_tensor(flat(g.kT), flat(g.kT), flat(inv[:, H:2 * H]), ALU.mult))


def gdn_build(k):
    g, ps, H = k.gdn, k.ps, GDN_H
    lay = Layout(k, g.at_Y)
    gm, dA, dI = lay.take(2, 4, P), lay.take(2, 4, P), lay.take(2, 4, P)
    row_e = lay.take(2, 2, P)
    lay = Layout(k, g.at_X)
    cum, far_a, far_i = lay.take(2, P), lay.take(4, P), lay.take(4, P)
    lay = Layout(k, g.at_X + 2048)
    total = lay.take(4, H)
    names = ("masks_here", "sums_mm", "sums_ready", "sums_exp", "gm_ready", "rows_mm", "build_mm", "natural_mm",
             "decays_ready", "head_built", "natural_out")
    (masks_here, sums_mm, sums_ready, sums_exp, gm_ready, rows_mm, build_mm, natural_mm,
     decays_ready, head_built, natural_out) = (ctx_sem(k, n) for n in names)
    own = Count(ctx_sem(k, "gdn_build_dve"))
    KQ, RA, RI, RU, NAT = ps[0:2], ps[2:4], ps[4:6], ps[6], ps[7]
    SUMS = ps[1]

    with k.nc.Block() as block:
        @block.sync
        def _(sp):
            sp.dma_start(cum, k.consts_dram[:, CON["cum"]:CON["cum"] + 2 * P].rearrange("p (d n) -> p d n", d=2))\
              .then_inc(masks_here, 16)
            sp.dma_start(far_a, k.consts_dram[:, CON["far_a"]:CON["far_a"] + 4 * P]
                         .rearrange("p (s n) -> p s n", s=4)).then_inc(masks_here, 16)
            sp.dma_start(far_i, k.consts_dram[:, CON["far_i"]:CON["far_i"] + 4 * P]
                         .rearrange("p (s n) -> p s n", s=4)).then_inc(masks_here, 16)
            sp.dma_start(g.levels, k.consts_dram[:, CON["levels"]:CON["levels"] + 28 * P]
                         .rearrange("p (l s n) -> p l s n", l=7, s=4)).then_inc(k.levels_here, 16)
            stream(k, sp, k.stream_to)

        @block.tensor
        def _(pe):
            pe.wait_ge(masks_here, 48)
            for d in range(2):
                pe.matmul(SUMS[:, d * 16:(d + 1) * 16], cum[:, d, :], g.g[:, 2 * d:2 * d + 2, :]
                          .rearrange("p s h -> p (s h)"), start=True, stop=True)
            pe.matmul(SUMS[:, 32:64], k.ones, g.g.rearrange("p s h -> p (s h)"), start=True, stop=True)\
              .then_inc(sums_mm, 1)
            for h in range(H):
                pe.wait_ge(gm_ready, h + 1)
                if h >= 2:
                    pe.wait_ge(decays_ready, 9 * (h - 1))
                rows = gm[:, h % 2].rearrange("p s n -> p (s n)")
                pe.matmul(RA[h % 2][:, :], k.ones, rows, start=True, stop=False)
                pe.matmul(RA[h % 2][:, :], k.ident, far_a.rearrange("p s n -> p (s n)"), start=False, stop=True)
                pe.matmul(RI[h % 2][:, :], k.ones, rows, start=True, stop=False)
                pe.matmul(RI[h % 2][:, :], k.ident, far_i.rearrange("p s n -> p (s n)"), start=False, stop=True)\
                  .then_inc(rows_mm, 1)
                if h == 1:
                    pe.wait_ge(sums_ready, 2)
                if h >= 2:
                    pe.wait_ge(head_built, h - 1)
                for tt in range(TT):
                    c = slice(tt * P, (tt + 1) * P)
                    pe.matmul(KQ[h % 2][:, tt * P:(tt + 1) * P], g.kT[:, h, c], g.kT[:, h, c], start=True, stop=True)
                    pe.matmul(KQ[h % 2][:, (2 + tt) * P:(3 + tt) * P], g.kT[:, h, c], g.qT[:, h, c], start=True,
                              stop=True)
                if h >= 1:
                    pe.wait_ge(decays_ready, 9 * h)
                pe.matmul(RU[:, 0:2 * P], k.ones, gm[:, h % 2, 1:3, :].rearrange("p s n -> p (s n)"),
                          start=True, stop=True).then_inc(build_mm, 1)
                if h >= 1:
                    pe.wait_ge(natural_out, 6 * h)
                for n, src in enumerate((g.kT, g.vT)):
                    for tt in range(TT):
                        last = pe.transpose(NAT[:, (2 * n + tt) * P:(2 * n + tt + 1) * P],
                                            src[:, h, tt * P:(tt + 1) * P], k.ident)
                last.then_inc(natural_mm, 1)

        @block.scalar
        def _(act):
            act.wait_ge(sums_ready, 2)
            act.activation(g.eG, g.G, ACT.Exp).then_inc(sums_exp, 1)
            act.activation(g.kd, g.kd, ACT.Exp).then_inc(sums_exp, 1)
            act.wait_ge(sums_exp, 2)
            for h in range(H):
                act.wait_ge(rows_mm, h + 1)
                if h >= 2:
                    act.wait_ge(head_built, h - 1)
                for s in range(4):
                    c = slice(s * P, (s + 1) * P)
                    act.activation(dA[:, h % 2, s, :], RA[h % 2][:, c], ACT.Exp, scale=-1.0, bias=g.G[:, s, h:h + 1])\
                       .then_inc(decays_ready, 1)
                    act.activation(dI[:, h % 2, s, :], RI[h % 2][:, c], ACT.Exp, bias=g.negG[:, s, h:h + 1])\
                       .then_inc(decays_ready, 1)
                act.wait_ge(build_mm, h + 1)
                act.activation(row_e[:, h % 2], RU[:, 0:2 * P].rearrange("p (d n) -> p d n", d=2), ACT.Exp)\
                   .then_inc(decays_ready, 1)
                nat = NAT
                act.wait_ge(natural_mm, h + 1)
                for tt in range(TT):
                    act.activation(g.kdec[:, h, tt, :], nat[:, tt * P:(tt + 1) * P], ACT.Copy,
                                   scale=g.kd[:, 3 * tt, h:h + 1]).then_inc(natural_out, 1)
                for s in range(4):
                    act.activation(g.bv[:, h, s, :], nat[:, (2 + s % 2) * P:(3 + s % 2) * P], ACT.Copy,
                                   scale=g.beta[:, s, h:h + 1]).then_inc(natural_out, 1)

        @block.vector
        def _(dve):
            dve.wait_ge(masks_here, 48)

            def running(h):
                if h >= 2:
                    dve.wait_ge(build_mm, h - 1)
                for s in range(4):
                    last = dve.tensor_scalar(gm[:, h % 2, s, :], cum[:, s // 2, :], g.g[:, s, h:h + 1], None, ALU.mult)
                    if s < 3:
                        own.up(last)
                last.then_inc(gm_ready, 1)

            running(0)
            dve.wait_ge(sums_mm, 1)
            sums = SUMS[:, 0:32].rearrange("p (s h) -> p s h", s=4)
            own.up(dve.tensor_copy(g.G, sums))
            own.up(dve.tensor_copy(total, SUMS[:, 32:64].rearrange("p (s h) -> p s h", s=4)))
            own.settle(dve)
            dve.tensor_scalar(g.negG, g.G, -1.0, None, ALU.mult).then_inc(sums_ready, 1)
            dve.tensor_tensor(g.kd, total, g.G, ALU.subtract).then_inc(sums_ready, 1)
            dve.wait_ge(sums_exp, 1)
            own.up(dve.scalar_tensor_tensor(out=g.nbe, in0=g.eG, scalar=-1.0, in1=g.beta, op0=ALU.mult,
                                            op1=ALU.mult))
            for h in range(H):
                if h + 1 < H:
                    running(h + 1)
                dve.wait_ge(decays_ready, 9 * (h + 1))
                both = lambda n: KQ[h % 2][:, 2 * n * P:2 * (n + 1) * P].rearrange("p (d s) -> p d s", d=1)\
                    .to_broadcast([P, 2, 2 * P])
                pair = lambda ap: ap.rearrange("p (d t) n -> p d (t n)", d=2)
                own.up(dve.tensor_tensor(pair(dA[:, h % 2]), pair(dA[:, h % 2]), both(0), ALU.mult))
                own.up(dve.tensor_tensor(pair(g.intraT[:, h]), pair(dI[:, h % 2]), both(1), ALU.mult))
                own.up(dve.tensor_tensor(g.qdec[:, h, 0, :], g.qT[:, h, P:2 * P], row_e[:, h % 2, 0, :], ALU.mult))
                own.up(dve.tensor_tensor(g.qdec[:, h, 1, :], g.qT[:, h, 0:P], row_e[:, h % 2, 1, :], ALU.mult))
                own.settle(dve)
                beta = g.beta[:, :, h:h + 1].to_broadcast([P, 4, P])
                dve.tensor_tensor(g.A[:, h], dA[:, h % 2], beta, ALU.mult).then_inc(head_built, 1)


def gdn_invert(k):
    g, ps, H = k.gdn, k.ps, GDN_H
    TOGETHER, LEVELS = 4, 7
    am = carve(k, 0, TOGETHER, 4, P)
    zs = carve(k, g.at_v, 2, 4, P)
    names = ("level_ready", "z_mm", "z_out", "delta_mm", "y_ready", "x_ready")
    level_ready, z_mm, z_out, delta_mm, y_ready, x_ready = (ctx_sem(k, n) for n in names)

    class Step:
        pass

    steps = []
    with_delta = with_x = 0
    for h0 in range(0, H, TOGETHER):
        for level in range(LEVELS):
            for h in range(h0, h0 + TOGETHER):
                s = Step()
                s.n, s.h, s.level = len(steps), h, level
                with_delta += level > 0
                with_x += level < LEVELS - 1
                s.deltas, s.xs = with_delta, with_x
                steps.append(s)

    def all4(ap):
        return ap.rearrange("p s n -> p (s n)")

    with k.nc.Block() as block:
        @block.sync
        def _(sp):
            stream(k, sp, k.stream_to)

        @block.gpsimd
        def _(pool):
            pool.wait_ge(k.levels_here, 16)
            for s in steps:
                if s.n >= TOGETHER:
                    last = steps[s.n - TOGETHER]
                    pool.wait_ge(z_mm, last.n + 1)
                    if last.level == 0:
                        pool.wait_ge(x_ready, last.xs)
                pool.tensor_tensor(all4(am[:, s.h % TOGETHER]), all4(g.A[:, s.h]), all4(g.levels[:, s.level]),
                                   ALU.mult).then_inc(level_ready, 1)

        @block.tensor
        def _(pe):
            def delta(s):
                pe.wait_ge(z_out, s.deltas)
                pe.wait_ge(y_ready, s.n - 1)
                pe.wait_ge(x_ready, steps[s.n - 2].xs)
                for c in range(4):
                    last = pe.matmul(ps[2 + s.n % 2][:, c * P:(c + 1) * P], g.X[:, s.h, c, :], zs[:, s.n % 2, c, :],
                                     start=True, stop=True)
                if s.level < LEVELS - 1:
                    for c in range(4):
                        last = pe.matmul(ps[4 + s.n % 2][:, c * P:(c + 1) * P], zs[:, s.n % 2, c, :],
                                         g.X[:, s.h, c, :], start=True, stop=True)
                last.then_inc(delta_mm, 1)

            before = None
            for s in steps:
                pe.wait_ge(level_ready, s.n + 1)
                if s.n >= 2:
                    if steps[s.n - 2].level == 0:
                        pe.wait_ge(y_ready, s.n - 1)
                    else:
                        pe.wait_ge(z_out, steps[s.n - 2].deltas)
                if s.level > 0:
                    pe.wait_ge(y_ready, s.n - TOGETHER + 1)
                for c in range(4):
                    y = k.ident if s.level == 0 else g.Y[:, s.h, c, :]
                    last = pe.matmul(ps[s.n % 2][:, c * P:(c + 1) * P], am[:, s.h % TOGETHER, c, :], y,
                                     start=True, stop=True)
                last.then_inc(z_mm, 1)
                if before is not None:
                    delta(before)
                before = s if s.level > 0 else None
            delta(before)

        @block.scalar
        def _(act):
            for s in steps:
                if s.level > 0:
                    act.wait_ge(z_mm, s.n + 1)
                    act.activation(all4(zs[:, s.n % 2]), ps[s.n % 2][:, :], ACT.Copy).then_inc(z_out, 1)

        @block.vector
        def _(dve):
            eye = k.ident.rearrange("p (s n) -> p s n", s=1).to_broadcast([P, 4, P])
            for s in steps:
                if s.level == 0:
                    dve.wait_ge(z_mm, s.n + 1)
                    dve.tensor_tensor(g.Y[:, s.h], eye, ps[s.n % 2][:, :].rearrange("p (s n) -> p s n", s=4),
                                      ALU.subtract).then_inc(y_ready, 1)
                    dve.tensor_tensor(g.X[:, s.h], eye, am[:, s.h % TOGETHER], ALU.subtract).then_inc(x_ready, 1)
                    continue
                dve.wait_ge(delta_mm, s.deltas)
                dve.tensor_tensor(all4(g.Y[:, s.h]), all4(g.Y[:, s.h]), ps[2 + s.n % 2][:, :], ALU.subtract)\
                   .then_inc(y_ready, 1)
                if s.level < LEVELS - 1:
                    dve.tensor_tensor(all4(g.X[:, s.h]), all4(g.X[:, s.h]), ps[4 + s.n % 2][:, :], ALU.subtract)\
                       .then_inc(x_ready, 1)


def gdn_recur(k):
    g, ps, U, H = k.gdn, k.ps, FIRST, GDN_H
    lay = Layout(k, g.at_A)
    v1, state = lay.take(2 * H, P), lay.take(2 * H, P)
    lay = Layout(k, g.at_X)
    rhs, v2 = lay.take(2 * H, P), lay.take(2 * H, P)
    oT = carve(k, 0, H, S)
    square = carve(k, 2 * H * S, H, S)
    inv = carve(k, g.at_levels, H, S)
    names = ("v1_mm", "v1_out", "state_mm", "state_out", "ks_mm", "rhs_ready", "v2_mm", "v2_out", "o_mm",
             "o_out", "o_square", "o_norm_mm", "o_mean", "o_root", "o_gated")
    (v1_mm, v1_out, state_mm, state_out, ks_mm, rhs_ready, v2_mm, v2_out, o_mm, o_out, o_square,
     o_norm_mm, o_mean, o_root, o_gated) = (ctx_sem(k, n) for n in names)
    own = Count(ctx_sem(k, "gdn_recur_dve"))
    GROUPS = H // 2
    first_s, second_s = (0, 3), (1, 2)
    members = [[(2 * q + hh, d) for hh in range(2) for d in range(2)] for q in range(GROUPS)]

    def group(ap, q):
        return ap[:, 4 * q:4 * q + 4, :].rearrange("p c n -> p (c n)")

    with k.nc.Block() as block:
        @block.sync
        def _(sp):
            stream(k, sp, k.stream_to)

        @block.tensor
        def _(pe):
            def products(q, bank, lhs, rhs_of, done):
                for c, (h, d) in enumerate(members[q]):
                    last = pe.matmul(bank[:, c * P:(c + 1) * P], lhs(h, d), rhs_of(h, d), start=True, stop=True)
                last.then_inc(done, 1)

            for q in range(GROUPS):
                products(q, ps[q], lambda h, d: g.Y[:, h, first_s[d], :], lambda h, d: g.bv[:, h, first_s[d], :], v1_mm)
            for q in range(GROUPS):
                pe.wait_ge(v1_out, q + 1)
                products(q, ps[4 + q], lambda h, d: g.kdec[:, h, d, :], lambda h, d: v1[:, 2 * h + d, :], state_mm)
            for q in range(GROUPS):
                pe.wait_ge(state_out, q + 1)
                products(q, ps[q], lambda h, d: g.kT[:, h, (1 - d) * P:(2 - d) * P],
                         lambda h, d: state[:, 2 * h + d, :], ks_mm)
            for q in range(GROUPS):
                pe.wait_ge(rhs_ready, q + 1)
                products(q, ps[4 + q], lambda h, d: g.Y[:, h, second_s[d], :], lambda h, d: rhs[:, 2 * h + d, :], v2_mm)
            for q in range(GROUPS):
                pe.wait_ge(v2_out, q + 1)
                for hh in range(2):
                    h = 2 * q + hh
                    for tt in range(TT):
                        f, s = tt, 1 - tt
                        out = ps[q][:, hh * S + tt * P:hh * S + (tt + 1) * P]
                        pe.matmul(out, v1[:, 2 * h + f, :], g.intraT[:, h, first_s[f], :], start=True, stop=False)
                        pe.matmul(out, v2[:, 2 * h + s, :], g.intraT[:, h, second_s[s], :], start=False, stop=False)
                        last = pe.matmul(out, state[:, 2 * h + s, :], g.qdec[:, h, s, :], start=False, stop=True)
                last.then_inc(o_mm, 1)
            for q in range(GROUPS):
                pe.wait_ge(o_square, q + 1)
                pe.matmul(ps[4 + q][:, :], k.ones, flat(square[:, 2 * q:2 * q + 2, :]), start=True, stop=True)\
                  .then_inc(o_norm_mm, 1)
            pe.wait_ge(o_gated, 1)
            for n in range(4):
                unit_N(k, pe, U["gdn_out"] + n, oT, [ps[n][:, 0:S], ps[n][:, S:2 * S]])

        @block.scalar
        def _(act):
            for mm, out, dst, bank in ((v1_mm, v1_out, v1, 0), (state_mm, state_out, state, 4),
                                       (v2_mm, v2_out, v2, 4)):
                for q in range(GROUPS):
                    act.wait_ge(mm, q + 1)
                    act.activation(group(dst, q), ps[bank + q][:, :], ACT.Copy).then_inc(out, 1)
            for q in range(GROUPS):
                act.wait_ge(o_mm, q + 1)
                act.activation(oT[:, 2 * q:2 * q + 2, :], halves(ps[q][:, :]), ACT.Copy).then_inc(o_out, 1)
            act.wait_ge(o_mean, 1)
            act.activation(flat(inv), flat(inv), ACT.Sqrt).then_inc(o_root, 1)

        @block.vector
        def _(dve):
            for q in range(GROUPS):
                dve.wait_ge(ks_mm, q + 1)
                for c, (h, d) in enumerate(members[q]):
                    s = second_s[d]
                    last = dve.scalar_tensor_tensor(out=rhs[:, 2 * h + d, :], in0=ps[q][:, c * P:(c + 1) * P],
                                                    scalar=g.nbe[:, s, h:h + 1], in1=g.bv[:, h, s, :],
                                                    op0=ALU.mult, op1=ALU.add)
                    if c < 3:
                        own.up(last)
                last.then_inc(rhs_ready, 1)
            for q in range(GROUPS):
                dve.wait_ge(o_out, q + 1)
                o = flat(oT[:, 2 * q:2 * q + 2, :])
                dve.tensor_tensor(flat(square[:, 2 * q:2 * q + 2, :]), o, o, ALU.mult).then_inc(o_square, 1)
            for q in range(GROUPS):
                dve.wait_ge(o_norm_mm, q + 1)
                own.up(dve.tensor_scalar(flat(inv[:, 2 * q:2 * q + 2, :]), ps[4 + q][:, :], 1.0 / P, EPS,
                                         ALU.mult, ALU.add))
            own.settle(dve)
            dve.reciprocal(flat(inv), flat(inv)).then_inc(o_mean, 1)
            own.up(dve.scalar_tensor_tensor(out=flat(oT), in0=flat(oT), scalar=col(k, "gdn_norm"), in1=flat(g.zT),
                                            op0=ALU.mult, op1=ALU.mult))
            own.settle(dve)
            dve.wait_ge(o_root, 1)
            dve.tensor_tensor(flat(oT), flat(oT), flat(inv), ALU.mult).then_inc(o_gated, 1)
            for n in range(4):
                dve.wait_ge(k.unit_done, U["gdn_out"] + n + 1)
                xs = k.x[:, :, n * S:(n + 1) * S]
                own.up(dve.tensor_tensor(xs, xs, halves(ps[n][:, :]), ALU.add))


def mlp(k, layer):
    ps, F1, F2 = k.ps, FIRST[f"mlp1_{layer}"], FIRST[f"mlp2_{layer}"]
    mid_hi, mid_lo = k.mid_r[:, 0], k.mid_r[:, 1]
    mid = carve(k, 2 * FF // P * S, 2, 2, S)
    relu_out, square_ready, mid_round, mid_ready, sum_out = (
        ctx_sem(k, f"{n}_{layer}") for n in ("relu_out", "mid_square", "mid_round", "mid_ready", "sum_out"))
    own = Count(ctx_sem(k, f"mlp_dve_{layer}"))
    N1 = FF // 256

    def add(dve, j):
        dve.wait_ge(k.unit_done, F2 + 4 * j + 4)
        for tt in range(TT):
            xs = k.x[:, tt, j * S:(j + 1) * S]
            last = dve.tensor_tensor(xs, xs, ps[4 + 2 * (j % 2) + tt][:, 0:S], ALU.add)
            if tt == 0:
                own.up(last)
        last.then_inc(sum_out, 1)

    with k.nc.Block() as block:
        @block.sync
        def _(sp):
            stream(k, sp, k.stream_to)

        @block.tensor
        def _(pe):
            def up(i, first):
                for n in range(RING):
                    if not first:
                        pe.wait_ge(relu_out, i * RING + (n - RING + 1))
                    unit_T_split(k, pe, F1 + n, k.hT_hi, k.hT_lo, ps[n], turn=i * RING)

            up(0, True)
            with pe.Fori(1, N1 // RING) as i:
                up(i, False)
            for j in range(4):
                if j >= 2:
                    pe.wait_ge(sum_out, j - 1)
                for q in range(4):
                    u = F2 + 4 * j + q
                    hi, lo = unit_parts(k, u)
                    for n, (m, w) in enumerate(((mid_hi, hi), (mid_lo, hi), (mid_hi, lo))):
                        split_ready(k, pe, u, n)
                        if j == 0 and n == 0:
                            pe.wait_ge(mid_ready, 4 * (q + 1))
                        for tt in range(TT):
                            for c in range(8):
                                last = pe.matmul(ps[4 + 2 * (j % 2) + tt][:, 0:S],
                                                 m[:, 8 * q + c, tt * P:(tt + 1) * P], w[:, c, :],
                                                 start=(q == 0 and n == 0 and c == 0),
                                                 stop=(q == 3 and n == 2 and c == 7))
                    last.then_inc(k.unit_done, 1)

        @block.scalar
        def _(act):
            def turn(i, first):
                for n in range(RING):
                    act.wait_ge(k.unit_done, i * RING + (F1 + n + 1))
                    if not (first and n < 2):
                        act.wait_ge(mid_ready, i * RING + (n - 1))
                    act.activation(flat(mid[:, n % 2]), ps[n][:, :], ACT.Relu).then_inc(relu_out, 1)
                    split_hi(k, act, F1 + n + 2, turn=i * RING, ring_turn=i)
                    act.wait_ge(square_ready, i * RING + (n + 1))
                    act.activation(mid_hi[:, bass.ds(i * (2 * RING) + 2 * n, 2), :], mid[:, n % 2], ACT.Copy)\
                       .then_inc(mid_round, 1)

            split_hi(k, act, F1 + 1)
            turn(0, True)
            with act.Fori(1, N1 // RING) as i:
                turn(i, False)
            for u in range(F2 + 2, F2 + RING):
                split_hi(k, act, u)
            with act.Fori(0, 3) as i:
                for n in range(RING):
                    split_hi(k, act, F2 + RING + n, turn=i * RING, ring_turn=i)

        @block.vector
        def _(dve):
            split_lo(k, dve, F1 + 1)
            with dve.Fori(0, N1 // RING) as i:
                for n in range(RING):
                    dve.wait_ge(relu_out, i * RING + (n + 1))
                    m = mid[:, n % 2]
                    dve.tensor_tensor(m, m, m, ALU.mult).then_inc(square_ready, 1)
                    split_lo(k, dve, F1 + n + 2, turn=i * RING)
                    dve.wait_ge(mid_round, i * RING + (n + 1))
                    at = bass.ds(i * (2 * RING) + 2 * n, 2)
                    dve.tensor_tensor(mid_lo[:, at, :], m, plain(mid_hi[:, at, :]), ALU.subtract).then_inc(mid_ready, 1)
            for j in range(4):
                for q in range(4):
                    if 4 * j + q >= 2:
                        split_lo(k, dve, F2 + 4 * j + q)
                    if j >= 1 and q == 1:
                        add(dve, j - 1)
            add(dve, 3)


def ds_project(k):
    ps, F = k.ps, FIRST["ds_in"]
    d = k.ds = Kernel()
    lay = Layout(k, 0)
    d.qkT = lay.take(18, S)
    d.v = lay.take(TT, 5 * S)
    d.oT = lay.take(9, S)
    d.at = lay.at
    rel, hot, seen, table = (lay.take(n) for n in (DS_HEADS, DELTAS, DELTAS, DELTAS))
    names = ("ds_out_of", "bias_here", "bias_mm", "bias_ready")
    ds_out, bias_here, bias_mm, bias_ready = (ctx_sem(k, n) for n in names)
    with k.nc.Block() as block:
        @block.sync
        def _(sp):
            sp.dma_start(rel[0:BUCKETS, :], k.args["rel_bias"]).then_inc(bias_here, 16)
            sp.dma_start(hot[0:BUCKETS, :], k.args["hot"]).then_inc(bias_here, 16)
            sp.dma_start(seen[0:DS_HEADS, :], k.args["seen"]).then_inc(bias_here, 16)
            sp.wait_ge(bias_ready, 1)
            rows = table[0:DS_HEADS, :].rearrange("h (c n) -> h c n", c=1).to_broadcast([DS_HEADS, P, DELTAS])
            sp.dma_start(k.bias_dram, rows).then_inc(k.bias_stored, 16)
            stream(k, sp, k.stream_to)

        @block.tensor
        def _(pe):
            pe.wait_ge(bias_here, 48)
            pe.matmul(ps[2][0:DS_HEADS, :], rel[0:BUCKETS, :], hot[0:BUCKETS, :], start=True, stop=True)\
              .then_inc(bias_mm, 1)
            for n in range(14):
                bank = ps[n % 2]
                if n >= 2:
                    pe.wait_ge(ds_out, n - 1)
                if n < 9:
                    unit_T_split(k, pe, F + n, k.hT_hi, k.hT_lo, bank)
                else:
                    unit_N_split(k, pe, F + n, (k.hT_hi, k.hT_lo), [bank[:, 0:S], bank[:, S:2 * S]])

        @block.scalar
        def _(act):
            split_hi(k, act, F + 1)
            for n in range(14):
                act.wait_ge(k.unit_done, F + n + 1)
                dst = d.qkT[:, 2 * n:2 * n + 2, :] if n < 9 else d.v[:, :, (n - 9) * S:(n - 8) * S]
                act.activation(dst, halves(ps[n % 2][:, :]), ACT.Copy).then_inc(ds_out, 1)
                if n + 2 < 14:
                    split_hi(k, act, F + n + 2)

        @block.vector
        def _(dve):
            split_lo(k, dve, F + 1)
            dve.wait_ge(bias_mm, 1)
            dve.tensor_tensor(table[0:DS_HEADS, :], ps[2][0:DS_HEADS, :], seen[0:DS_HEADS, :], ALU.add)\
               .then_inc(bias_ready, 1)
            for n in range(2, 14):
                split_lo(k, dve, F + n)


def ds_attend(k):
    ps, F, d = k.ps, FIRST["ds_out"], k.ds
    G = len(DS_DIL)
    E = DS_E
    lay = Layout(k, d.at)
    bias = lay.take(2, G, TT * S)
    sc = lay.take(2, G, TT, S)
    ptS = lay.take(2, G, 2, S)
    stat = k.small[:, 16:48]
    names = ("ds_bias_here0", "ds_bias_here1", "ds_scores", "ds_scaled", "ds_maxed", "ds_exped", "ds_probs",
             "ds_turned", "ds_pt_out", "ds_pv", "ds_pv_out")
    (here0, here1, scores, scaled, maxed, exped, probs, turned, pt_out, pv, pv_out) = (ctx_sem(k, n) for n in names)
    here = [here0, here1]
    own = Count(ctx_sem(k, "ds_dve"))
    J = DS_PER

    with k.nc.Block() as block:
        @block.sync
        def _(sp):
            sp.wait_ge(k.bias_stored, 16)
            for j in range(J):
                if j >= 2:
                    sp.wait_ge(scaled, G * (j - 1))
                for tt in range(TT):
                    src = bass.AP(k.bias_dram.tensor, j * P * DELTAS + S - 1 - tt * P,
                                  [[DELTAS - 1, P], [DS_PER * P * DELTAS, G], [1, S]])
                    sp.dma_start(bias[:, j % 2, :, tt * S:(tt + 1) * S], src).then_inc(here[j % 2], 16)
            stream(k, sp, k.stream_to)

        @block.tensor
        def _(pe):
            def score(j):
                rows = slice(E * (j % 2), E * (j % 2) + E)
                if j >= 1:
                    pe.wait_ge(scaled, G * j)
                for g in range(G):
                    c = (DS_PER * g + j) // 2
                    for tt in range(TT):
                        last = pe.matmul(ps[g][:, tt * S:(tt + 1) * S], d.qkT[rows, c, tt * P:(tt + 1) * P],
                                         d.qkT[rows, 9 + c, :], start=True, stop=True)
                    last.then_inc(scores, 1)

            def turn(j):
                pe.wait_ge(probs, j + 1)
                if j >= 1:
                    pe.wait_ge(pt_out, G * j)
                for g in range(G):
                    for kt in range(TT):
                        for tt in range(TT):
                            last = pe.transpose(ps[3 + g][:, kt * S + tt * P:kt * S + (tt + 1) * P],
                                                sc[:, j % 2, g, tt, kt * P:(kt + 1) * P], k.ident)
                    last.then_inc(turned, 1)

            def weigh(j):
                rows = slice(E * (j % 2), E * (j % 2) + E)
                if j >= 1:
                    pe.wait_ge(pv_out, 2 * j)
                for g in range(G):
                    pe.wait_ge(pt_out, G * j + g + 1)
                    h = DS_PER * g + j
                    out = ps[6 + g // 2][rows, (g % 2) * S:(g % 2 + 1) * S]
                    for kt in range(TT):
                        last = pe.matmul(out, d.v[:, kt, E * h:E * h + E], ptS[:, j % 2, g, kt, :],
                                         start=(kt == 0), stop=(kt == TT - 1))
                last.then_inc(pv, 1)

            for j in range(J + 1):
                if j < J:
                    score(j)
                if j >= 1:
                    turn(j - 1)
                    weigh(j - 1)
            pe.wait_ge(pv_out, 2 * J)
            for n in range(4):
                for u in (F + 9 * n // 8, F + (9 * n + 8) // 8):
                    loaded(k, pe, u)
                for tt in range(TT):
                    for c in range(9):
                        i = 9 * n + c
                        w = slot(k, F + i // 8)[:, i % 8, :]
                        last = pe.matmul(ps[n][:, tt * S:(tt + 1) * S], d.oT[:, c, tt * P:(tt + 1) * P], w,
                                         start=(c == 0), stop=(c == 8))
                last.then_inc(k.unit_done, 1)
            done_mark(k, pe, k.unit_done)

        @block.scalar
        def _(act):
            for j in range(J + 1):
                if j < J:
                    o = 16 * (j % 2)
                    act.wait_ge(maxed, j + 1)
                    for tt in range(TT):
                        act.activation(sc[:, j % 2, :, tt, :], sc[:, j % 2, :, tt, :], ACT.Exp,
                                       bias=stat[:, o + 2 + tt:o + 3 + tt],
                                       accum_out=stat[:, o + 4 + tt:o + 5 + tt]).then_inc(exped, 1)
                if j >= 1:
                    rows = slice(E * ((j - 1) % 2), E * ((j - 1) % 2) + E)
                    if j >= 3:
                        act.wait_ge(pv, j - 2)
                    for g in range(G):
                        act.wait_ge(turned, G * (j - 1) + g + 1)
                        act.activation(ptS[:, (j - 1) % 2, g], halves(ps[3 + g][:, :]), ACT.Copy).then_inc(pt_out, 1)
                    act.wait_ge(pv, j)
                    c = (j - 1) // 2
                    act.activation(d.oT[rows, c:c + 4:3, :], halves(ps[6][rows, :]), ACT.Copy).then_inc(pv_out, 1)
                    act.activation(d.oT[rows, c + 6, :], ps[7][rows, 0:S], ACT.Copy).then_inc(pv_out, 1)

        @block.vector
        def _(dve):
            for j in range(J):
                o = 16 * (j % 2)
                dve.wait_ge(here[j % 2], 16 * TT * (j // 2 + 1))
                if j >= 2:
                    dve.wait_ge(turned, G * (j - 1))
                for g in range(G):
                    dve.wait_ge(scores, G * j + g + 1)
                    dve.scalar_tensor_tensor(out=sc[:, j % 2, g].rearrange("p t s -> p (t s)"), in0=ps[g][:, :],
                                             scalar=E ** -0.5, in1=bias[:, j % 2, g, :], op0=ALU.mult,
                                             op1=ALU.add).then_inc(scaled, 1)
                dve.wait_ge(scaled, G * (j + 1))
                own.up(dve.tensor_reduce(stat[:, o:o + 2], sc[:, j % 2].rearrange("p g t s -> p t g s"), AX.XY,
                                         ALU.max))
                own.settle(dve)
                dve.tensor_scalar(stat[:, o + 2:o + 4], stat[:, o:o + 2], -1.0, None, ALU.mult).then_inc(maxed, 1)
                dve.wait_ge(exped, 2 * (j + 1))
                own.up(dve.reciprocal(stat[:, o + 6:o + 8], stat[:, o + 4:o + 6]))
                own.settle(dve)
                for tt in range(TT):
                    last = dve.tensor_scalar(sc[:, j % 2, :, tt, :], sc[:, j % 2, :, tt, :],
                                             stat[:, o + 6 + tt:o + 7 + tt], None, ALU.mult)
                    if tt == 0:
                        own.up(last)
                last.then_inc(probs, 1)
                own.settle(dve)
            for n in range(4):
                dve.wait_ge(k.unit_done, F + n + 1)
                xs = k.x[:, :, n * S:(n + 1) * S]
                own.up(dve.tensor_tensor(xs, xs, halves(ps[n][:, :]), ALU.add))


def build(nc, args, out):
    k = Kernel()
    k.nc, k.mix = nc, Kernel()
    k.ARENA = 36864
    k.weights, k.consts_dram, k.cols_dram = args["weights"], args["consts"], args["cols"]
    k.x_dram, k.mem_dram, k.pos_dram, k.rows_dram = args["x"], args["mem"], args["pos"], args["rows"]
    k.args, k.out = args, out
    with ExitStack() as stack:
        k.stack = stack

        def sb(name, shape, dt=F32):
            return stack.enter_context(nc.sbuf_tensor("s_" + name, shape, dt))

        with ExitStack() as first:
            def low(name, *dims):
                return first.enter_context(nc.sbuf_tensor("s_" + name, [P, *dims], F32R))

            k.ring_lo = low("ring_lo", RING, UNIT)
            k.x_r = low("x_r", TT * D)
            k.hT_lo = low("hT_lo", KC, S)
            k.mid_r = low("mid_r", 2, FF // P, S)
            k.spare_r = low("spare_r", k.ARENA - 2 * FF // P * S - 2 * UNIT)
            k.w_hi = low("w_hi", 2, UNIT)
        k.ring = sb("ring", [P, RING, UNIT])
        k.x = sb("x", [P, TT, D])
        k.hT = sb("hT", [P, KC, S])
        k.arena = sb("arena", [P, k.ARENA])
        k.hT_hi = sb("hT_hi", [P, KC, S], F32R)
        k.consts = sb("consts", [P, CON["window"]])
        k.cols = sb("cols", [P, NCOLS])
        k.rows = sb("rows", [P, NROWS])
        k.small = sb("small", [P, 64])
        k.gdn_small = sb("gdn_small", [P, 7, 4, GDN_H])
        k.half_b = sb("half_b", [P, 48])
        k.rate = sb("rate", [P, 2 * LRU_B])
        k.ps = [stack.enter_context(nc.psum_tensor(f"bank{n}", [P, 512], F32)) for n in range(8)]
        k.ident = k.consts[:, CON["ident"]:CON["ident"] + P]
        k.ones = k.consts[:, CON["ones"]:CON["ones"] + P]
        k.iota = k.consts[:, CON["iota"]:CON["iota"] + P]
        k.rot = k.consts[:, CON["rot"]:CON["rot"] + P]
        k.w_loaded = [ctx_sem(k, f"weights_loaded{s}") for s in range(RING)]
        k.unit_done = ctx_sem(k, "unit_done")
        k.squares, k.mean_ready, k.root_ready = (ctx_sem(k, n) for n in ("squares", "mean_ready", "root_ready"))
        k.scaled, k.turned, k.norm_steps = ctx_sem(k, "scaled"), ctx_sem(k, "turned"), Count(ctx_sem(k, "norm_steps"))
        k.g_here, k.levels_here, k.bias_stored = (ctx_sem(k, n) for n in ("g_rows_here", "levels_here", "bias_stored"))
        k.hi_ready, k.lo_ready, k.rounded_out = (ctx_sem(k, n) for n in ("hi_ready", "lo_ready", "rounded_out"))
        k.x_saved, k.x_here = ctx_sem(k, "x_saved"), ctx_sem(k, "x_here")
        k.x_away = nc.dram_tensor("x_away", (P, TT * D), F32, kind="Internal").ap()
        k.norms = k.norms_T = k.rows_normed = k.rounds = 0
        k.bias_dram = nc.dram_tensor("bias_by_distance", (DS_HEADS, P, DELTAS), F32, kind="Internal").ap()
        program(k)


def program(k):
    mixer_layout(k)
    high = Layout(k, k.ARENA - 2 * UNIT - TT * D - 2 * S)
    k.mem_rows = high.take(TT, D)
    k.sin, k.cos = high.take(S), high.take(S)
    load_and_tables(k)
    k.stream_to = RING
    k.whole_units = 0
    normalise(k, k.mem_rows, col(k, "g_mem", KC), None, k.mix.free_f, split=(*k.mix.memT, 0))
    normalise(k, k.x, col(k, "g_mix", KC), None, k.mix.free_f, split=(k.hT_hi, k.hT_lo, 1))
    projections(k)
    k.whole_units = FIRST["gates"] - FIRST["lru_w"]
    attention(k)
    k.stream_to = FIRST["peer_q"] + RING
    merge(k)
    normalise(k, k.x, col(k, "g_ffn", KC), k.hT, 0)
    k.stream_to = FIRST["peer"] + RING
    route(k)
    spread(k)
    k.stream_to = FIRST["gdn_qkv"] + RING
    k.whole_units += FIRST["peer"] - FIRST["peer_q"]
    experts(k)
    normalise_rows(k, k.x, k.args["g_final"], k.x)
    normalise(k, k.x, col(k, "g_a", KC), None, 0, split=(k.hT_hi, k.hT_lo, FIRST["gdn_qkv"]))
    k.stream_to = FIRST["gdn_out"] + RING
    gdn_layout(k)
    gdn_project(k)
    gdn_build(k)
    gdn_invert(k)
    k.stream_to = FIRST["mlp1_0"] + RING
    gdn_recur(k)
    k.whole_units += FIRST["mlp1_0"] - FIRST["gdn_out"]
    normalise(k, k.x, col(k, "g_mlp0", KC), None, 0, split=(k.hT_hi, k.hT_lo, FIRST["mlp1_0"]))
    k.stream_to = FIRST["ds_in"] + RING
    mlp(k, 0)
    normalise(k, k.x, col(k, "g_b", KC), None, 0, split=(k.hT_hi, k.hT_lo, FIRST["ds_in"]))
    k.stream_to = FIRST["ds_out"] + RING
    ds_project(k)
    k.stream_to = FIRST["mlp1_1"] + RING
    ds_attend(k)
    k.whole_units += FIRST["mlp1_1"] - FIRST["ds_out"]
    normalise(k, k.x, col(k, "g_mlp1", KC), None, 0, split=(k.hT_hi, k.hT_lo, FIRST["mlp1_1"]))
    k.stream_to = UNITS
    mlp(k, 1)
    normalise_rows(k, k.x, k.args["norm_final"], k.x)
    store(k, k.x)


def store(k, src):
    done = ctx_sem(k, "stored")
    with k.nc.Block() as block:
        @block.sync
        def _(sp):
            sp.dma_start(k.out.rearrange("(t p) d -> p t d", p=P), src[:, :, :]).then_inc(done, 16)
            sp.wait_ge(done, 16)


def columns(w):
    n = w.shape[1] // 256
    return w.reshape(8, P, n, 256).transpose(2, 1, 0, 3).reshape(n, P, UNIT)


def lay_out(i):
    w_in = i["w_in"][0]
    at = np.cumsum([0, HEADS * P, KV_HEADS * P, KV_HEADS * P, 768, 768, MEM_HEADS * P, 3 * D])
    q, kk, v, lx, lg, mq, gates = (w_in[:, a:b] for a, b in zip(at[:-1], at[1:]))
    mem = i["w_mem_kv"][0]
    branches = np.concatenate([i["p_attn"][0], i["p_lru"][0], i["p_mem"][0]], 0)
    lru = np.stack([i["lru_wr"][0], i["lru_wi"][0]])
    lru = lru.transpose(0, 2, 1, 3, 4).reshape(24, P, P).transpose(1, 0, 2).reshape(P, 24 * P)
    lru = np.concatenate([lru, np.zeros((P, 8 * P), np.float32)], 1).reshape(P, 2, UNIT).transpose(1, 0, 2)
    units = {
        "mem_k": columns(mem[:, :512]), "mem_v": columns(mem[:, 512:]), "q": columns(q), "k": columns(kk),
        "v": columns(v), "mem_q": columns(mq), "lru_x": columns(lx), "lru_gate": columns(lg), "lru_w": lru,
        "gates": columns(gates),
        "merge": branches.reshape(16, P, 8, P).transpose(2, 1, 0, 3).reshape(8, P, UNIT),
        "out": columns(i["w_out"][0]), "peer_q": columns(i["w_peer_q"][0]),
    }
    u = i["peer_u"][0].reshape(KEYS, 64, 2, 8, P).transpose(1, 4, 3, 2, 0).reshape(64, P, UNIT)
    v = i["peer_v"][0].reshape(KEYS, 64, 2, D).transpose(1, 0, 2, 3).reshape(64, P, UNIT)
    units["peer"] = np.concatenate([u[:1], np.stack([u[1:], v[:-1]], 1).reshape(126, P, UNIT), v[-1:]], 0)
    g = i["gdn_w_in_2"][0]
    units["gdn_qkv"], units["gdn_z"] = columns(g[:, :3 * D]), columns(g[:, 3 * D:4 * D])
    units["gdn_out"] = columns(i["gdn_w_out_2"][0])
    for n in range(2):
        units[f"mlp1_{n}"] = columns(i["mlp_w1_2"][n])
        w2 = i["mlp_w2_2"][n]
        units[f"mlp2_{n}"] = w2.reshape(4, 8, P, 4, 256).transpose(3, 0, 2, 1, 4).reshape(16, P, UNIT)
    ds = np.concatenate([i["dswa_w_in_2"][0], np.zeros((D, P), np.float32)], 1)
    units["ds_in"] = columns(ds)
    out = i["dswa_w_out_2"][0].reshape(9, P, 4, 256).transpose(2, 0, 1, 3).reshape(36, P, 256)
    out = np.concatenate([out, np.zeros((4, P, 256), np.float32)], 0)
    units["ds_out"] = out.reshape(5, 8, P, 256).transpose(0, 2, 1, 3).reshape(5, P, UNIT)
    for name, n in STREAM:
        assert units[name].shape == (n, P, UNIT), (name, units[name].shape)
    weights = np.concatenate([units[name] for name, _ in STREAM], 0)

    def cols(a):
        return np.asarray(a, np.float32).reshape(-1, P).T

    parts = {
        "g_mix": i["g_mix"][0], "g_mem": i["g_mem"][0], "g_ffn": i["g_ffn"][0], "g_a": i["norm_mix_2"][0],
        "g_mlp0": i["norm_mlp_2"][0], "g_b": i["norm_mix_2"][1], "g_mlp1": i["norm_mlp_2"][1],
        "gate_b": i["gate_b"][0], "conv_w": i["conv_w"][0], "conv_b": i["conv_b"][0],
        "lru_b": np.stack([i["lru_br"][0], i["lru_bi"][0]]), "lam": i["lru_lambda"][0],
        "gdn_conv": i["gdn_conv_w_2"][0], "gdn_norm": i["gdn_norm_w_2"][0],
    }
    packed = np.concatenate([cols(parts[name]) for name, _ in COLS], 1)
    assert packed.shape == (P, NCOLS)
    rows = np.concatenate([i["attn_sink"][0], i["gdn_a_log_2"][0].ravel(), i["gdn_dt_bias_2"][0].ravel()])
    ab = i["gdn_w_in_2"][0][:, 4 * D:].reshape(8, P, 32).transpose(1, 0, 2).reshape(P, 256)
    hot, seen = distance_constants()
    sub_keys = i["peer_sub_keys"][0].reshape(16, KEYS, P).transpose(2, 0, 1).reshape(P, UNIT)
    arrays = {
        "sub_keys": sub_keys,
        "weights": weights, "cols": packed, "rows": rows, "consts": shape_constants(), "x": i["x"][0],
        "mem": i["mem"][0], "pos": i["positions"][0], "ab": ab, "rel_bias": i["rel_bias_2"],
        "g_final": i["g_final"], "norm_final": i["norm_final_2"], "hot": hot, "seen": seen,
    }
    return {n: np.ascontiguousarray(a) for n, a in arrays.items()}


def kernel(**inputs):
    from concourse import bacc
    from concourse.bass_utils import run_bass_kernel_spmd

    arrays = lay_out({n: np.asarray(a) for n, a in inputs.items()})
    nc = bacc.Bacc("TRN2", target_bir_lowering=False, num_devices=1)
    args = {n: nc.dram_tensor(n, a.shape, mybir.dt.from_np(a.dtype), kind="ExternalInput").ap()
            for n, a in arrays.items()}
    out = nc.dram_tensor("out", (S, D), F32, kind="ExternalOutput").ap()
    build(nc, args, out)
    r = run_bass_kernel_spmd(nc, [arrays], core_ids=[0])
    return r.results[0]["out"].reshape(1, S, D)
```
